# Optimizing a Trainium2 kernel written in Bass

```python
import math
import jax, jax.numpy as jnp
from jax import lax
import numpy as np

D_MODEL = 1024
BATCH = 1
SEQ = 256
DEPTH = 2

GRID_W = 64
CTX_LEN = 256
N_MIXERS = 2
N_A = (DEPTH + 1) // 2
N_B = DEPTH // 2
D_MIX = D_MODEL
CHUNK = 128
CM_GROUPS = 8
CM_GROUP_DIM = D_MIX // CM_GROUPS
SSM_GROUP = 16
SSM_GROUPS = D_MIX // SSM_GROUP
SSM_STATE = 64
PEER_HEADS = 8
PEER_KEYS = 128
PEER_EXPERTS = PEER_KEYS * PEER_KEYS
PEER_TOPK = 16
PEER_DKEY = 512
PEER_DHALF = PEER_DKEY // 2
PEER_BLOCK = 128
N_MOD = 6
EPS = 1e-6


def _rmsnorm(x, g):
    x32 = x.astype(jnp.float32)
    y = x32 * lax.rsqrt(jnp.mean(x32 * x32, axis=-1, keepdims=True) + EPS)
    return (y * g.astype(jnp.float32)).astype(x.dtype)

def _layernorm(x, g, b):
    x32 = x.astype(jnp.float32)
    mu = jnp.mean(x32, axis=-1, keepdims=True)
    xc = x32 - mu
    y = xc * lax.rsqrt(jnp.mean(xc * xc, axis=-1, keepdims=True) + EPS)
    return (y * g.astype(jnp.float32) + b.astype(jnp.float32)).astype(x.dtype)

def _modulate(h, shift, scale):
    return h * (1.0 + scale) + shift

def _sincos_1d(pos, dim):
    omega = 1.0 / (10000.0 ** (jnp.arange(dim // 2, dtype=jnp.float32) / (dim // 2)))
    ang = pos[:, None] * omega[None, :]
    return jnp.concatenate([jnp.sin(ang), jnp.cos(ang)], axis=-1)

def _pos_embed_2d(rows, dim):
    r = jnp.repeat(jnp.arange(rows, dtype=jnp.float32), GRID_W)
    col = jnp.tile(jnp.arange(GRID_W, dtype=jnp.float32), rows)
    return jnp.concatenate([_sincos_1d(r, dim // 2), _sincos_1d(col, dim // 2)], axis=-1)

def _chunk_mixer(h, w_in, ln_g, ln_b, w_s, b_s, w_out):
    bsz, length, _ = h.shape
    z = jax.nn.gelu(h @ w_in)
    u, v = jnp.split(z, 2, axis=-1)
    v = _layernorm(v, ln_g, ln_b)
    v = v.reshape(bsz, length // CHUNK, CHUNK, CM_GROUPS, CM_GROUP_DIM)
    v = jnp.einsum("hpq,bnqhd->bnphd", w_s, v) + b_s.T[:, :, None]
    return (u * v.reshape(bsz, length, D_MIX)) @ w_out

def _cmul(ar, ai, br, bi):
    return ar * br - ai * bi, ar * bi + ai * br

def _scan_combine(e1, e2):
    a1r, a1i, b1r, b1i = e1
    a2r, a2i, b2r, b2i = e2
    ar, ai = _cmul(a2r, a2i, a1r, a1i)
    br, bi = _cmul(a2r, a2i, b1r, b1i)
    return ar, ai, br + b2r, bi + b2i

def _diag_scan(a_r, a_i, bu_r, bu_i, h0=None):
    if h0 is not None:
        inj_r, inj_i = _cmul(a_r, a_i, h0[0], h0[1])
        bu_r = bu_r.at[0].add(inj_r)
        bu_i = bu_i.at[0].add(inj_i)
    a_full_r = jnp.broadcast_to(a_r, bu_r.shape)
    a_full_i = jnp.broadcast_to(a_i, bu_i.shape)
    _, _, h_r, h_i = lax.associative_scan(_scan_combine, (a_full_r, a_full_i, bu_r, bu_i), axis=0)
    return h_r, h_i

def _ssm_direction(u_lat, u_ctx, a_r, a_i, bb_r, bb_i, c_r, c_i, need_ctx_out):
    def inject(u):
        return (jnp.einsum("lgc,gpc->lgp", u, bb_r), jnp.einsum("lgc,gpc->lgp", u, bb_i))

    def readout(h_r, h_i):
        return jnp.einsum("lgp,gcp->lgc", h_r, c_r) - jnp.einsum("lgp,gcp->lgc", h_i, c_i)

    hc_r, hc_i = _diag_scan(a_r, a_i, *inject(u_ctx))
    hx_r, hx_i = _diag_scan(a_r, a_i, *inject(u_lat), h0=(hc_r[-1], hc_i[-1]))
    if need_ctx_out:
        return readout(hx_r, hx_i), readout(hc_r, hc_i)
    return readout(hx_r, hx_i), None

def _ssm_mixer(xn, cn, w_in, lam_re, lam_im, log_step, b_re, b_im, c_re, c_im, d_skip, w_out,
               need_ctx_out):
    u_x = xn @ w_in
    u_c = cn @ w_in
    lr = lam_re.astype(jnp.float32)
    li = lam_im.astype(jnp.float32)
    step = jnp.exp(log_step.astype(jnp.float32))[..., None]
    mag = jnp.exp(lr * step)
    a_r = mag * jnp.cos(li * step)
    a_i = mag * jnp.sin(li * step)
    den = lr * lr + li * li
    coef_r = ((a_r - 1.0) * lr + a_i * li) / den
    coef_i = (a_i * lr - (a_r - 1.0) * li) / den
    bb_r, bb_i = _cmul(coef_r[..., None], coef_i[..., None],
                       b_re.astype(jnp.float32), b_im.astype(jnp.float32))
    c_r = c_re.astype(jnp.float32)
    c_i = c_im.astype(jnp.float32)

    def per_sample(args):
        ux, uc = args
        ux = ux.astype(jnp.float32).reshape(-1, SSM_GROUPS, SSM_GROUP)
        uc = uc.astype(jnp.float32).reshape(-1, SSM_GROUPS, SSM_GROUP)
        yf_x, yf_c = _ssm_direction(ux, uc, a_r[0], a_i[0], bb_r[0], bb_i[0], c_r[0], c_i[0],
                                    need_ctx_out)
        yb_x, yb_c = _ssm_direction(ux[::-1], uc[::-1], a_r[1], a_i[1], bb_r[1], bb_i[1],
                                    c_r[1], c_i[1], need_ctx_out)
        y_lat = yf_x + yb_x[::-1]
        if need_ctx_out:
            return y_lat, yf_c + yb_c[::-1]
        return y_lat

    out = lax.map(per_sample, (u_x, u_c))

    def finish(y, u):
        y = y.reshape(u.shape).astype(u.dtype) + d_skip * u
        val, gate = jnp.split(jax.nn.gelu(y) @ w_out, 2, axis=-1)
        return val * jax.nn.sigmoid(gate)

    if need_ctx_out:
        return finish(out[0], u_x), finish(out[1], u_c)
    return finish(out, u_x), None

def _peer(h, w_q, sub_keys, u_tab, v_tab):
    shape = h.shape
    blocks = h.reshape(-1, PEER_BLOCK, D_MODEL)

    def block(hb):
        q = (hb @ w_q).reshape(PEER_BLOCK, PEER_HEADS, 2, PEER_DHALF)
        s = jnp.einsum("nhkd,hkmd->nhkm", q.astype(jnp.float32), sub_keys.astype(jnp.float32))
        s_half, i_half = lax.top_k(s, PEER_TOPK)
        cand = s_half[:, :, 0, :, None] + s_half[:, :, 1, None, :]
        top_s, top_c = lax.top_k(cand.reshape(PEER_BLOCK, PEER_HEADS, PEER_TOPK * PEER_TOPK),
                                 PEER_TOPK)
        k1 = jnp.take_along_axis(i_half[:, :, 0], top_c // PEER_TOPK, axis=-1)
        k2 = jnp.take_along_axis(i_half[:, :, 1], top_c % PEER_TOPK, axis=-1)
        ids = k1 * PEER_KEYS + k2
        g = jax.nn.softmax(top_s, axis=-1)
        ue = jnp.take(u_tab, ids, axis=0)
        ve = jnp.take(v_tab, ids, axis=0)
        act = jax.nn.gelu(jnp.einsum("nd,nhkd->nhk", hb, ue).astype(jnp.float32))
        return jnp.einsum("nhk,nhkd->nd", (g * act).astype(hb.dtype), ve)

    return lax.map(block, blocks).reshape(shape)

def first_inputs(seed: int = 0) -> dict:
    key = jax.random.key(seed)
    ks = jax.random.split(key, 32)
    f32 = jnp.float32
    nrm = lambda k, s, std: jax.random.normal(k, s, f32) * std
    G, P = SSM_GROUPS, SSM_STATE
    lam_im0 = jnp.broadcast_to(jnp.pi * jnp.arange(P, dtype=f32), (N_B, 2, G, P))
    return {
        "x": nrm(ks[0], (BATCH, SEQ, D_MODEL), 1.0),
        "c": nrm(ks[1], (BATCH, D_MODEL), 1.0),
        "ctx": nrm(ks[2], (BATCH, CTX_LEN, D_MODEL), 1.0),
        "c_ctx": nrm(ks[3], (D_MODEL,), 1.0),
        "ada_w": nrm(ks[4], (DEPTH, D_MODEL, N_MOD * D_MODEL), 0.5 * D_MODEL ** -0.5),
        "ada_b": nrm(ks[5], (DEPTH, N_MOD * D_MODEL), 0.02),
        "norm1_g": 1.0 + nrm(ks[6], (DEPTH, D_MODEL), 0.02),
        "norm2_g": 1.0 + nrm(ks[7], (DEPTH, D_MODEL), 0.02),
        "final_g": 1.0 + nrm(ks[8], (D_MODEL,), 0.02),
        "cm_w_in": nrm(ks[9], (N_A, D_MODEL, 2 * D_MIX), D_MODEL ** -0.5),
        "cm_ln_g": 1.0 + nrm(ks[10], (N_A, D_MIX), 0.02),
        "cm_ln_b": nrm(ks[11], (N_A, D_MIX), 0.02),
        "cm_w_s": nrm(ks[12], (N_A, CM_GROUPS, CHUNK, CHUNK), CHUNK ** -0.5),
        "cm_b_s": 1.0 + nrm(ks[13], (N_A, CM_GROUPS, CHUNK), 0.02),
        "cm_w_out": nrm(ks[14], (N_A, D_MIX, D_MODEL), D_MIX ** -0.5),
        "ssm_w_in": nrm(ks[15], (N_B, D_MODEL, D_MIX), D_MODEL ** -0.5),
        "ssm_lam_re": -0.5 + nrm(ks[16], (N_B, 2, G, P), 0.01),
        "ssm_lam_im": lam_im0 + nrm(ks[17], (N_B, 2, G, P), 0.01),
        "ssm_log_step": jax.random.uniform(ks[18], (N_B, 2, G), f32,
                                           minval=math.log(1e-3), maxval=math.log(1e-1)),
        "ssm_b_re": nrm(ks[19], (N_B, 2, G, P, SSM_GROUP), (2 * SSM_GROUP) ** -0.5),
        "ssm_b_im": nrm(ks[20], (N_B, 2, G, P, SSM_GROUP), (2 * SSM_GROUP) ** -0.5),
        "ssm_c_re": nrm(ks[21], (N_B, 2, G, SSM_GROUP, P), P ** -0.5),
        "ssm_c_im": nrm(ks[22], (N_B, 2, G, SSM_GROUP, P), P ** -0.5),
        "ssm_d": nrm(ks[23], (N_B, D_MIX), 1.0),
        "ssm_w_out": nrm(ks[24], (N_B, D_MIX, 2 * D_MODEL), D_MIX ** -0.5),
        "peer_w_q": nrm(ks[25], (DEPTH, D_MODEL, PEER_HEADS * PEER_DKEY), D_MODEL ** -0.5),
        "peer_keys": nrm(ks[26], (DEPTH, PEER_HEADS, 2, PEER_KEYS, PEER_DHALF), PEER_DHALF ** -0.5),
        "peer_u": nrm(ks[27], (DEPTH, PEER_EXPERTS, D_MODEL), D_MODEL ** -0.5),
        "peer_v": nrm(ks[28], (DEPTH, PEER_EXPERTS, D_MODEL), (PEER_HEADS * PEER_TOPK) ** -0.5),
    }

def first_block(x, c, ctx, c_ctx, ada_w, ada_b, norm1_g, norm2_g, final_g,
              cm_w_in, cm_ln_g, cm_ln_b, cm_w_s, cm_b_s, cm_w_out,
              ssm_w_in, ssm_lam_re, ssm_lam_im, ssm_log_step, ssm_b_re, ssm_b_im,
              ssm_c_re, ssm_c_im, ssm_d, ssm_w_out,
              peer_w_q, peer_keys, peer_u, peer_v):
    rows = x.shape[1] // GRID_W
    x = x + _pos_embed_2d(rows, D_MODEL).astype(x.dtype)[None]
    h_ctx = ctx
    silu_c = jax.nn.silu(c)
    silu_cc = jax.nn.silu(c_ctx)
    for i in range(DEPTH):
        last = i == DEPTH - 1
        k = i // N_MIXERS
        use_chunk = (i % N_MIXERS) == 0
        need_ctx_mix = (not last) or (not use_chunk)
        mod_x = (silu_c @ ada_w[i] + ada_b[i])[:, None, :]
        mod_c = (silu_cc @ ada_w[i] + ada_b[i])[None, None, :]
        sh1, sc1, g1, sh2, sc2, g2 = jnp.split(mod_x, N_MOD, axis=-1)
        csh1, csc1, cg1, csh2, csc2, cg2 = jnp.split(mod_c, N_MOD, axis=-1)

        xn = _modulate(_rmsnorm(x, norm1_g[i]), sh1, sc1)
        cn = _modulate(_rmsnorm(h_ctx, norm1_g[i]), csh1, csc1) if need_ctx_mix else None
        if use_chunk:
            y_x = _chunk_mixer(xn, cm_w_in[k], cm_ln_g[k], cm_ln_b[k], cm_w_s[k], cm_b_s[k],
                               cm_w_out[k])
            y_c = None if last else _chunk_mixer(cn, cm_w_in[k], cm_ln_g[k], cm_ln_b[k],
                                                 cm_w_s[k], cm_b_s[k], cm_w_out[k])
        else:
            y_x, y_c = _ssm_mixer(xn, cn, ssm_w_in[k], ssm_lam_re[k], ssm_lam_im[k],
                                  ssm_log_step[k], ssm_b_re[k], ssm_b_im[k], ssm_c_re[k],
                                  ssm_c_im[k], ssm_d[k], ssm_w_out[k], not last)
        x = x + g1 * y_x
        x = x + g2 * _peer(_modulate(_rmsnorm(x, norm2_g[i]), sh2, sc2),
                           peer_w_q[i], peer_keys[i], peer_u[i], peer_v[i])
        if not last:
            h_ctx = h_ctx + cg1 * y_c
            h_ctx = h_ctx + cg2 * _peer(_modulate(_rmsnorm(h_ctx, norm2_g[i]), csh2, csc2),
                                        peer_w_q[i], peer_keys[i], peer_u[i], peer_v[i])
    return _rmsnorm(x, final_g)


CHUNK_2 = 64
QBLOCK = 128
N_A_2 = DEPTH // 2
N_B_2 = DEPTH - N_A_2
FOX_HEADS = 16
FOX_HEAD_DIM = 64
FOX_WIDTH = FOX_HEADS * FOX_HEAD_DIM
MLA_HEADS = 16
MLA_NOPE = 128
MLA_ROPE = 64
MLA_V = 128
KV_LORA = 256
Q_LORA = 768
ROPE_THETA = 10000.0
D_FF = 2816
CONV_W = 3


def rmsnorm(x, g):
    xf = x.astype(jnp.float32)
    y = xf * lax.rsqrt(jnp.mean(xf * xf, axis=-1, keepdims=True) + EPS)
    return (y * g.astype(jnp.float32)).astype(x.dtype)

def rope_tables(seq, dtype):
    pos = jnp.arange(seq, dtype=jnp.float32)
    inv = ROPE_THETA ** (-jnp.arange(0, MLA_ROPE, 2, dtype=jnp.float32) / MLA_ROPE)
    ang = pos[:, None] * inv[None, :]
    return jnp.cos(ang).astype(dtype), jnp.sin(ang).astype(dtype)

def apply_rope(x, cos, sin):
    x1, x2 = jnp.split(x, 2, axis=-1)
    return jnp.concatenate([x1 * cos - x2 * sin, x1 * sin + x2 * cos], axis=-1)

def to_blocks(a):
    b, s = a.shape[:2]
    a = a.reshape((b, s // QBLOCK, QBLOCK) + a.shape[2:])
    return jnp.moveaxis(a, 1, 0)

def from_blocks(a):
    a = jnp.moveaxis(a, 0, 1)
    return a.reshape((a.shape[0], a.shape[1] * a.shape[2]) + a.shape[3:])

def fox_mixer(h, w_in, b_f, w_out):
    b, s_len, _ = h.shape
    proj = h @ w_in
    qkv = proj[..., :3 * FOX_WIDTH].reshape(b, s_len, 3, FOX_HEADS, FOX_HEAD_DIM)
    q, k, v = qkv[:, :, 0], qkv[:, :, 1], qkv[:, :, 2]
    logf = jax.nn.log_sigmoid((proj[..., 3 * FOX_WIDTH:] + b_f).astype(jnp.float32))
    cum = jnp.cumsum(logf, axis=1)
    cum_k = jnp.transpose(cum, (0, 2, 1))
    kpos = jnp.arange(s_len)
    scale = FOX_HEAD_DIM ** -0.5

    def block(args):
        i, qi, ci = args
        sc = jnp.einsum('bqhd,bkhd->bhqk', qi, k, preferred_element_type=jnp.float32) * scale
        sc = sc + (jnp.transpose(ci, (0, 2, 1))[..., :, None] - cum_k[:, :, None, :])
        qpos = i * QBLOCK + jnp.arange(QBLOCK)
        sc = jnp.where(kpos[None, :] <= qpos[:, None], sc, -jnp.inf)
        p = jax.nn.softmax(sc, axis=-1).astype(v.dtype)
        return jnp.einsum('bhqk,bkhd->bqhd', p, v)

    o = lax.map(block, (jnp.arange(s_len // QBLOCK), to_blocks(q), to_blocks(cum)))
    return from_blocks(o).reshape(b, s_len, FOX_WIDTH) @ w_out

def mla_shared_kv(x, kv_in_g, w_dkv, kv_norm_g, w_uk, w_uv, cos, sin):
    b, s_len, _ = x.shape
    ckv = rmsnorm(x, kv_in_g) @ w_dkv
    latent = rmsnorm(ckv[..., :KV_LORA], kv_norm_g)
    k_rope = apply_rope(ckv[..., KV_LORA:], cos, sin)
    k_nope = (latent @ w_uk).reshape(b, s_len, MLA_HEADS, MLA_NOPE)
    v = (latent @ w_uv).reshape(b, s_len, MLA_HEADS, MLA_V)
    return k_nope, k_rope, v

def mla_mixer(h, w_dq, q_norm_g, w_uq, w_out, k_nope, k_rope, v, cos, sin):
    b, s_len, _ = h.shape
    q = (rmsnorm(h @ w_dq, q_norm_g) @ w_uq).reshape(b, s_len, MLA_HEADS, MLA_NOPE + MLA_ROPE)
    q_nope = q[..., :MLA_NOPE]
    q_rope = apply_rope(q[..., MLA_NOPE:], cos[:, None, :], sin[:, None, :])
    kpos = jnp.arange(s_len)
    scale = (MLA_NOPE + MLA_ROPE) ** -0.5

    def block(args):
        i, qn, qr = args
        sc = (jnp.einsum('bqhd,bkhd->bhqk', qn, k_nope, preferred_element_type=jnp.float32)
              + jnp.einsum('bqhr,bkr->bhqk', qr, k_rope, preferred_element_type=jnp.float32)) * scale
        qpos = i * QBLOCK + jnp.arange(QBLOCK)
        visible = kpos[None, :] < (qpos[:, None] // CHUNK_2 + 1) * CHUNK_2
        sc = jnp.where(visible, sc, -jnp.inf)
        p = jax.nn.softmax(sc, axis=-1).astype(v.dtype)
        return jnp.einsum('bhqk,bkhd->bqhd', p, v)

    o = lax.map(block, (jnp.arange(s_len // QBLOCK), to_blocks(q_nope), to_blocks(q_rope)))
    return from_blocks(o).reshape(b, s_len, MLA_HEADS * MLA_V) @ w_out

def conv_ffn(h, w_in, conv_w, conv_b, w_out):
    s_len = h.shape[1]
    u = h @ w_in
    up = jnp.pad(u, ((0, 0), (CONV_W - 1, 0), (0, 0)))
    u = conv_b + sum(up[:, j:j + s_len] * conv_w[j] for j in range(CONV_W))
    gate, val = jnp.split(u, 2, axis=-1)
    return (jax.nn.silu(gate) * val) @ w_out

def second_inputs(seed: int = 0) -> dict:
    key = jax.random.key(seed)
    ks = jax.random.split(key, 24)
    f32 = jnp.float32
    res = (2.0 * DEPTH) ** -0.5

    def nrm(k, shape, scale):
        return jax.random.normal(k, shape, f32) * scale

    def gain(k, shape):
        return 1.0 + 0.02 * jax.random.normal(k, shape, f32)

    w_fox_in = jnp.concatenate([
        nrm(ks[2], (N_A_2, D_MODEL, 3 * FOX_WIDTH), D_MODEL ** -0.5),
        nrm(ks[3], (N_A_2, D_MODEL, FOX_HEADS), 0.1 * D_MODEL ** -0.5)], axis=-1)
    return {
        'x': jax.random.normal(ks[0], (BATCH, SEQ, D_MODEL), f32),
        'fox_norm': gain(ks[1], (N_A_2, D_MODEL)),
        'w_fox_in': w_fox_in,
        'b_fox_f': jax.random.uniform(ks[4], (N_A_2, FOX_HEADS), f32, 1.0, 6.0),
        'w_fox_out': nrm(ks[5], (N_A_2, FOX_WIDTH, D_MODEL), FOX_WIDTH ** -0.5 * res),
        'kv_in_norm': gain(ks[6], (D_MODEL,)),
        'w_dkv': nrm(ks[7], (D_MODEL, KV_LORA + MLA_ROPE), D_MODEL ** -0.5),
        'kv_norm': gain(ks[8], (KV_LORA,)),
        'w_uk': nrm(ks[9], (KV_LORA, MLA_HEADS * MLA_NOPE), KV_LORA ** -0.5),
        'w_uv': nrm(ks[10], (KV_LORA, MLA_HEADS * MLA_V), KV_LORA ** -0.5),
        'mla_norm': gain(ks[11], (N_B_2, D_MODEL)),
        'w_dq': nrm(ks[12], (N_B_2, D_MODEL, Q_LORA), D_MODEL ** -0.5),
        'q_norm': gain(ks[13], (N_B_2, Q_LORA)),
        'w_uq': nrm(ks[14], (N_B_2, Q_LORA, MLA_HEADS * (MLA_NOPE + MLA_ROPE)), Q_LORA ** -0.5),
        'w_mla_out': nrm(ks[15], (N_B_2, MLA_HEADS * MLA_V, D_MODEL), (MLA_HEADS * MLA_V) ** -0.5 * res),
        'ffn_norm': gain(ks[16], (DEPTH, D_MODEL)),
        'w_ffn_in': nrm(ks[17], (DEPTH, D_MODEL, 2 * D_FF), D_MODEL ** -0.5),
        'ffn_conv_w': nrm(ks[18], (DEPTH, CONV_W, 2 * D_FF), CONV_W ** -0.5),
        'ffn_conv_b': nrm(ks[19], (DEPTH, 2 * D_FF), 0.01),
        'w_ffn_out': nrm(ks[20], (DEPTH, D_FF, D_MODEL), D_FF ** -0.5 * res),
        'final_norm': gain(ks[21], (D_MODEL,)),
    }

def second_block(x, fox_norm, w_fox_in, b_fox_f, w_fox_out, kv_in_norm, w_dkv, kv_norm, w_uk, w_uv,
              mla_norm, w_dq, q_norm, w_uq, w_mla_out, ffn_norm, w_ffn_in, ffn_conv_w, ffn_conv_b,
              w_ffn_out, final_norm):
    cos, sin = rope_tables(x.shape[1], x.dtype)
    k_nope = k_rope = v = None
    for layer in range(DEPTH):
        if layer < N_A_2:
            x = x + fox_mixer(rmsnorm(x, fox_norm[layer]), w_fox_in[layer], b_fox_f[layer],
                              w_fox_out[layer])
        else:
            if layer == N_A_2:
                k_nope, k_rope, v = mla_shared_kv(x, kv_in_norm, w_dkv, kv_norm, w_uk, w_uv, cos, sin)
            j = layer - N_A_2
            x = x + mla_mixer(rmsnorm(x, mla_norm[j]), w_dq[j], q_norm[j], w_uq[j], w_mla_out[j],
                              k_nope, k_rope, v, cos, sin)
        x = x + conv_ffn(rmsnorm(x, ffn_norm[layer]), w_ffn_in[layer], ffn_conv_w[layer],
                         ffn_conv_b[layer], w_ffn_out[layer])
    return rmsnorm(x, final_norm)


def setup_inputs(seed=0):
    out = dict(first_inputs(seed))
    for name, value in second_inputs(seed + 1).items():
        if name != "x":
            out[name + "_2"] = value
    return out


def reference(
    x, c, ctx, c_ctx, ada_w, ada_b, norm1_g, norm2_g, final_g, cm_w_in, cm_ln_g, cm_ln_b,
    cm_w_s, cm_b_s, cm_w_out, ssm_w_in, ssm_lam_re, ssm_lam_im, ssm_log_step, ssm_b_re,
    ssm_b_im, ssm_c_re, ssm_c_im, ssm_d, ssm_w_out, peer_w_q, peer_keys, peer_u, peer_v,
    fox_norm_2, w_fox_in_2, b_fox_f_2, w_fox_out_2, kv_in_norm_2, w_dkv_2, kv_norm_2, w_uk_2,
    w_uv_2, mla_norm_2, w_dq_2, q_norm_2, w_uq_2, w_mla_out_2, ffn_norm_2, w_ffn_in_2,
    ffn_conv_w_2, ffn_conv_b_2, w_ffn_out_2, final_norm_2,
):
    x = first_block(
        x, c, ctx, c_ctx, ada_w, ada_b, norm1_g, norm2_g, final_g, cm_w_in, cm_ln_g, cm_ln_b,
        cm_w_s, cm_b_s, cm_w_out, ssm_w_in, ssm_lam_re, ssm_lam_im, ssm_log_step, ssm_b_re,
        ssm_b_im, ssm_c_re, ssm_c_im, ssm_d, ssm_w_out, peer_w_q, peer_keys, peer_u, peer_v,
    )
    return second_block(
        x, fox_norm_2, w_fox_in_2, b_fox_f_2, w_fox_out_2, kv_in_norm_2, w_dkv_2, kv_norm_2,
        w_uk_2, w_uv_2, mla_norm_2, w_dq_2, q_norm_2, w_uq_2, w_mla_out_2, ffn_norm_2,
        w_ffn_in_2, ffn_conv_w_2, ffn_conv_b_2, w_ffn_out_2, final_norm_2,
    )


_drawn_inputs = setup_inputs


def setup_inputs(seed=0):
    import zlib

    import numpy as np

    out = dict(_drawn_inputs(seed))
    spreads = {}
    factors = {'ctx': 8.0,
     'c_ctx': 8.0,
     'ada_b': 2.832,
     'norm1_g': 7.885,
     'norm2_g': 8.0,
     'final_g': 2.759,
     'cm_ln_g': 8.0,
     'cm_ln_b': 8.0,
     'cm_b_s': 8.0,
     'ssm_lam_re': 8.0,
     'ssm_lam_im': 3.269,
     'ssm_log_step': 4.484,
     'ssm_b_re': 4.671,
     'ssm_b_im': 4.797,
     'ssm_c_re': 4.796,
     'ssm_c_im': 4.724,
     'peer_w_q': 3.276,
     'peer_keys': 3.295,
     'peer_u': 3.658,
     'peer_v': 3.252,
     'fox_norm_2': 8.0,
     'kv_in_norm_2': 8.0,
     'kv_norm_2': 8.0,
     'mla_norm_2': 8.0,
     'q_norm_2': 8.0,
     'ffn_norm_2': 4.926,
     'ffn_conv_b_2': 8.0,
     'final_norm_2': 2.839}
    for name, (base, spread) in spreads.items():
        noise = np.random.default_rng([zlib.crc32(name.encode()), seed]).standard_normal(out[name].shape)
        drawn = base * np.exp(spread * noise) if base else spread * noise
        out[name] = __import__('jax').numpy.asarray(drawn.astype(out[name].dtype))
    for name, factor in factors.items():
        out[name] = (out[name] * factor).astype(out[name].dtype)
    return out
```

```python
import math
from contextlib import ExitStack

import numpy as np

import concourse.bass as bass
from concourse import mybir

ALU = mybir.AluOpType
ACT = mybir.ActivationFunctionType
F32 = mybir.dt.float32
U32 = mybir.dt.uint32
AX_X = mybir.AxisListType.X
ds = bass.ds

P = 128
D = 1024
KT = D // P
SEQ = 256
TOK = 2 * SEQ
DEPTH = 2
N_MOD = 6
EPS = 1e-6
GRID_W = 64
BLK = 2048
COLS = BLK // KT
SLOTS = 4
HEADS, KEYS, TOPK, DHALF = 8, 128, 16, 256
EXPERTS = KEYS * KEYS
RING = 8
GROUPS, GDIM, STATE = 64, 16, 64
T8 = 8
NBLK = TOK // T8
LATB = SEQ // T8
CG = 8
FOX_H, FOX_D = 16, 64
MLA_H, NOPE, ROPE, VD = 16, 128, 64, 128
KVL, QL = 256, 768
D_FF = 2816
FFC = D_FF // 256
NEG = -3.0e38
MASKED = -1.0e30
TWO_PI = 2.0 * math.pi
PI_A = 6.28125
PI_B = float(np.float32(round((TWO_PI - PI_A) * 2.0 ** 21) / 2.0 ** 21))
PI_C = TWO_PI - PI_A - PI_B
ROUND = 1.5 * 2.0 ** 23
PI_F = 3.1415925

C_ID, C_TRI, C_FOX, C_MLA, C_COS, C_SIN, C_IOTA = 0, 128, 512, 896, 1280, 1536, 1792
C_ALL = 1808
C_SUF = C_ALL


class Signal:

    def __init__(self, sem, credit=0):
        self.sem, self.total, self.credit = sem, credit, credit

    def plan(self, n):
        base = self.total
        self.total += n
        return base


class Chain:

    def __init__(self, sem):
        self.sem, self.n, self.it, self.per = sem, 0, None, 0

    def link(self, eng, ins):
        self.n += 1
        ins.then_inc(self.sem, 1)
        eng.wait_ge(self.sem, self.n if self.it is None else self.it * self.per + self.n)

    def enter(self, it, per):
        self.it, self.per, self.start = it, per, self.n

    def leave(self, rounds):
        assert self.n - self.start == self.per, (self.n - self.start, self.per)
        self.n = self.start + self.per * rounds
        self.it = None


class Stage:
    def __init__(self, sync=None, pe=None, act=None, dve=None, pool=None):
        self.sync, self.pe, self.act, self.dve, self.pool = sync, pe, act, dve, pool


def program(nc, t):
    with ExitStack() as ctx:
        def sb(name, shape, dt=F32):
            return ctx.enter_context(nc.sbuf_tensor(name, shape, dt))

        def sem(name):
            return ctx.enter_context(nc.semaphore(name))

        primed_sems = []

        def primed(name):
            primed_sems.append(sem(name))
            return primed_sems[-1]

        def dram(name, shape):
            return nc.dram_tensor(name, shape, F32, kind="Internal").ap()

        XA = sb("XA", [P, 4, D])
        H = sb("H", [P, 4, D])
        HT = sb("HT", [P, KT, TOK])
        W = sb("W", [P, SLOTS, BLK])
        CON = sb("CON", [P, C_ALL])
        AR = sb("AR", [P, 30208])
        SM = sb("SM", [P, 512])
        PS = ctx.enter_context(nc.psum_tensor("PS", [P, 8, 512], F32))

        u_scr = dram("u_scr", [TOK, D])
        y_scr = dram("y_scr", [SEQ, D])
        min_scr = dram("min_scr", [GROUPS // CG, P, CG * 2 * P])
        mout_scr = dram("mout_scr", [GROUPS // CG, P, 2 * CG * P])
        lag_scr = dram("lag_scr", [2, GROUPS, GDIM, (2 * T8 - 1) * GDIM])

        def view(off, *dims):
            n = int(np.prod(dims))
            assert off + n <= 30208
            ap = AR[:, off:off + n]
            if len(dims) == 2:
                return ap.rearrange("p (a b) -> p a b", a=dims[0])
            if len(dims) == 3:
                return ap.rearrange("p (a b c) -> p a b c", a=dims[0], b=dims[1])
            if len(dims) == 4:
                return ap.rearrange("p (a b c d) -> p a b c d", a=dims[0], b=dims[1], c=dims[2])
            return ap

        IDENT = CON[:, C_ID:C_ID + P]
        TRI = CON[:, C_TRI:C_TRI + 3 * P]
        FOX_MASK, MLA_MASK = CON[:, C_FOX:C_FOX + 3 * P], CON[:, C_MLA:C_MLA + 3 * P]
        COS, SIN = CON[:, C_COS:C_COS + SEQ], CON[:, C_SIN:C_SIN + SEQ]
        IOTA = CON[:, C_IOTA:C_IOTA + TOPK]
        MODX = [view(r * D, D) for r in range(N_MOD)]
        MODC = [view((N_MOD + r) * D, D) for r in range(N_MOD)]
        GAIN = view(29184, D)
        CB = view(20480, 2, KT, P)

        w_full = [sem(f"w_full{s}") for s in range(SLOTS)]
        w_used = [sem(f"w_used{s}") for s in range(SLOTS)]
        uses = [0] * SLOTS
        sums_taken = Signal(sem("sums_taken"), 64)
        x_ready = Signal(sem("x_ready"))
        n_sumsq = Signal(sem("n_sumsq"))
        n_var = Signal(sem("n_var"))
        n_std = Signal(sem("n_std"))
        n_h = Signal(sem("n_h"))
        n_turned = Signal(sem("n_turned"))
        n_ht = Signal(sem("n_ht"))
        gain_in = Signal(sem("gain_in"))
        parted = sem("parted")
        load_in = Signal(sem("load_in"))
        dve = Chain(sem("dve_chain"))
        act = Chain(sem("act_chain"))
        pool = Chain(sem("pool_chain"))
        v, a, g, pe, sp = nc.vector, nc.scalar, nc.gpsimd, nc.tensor, nc.sync

        def take(counts):
            base = list(uses)
            for s, n in enumerate(counts):
                uses[s] += n
            return base

        def load(slot, n, src, cols=BLK):
            sp.wait_ge(w_used[slot], n + 1)
            sp.dma_start(W[:, slot, 0:cols], src).then_inc(w_full[slot], 16)

        def wblock(w, i):
            return w[ds(i, 1)].rearrange("a p c -> (a p) c")

        def apart(eng):
            eng.sem_inc(parted, 1)

        def row(ap):
            return ap.partition_broadcast(P)

        def setup():
            in_sem, cs_done, cb_done = sem("inputs_in"), sem("silu_done"), sem("cond_spread")
            CV = view(18432, KT, 2)
            CS = SM[:, 44:44 + 2 * KT].rearrange("p (k c) -> p k c", c=2)
            xr = x_ready.plan(1)

            def sync():
                for one in w_used + primed_sems:
                    sp.sem_inc(one, 1)
                for signal in (sums_taken, u_used, v_used, y_taken, q_saved, s_saved):
                    sp.sem_inc(signal.sem, signal.credit)
                sp.dma_start(CV, t["cond"]).then_inc(in_sem, 16)
                sp.dma_start(XA[:, 0:2, :], t["x"].rearrange("(t p) d -> p t d", p=P)).then_inc(in_sem, 16)
                sp.dma_start(XA[:, 2:4, :], t["ctx"].rearrange("(t p) d -> p t d", p=P)).then_inc(in_sem, 16)
                sp.dma_start(H[:, 0:2, :], t["pos"].rearrange("(t p) d -> p t d", p=P)).then_inc(in_sem, 16)
                sp.dma_start(CON[:, :], t["consts"][:, 0:C_ALL]).then_inc(in_sem, 16)

            def act_():
                a.wait_ge(in_sem, 80)
                a.activation(CS, CV, ACT.Silu).then_inc(cs_done, 1)

            def dve_():
                v.wait_ge(in_sem, 80)
                v.tensor_tensor(XA[:, 0:2, :], XA[:, 0:2, :], H[:, 0:2, :], ALU.add).then_inc(x_ready.sem, 1)

            return Stage(sync=sync, act=act_, dve=dve_), cs_done, CS

        def ada(layer, rows_c, cs_done, CS):
            uw = take([N_MOD] * SLOTS)
            n_c = rows_c * SLOTS
            st = sums_taken.plan(N_MOD * SLOTS + n_c)
            li = load_in.plan(32)
            cb_done = sem(f"cond_spread{layer}")
            xr = x_ready.total

            def sync():
                if layer:
                    sp.wait_ge(x_ready.sem, xr)
                for base, n in ((0, N_MOD), (N_MOD, rows_c)):
                    sp.dma_start(AR[:, base * D:(base + n) * D], row(t["ada_b"][layer, 0:n * D])).then_inc(load_in.sem, 16)
                with sp.Fori(0, N_MOD) as r:
                    for s in range(SLOTS):
                        load(s, r + uw[s], wblock(t[f"ada_w{layer}"], r * SLOTS + s))

            def loops(eng):
                return [(0, rows_c, 2)] + ([(rows_c, N_MOD, 1)] if rows_c < N_MOD else [])

            def pe_():
                pe.wait_ge(cb_done, 2)
                before = 0
                for lo, hi, ns in loops(pe):
                    with pe.Fori(lo, hi) as r:
                        for s in range(SLOTS):
                            pe.wait_ge(w_full[s], (r + uw[s] + 1) * 16)
                            pe.wait_ge(sums_taken.sem, r * (SLOTS * ns) + (st + before - lo * SLOTS * ns + (s - 3) * ns))
                            for c in range(ns):
                                for k in range(KT):
                                    mm = pe.matmul(PS[:, s, c * COLS:(c + 1) * COLS], CB[:, c, k, :],
                                                   W[:, s, k * COLS:(k + 1) * COLS], start=(k == 0), stop=(k == KT - 1))
                            mm.then_inc(w_used[s], 1)
                    before += (hi - lo) * SLOTS * ns

            def dve_():
                if layer:
                    v.wait_ge(x_ready.sem, xr)
                v.wait_ge(cs_done, 1)
                v.wait_ge(load_in.sem, li + 32)
                for c in range(2):
                    v.tensor_copy(CB[:, c], CS[:, :, c].unsqueeze(2).to_broadcast([P, KT, P])).then_inc(cb_done, 1)
                for lo, hi, ns in loops(v):
                    with v.Fori(lo, hi) as r:
                        for s in range(SLOTS):
                            v.wait_ge(w_used[s], r + uw[s] + 2)
                            for c in range(ns):
                                dst = AR[:, ds(r * D + (c * N_MOD * D + s * COLS), COLS)]
                                v.tensor_tensor(dst, dst, PS[:, s, c * COLS:(c + 1) * COLS], ALU.add).then_inc(sums_taken.sem, 1)

            return Stage(sync=sync, pe=pe_, dve=dve_)

        NEPS = SM[:, 0:1]
        SUMSQ, VAR, STD, RSTD = (SM[:, 4 + 4 * i:8 + 4 * i] for i in range(4))

        def norm(src, tbs, gain=None, mod=None, dst=None, width=D, junk=None, out_ht=True, ht_off=0):
            src = src or (lambda tb: XA[:, tb, :])
            dst = dst or (lambda tb: H[:, tb, :])
            n = len(tbs)
            xr = x_ready.total
            ss, va, sd, hh = n_sumsq.plan(n), n_var.plan(n), n_std.plan(n), n_h.plan(n)
            kt = width // P
            halves = (kt + 3) // 4
            tu, ht = n_turned.plan(n * halves), n_ht.plan(n * halves)
            gi = gain_in.plan(16)
            grow = GAIN[:, 0:width]

            def sync():
                sp.wait_ge(x_ready.sem, xr)
                if hh:
                    sp.wait_ge(n_h.sem, hh)
                sp.dma_start(grow, row(gain)).then_inc(gain_in.sem, 16)

            def act_():
                a.wait_ge(x_ready.sem, xr)
                if hh:
                    a.wait_ge(n_h.sem, hh)
                if tu:
                    a.wait_ge(n_turned.sem, tu)
                for i, tb in enumerate(tbs):
                    a.activation((junk or dst)(tb), src(tb), ACT.Square, accum_out=SUMSQ[:, i:i + 1]).then_inc(n_sumsq.sem, 1)
                for i, tb in enumerate(tbs):
                    a.wait_ge(n_var.sem, va + i + 1)
                    a.activation(STD[:, i:i + 1], VAR[:, i:i + 1], ACT.Sqrt).then_inc(n_std.sem, 1)
                if not out_ht:
                    return
                for i, tb in enumerate(tbs):
                    for q in range(halves):
                        m = min(4, kt - 4 * q)
                        a.wait_ge(n_turned.sem, tu + i * halves + q + 1)
                        a.copy(HT[:, 4 * q:4 * q + m, ht_off + i * P:ht_off + (i + 1) * P],
                               PS[:, 4 + (i * halves + q) % 4, 0:m * P].rearrange("p (k t) -> p k t", k=m)).then_inc(n_ht.sem, 1)

            def dve_():
                for i, tb in enumerate(tbs):
                    v.wait_ge(n_sumsq.sem, ss + i + 1)
                    v.tensor_scalar(VAR[:, i:i + 1], SUMSQ[:, i:i + 1], 1.0 / width, EPS, ALU.mult, ALU.add).then_inc(n_var.sem, 1)
                v.wait_ge(gain_in.sem, gi + 16)
                if mod:
                    for shift, scale in dict.fromkeys(mod):
                        sc = AR[:, scale:scale + D]
                        dve.link(v, v.scalar_tensor_tensor(sc, sc, 1.0, grow, ALU.add, ALU.mult))
                for i, tb in enumerate(tbs):
                    v.wait_ge(n_std.sem, sd + i + 1)
                    dve.link(v, v.reciprocal(RSTD[:, i:i + 1], STD[:, i:i + 1]))
                    mul = AR[:, mod[i][1]:mod[i][1] + D] if mod else grow
                    one = v.scalar_tensor_tensor(dst(tb), src(tb), RSTD[:, i:i + 1], mul, ALU.mult, ALU.mult)
                    if mod:
                        dve.link(v, one)
                        one = v.tensor_tensor(dst(tb), dst(tb), AR[:, mod[i][0]:mod[i][0] + D], ALU.add)
                    one.then_inc(n_h.sem, 1)

            def pe_():
                if not out_ht:
                    return
                for i, tb in enumerate(tbs):
                    pe.wait_ge(n_h.sem, hh + i + 1)
                    for q in range(halves):
                        b = i * halves + q
                        if b >= 4:
                            pe.wait_ge(n_ht.sem, ht + b - 3)
                        elif ht:
                            pe.wait_ge(n_ht.sem, ht)
                        m = min(4, kt - 4 * q)
                        for k in range(m):
                            mm = pe.transpose(PS[:, 4 + b % 4, k * P:(k + 1) * P],
                                              dst(tb)[:, (4 * q + k) * P:(4 * q + k + 1) * P], IDENT)
                        mm.then_inc(n_turned.sem, 1)

            if not out_ht:
                n_turned.total -= n * halves
                n_ht.total -= n * halves
            return Stage(sync=sync, pe=pe_ , act=act_, dve=dve_)

        def turn(src, tbs, kt, ready, ready_at, dst):
            halves = kt // 4
            n = len(tbs)
            tu, ht = n_turned.plan(n * halves), n_ht.plan(n * halves)

            def pe_():
                for i, tb in enumerate(tbs):
                    pe.wait_ge(ready, ready_at(i))
                    for q in range(halves):
                        b = i * halves + q
                        pe.wait_ge(n_ht.sem, ht + max(0, b - 3))
                        for k in range(4):
                            mm = pe.transpose(PS[:, 4 + b % 4, k * P:(k + 1) * P],
                                              src(tb)[:, (4 * q + k) * P:(4 * q + k + 1) * P], IDENT)
                        mm.then_inc(n_turned.sem, 1)

            def act_():
                for i, tb in enumerate(tbs):
                    for q in range(halves):
                        b = i * halves + q
                        a.wait_ge(n_turned.sem, tu + b + 1)
                        a.copy(dst(q, i), PS[:, 4 + b % 4, :].rearrange("p (k t) -> p k t", k=4)).then_inc(n_ht.sem, 1)

            return pe_, act_, ht + n * halves

        def linear(w, nblk, ntb, lhs, evac, unroll=4, ht_at=None, kt=KT):
            uw = take([nblk // unroll if s < unroll else 0 for s in range(SLOTS)])
            st = sums_taken.plan(nblk * ntb)
            rounds = nblk // unroll
            cols = BLK // kt

            def sync():
                with sp.Fori(0, rounds) as r:
                    for s in range(unroll):
                        load(s, r + uw[s], wblock(w, r * unroll + s))

            def bank(s, tb):
                return PS[:, (s % 2) * 2 + tb // 2, (tb % 2) * cols:(tb % 2 + 1) * cols]

            def pe_():
                if ht_at is not None:
                    pe.wait_ge(n_ht.sem, ht_at)
                pe.wait_ge(sums_taken.sem, st)
                with pe.Fori(0, rounds) as r:
                    for s in range(unroll):
                        pe.wait_ge(w_full[s], (r + uw[s] + 1) * 16)
                        pe.wait_ge(sums_taken.sem, r * (unroll * ntb) + (st + (s - 1) * ntb))
                        for tb in range(ntb):
                            for k in range(kt):
                                mm = pe.matmul(bank(s, tb), lhs(k, tb), W[:, s, k * cols:(k + 1) * cols],
                                               start=(k == 0), stop=(k == kt - 1))
                        mm.then_inc(w_used[s], 1)

            def take_sums(eng, chain=None, per=0):
                with eng.Fori(0, rounds) as r:
                    if chain:
                        chain.enter(r, per)
                    for s in range(unroll):
                        eng.wait_ge(w_used[s], r + uw[s] + 2)
                        for tb in range(ntb):
                            evac(r * unroll + s, tb, bank(s, tb)).then_inc(sums_taken.sem, 1)
                if chain:
                    chain.leave(rounds)

            return sync, pe_, take_sums, st + nblk * ntb

        def add_gated(gate_of, ntb, tmp, cols=COLS):
            def evac(blk, tb, sums):
                dst = XA[:, tb, ds(blk * cols, cols)]
                if gate_of is None:
                    return v.tensor_tensor(dst, dst, sums, ALU.add)
                half = tmp[:, tb % 2, :]
                dve.link(v, v.tensor_tensor(half, sums, AR[:, ds(blk * cols + gate_of(tb), cols)], ALU.mult))
                return v.tensor_tensor(dst, dst, half, ALU.add)
            return evac

        def mark_x(n_h_unused=None):
            x_ready.plan(1)

            def dve_():
                v.wait_ge(sums_taken.sem, sums_now[0])
                v.memset(SM[:, 500:501], 0.0).then_inc(x_ready.sem, 1)
            sums_now = [sums_taken.total]
            return dve_

        def chunk_mixer(ht_at):
            Z = view(12288, 4, 2 * D)
            WS = view(20480, KT, P)
            BS = view(21504, KT)
            LNG, LNB = view(22528, D), view(23552, D)
            JUNK = view(24576, D)
            TMP = view(25600, 2, COLS)
            MEAN, NMEAN, VARV, STDV, RV = (SM[:, 24 + 4 * i:28 + 4 * i] for i in range(5))
            z_done = sem("z_done")
            mean_done, nmean_done, var_sum, var_done, std_done, v_done = (sem("cm_" + n) for n in
                ("sum", "negmean", "sqsum", "var", "std", "v"))
            mix_done, mixed = sem("cm_spatial"), sem("cm_mixed")
            li = load_in.plan(64)
            par_in = load_in.sem

            def gelu_out(blk, tb, sums):
                return a.activation(Z[:, tb, ds(blk * COLS, COLS)], sums, ACT.Gelu_apprx_tanh)

            in_sync, in_pe, in_take, in_end = linear(t["cm_w_in"], 8, 4, lambda k, tb: HT[:, k, tb * P:(tb + 1) * P],
                                                     gelu_out, ht_at=ht_at)
            turn_pe, turn_act, turn_end = turn(lambda tb: Z[:, tb, 0:D], range(4), KT, mixed, lambda i: 8 * (i + 1),
                                               lambda q, i: HT[:, 4 * q:4 * q + 4, i * P:(i + 1) * P])
            out_sync, out_pe, out_take, out_end = linear(t["cm_w_out"], 4, 4, lambda k, tb: HT[:, k, tb * P:(tb + 1) * P],
                                                         add_gated(lambda tb: (2 if tb < 2 else 8) * D, 4, TMP), ht_at=turn_end)
            mark = mark_x()
            cb_free = n_h.total

            def sync():
                sp.wait_ge(n_h.sem, cb_free)
                sp.dma_start(WS, t["cm_ws"]).then_inc(par_in, 16)
                sp.dma_start(BS, t["cm_bs"]).then_inc(par_in, 16)
                sp.dma_start(LNG, row(t["cm_ln_g"])).then_inc(par_in, 16)
                sp.dma_start(LNB, row(t["cm_ln_b"])).then_inc(par_in, 16)
                in_sync()
                out_sync()

            def act_():
                in_take(a)
                a.wait_ge(sums_taken.sem, in_end)
                for tb in range(4):
                    a.activation(JUNK, Z[:, tb, D:2 * D], ACT.Copy, accum_out=MEAN[:, tb:tb + 1]).then_inc(mean_done, 1)
                    a.wait_ge(mean_done, tb + 1)
                for tb in range(4):
                    a.wait_ge(nmean_done, tb + 1)
                    a.activation(JUNK, Z[:, tb, D:2 * D], ACT.Square, bias=NMEAN[:, tb:tb + 1],
                                 accum_out=VARV[:, tb:tb + 1]).then_inc(var_sum, 1)
                    a.wait_ge(var_sum, tb + 1)
                for tb in range(4):
                    a.wait_ge(var_done, tb + 1)
                    a.activation(STDV[:, tb:tb + 1], VARV[:, tb:tb + 1], ACT.Sqrt).then_inc(std_done, 1)
                turn_act()

            def dve_():
                for tb in range(4):
                    v.wait_ge(mean_done, tb + 1)
                    v.tensor_scalar(NMEAN[:, tb:tb + 1], MEAN[:, tb:tb + 1], -1.0 / D, None, ALU.mult).then_inc(nmean_done, 1)
                for tb in range(4):
                    v.wait_ge(var_sum, tb + 1)
                    v.tensor_scalar(VARV[:, tb:tb + 1], VARV[:, tb:tb + 1], 1.0 / D, EPS, ALU.mult, ALU.add).then_inc(var_done, 1)
                v.wait_ge(par_in, li + 64)
                v.wait_ge(nmean_done, 4)
                for tb in range(4):
                    zv = Z[:, tb, D:2 * D]
                    v.wait_ge(std_done, tb + 1)
                    dve.link(v, v.reciprocal(RV[:, tb:tb + 1], STDV[:, tb:tb + 1]))
                    dve.link(v, v.tensor_scalar(zv, zv, NMEAN[:, tb:tb + 1], RV[:, tb:tb + 1], ALU.add, ALU.mult))
                    dve.link(v, v.tensor_tensor(zv, zv, LNG, ALU.mult))
                    v.tensor_tensor(zv, zv, LNB, ALU.add).then_inc(v_done, 1)
                for tb in range(4):
                    v.wait_ge(mix_done, tb + 1)
                    for h in range(KT):
                        u = Z[:, tb, h * P:(h + 1) * P]
                        v.scalar_tensor_tensor(u, PS[:, 4 + (tb % 2) * 2 + h // 4, (h % 4) * P:(h % 4 + 1) * P], BS[:, h:h + 1], u,
                                               ALU.add, ALU.mult).then_inc(mixed, 1)
                out_take(v, dve, 16)
                mark()

            def pe_():
                in_pe()
                pe.wait_ge(par_in, li + 64)
                for tb in range(4):
                    pe.wait_ge(v_done, tb + 1)
                    if tb >= 2:
                        pe.wait_ge(mixed, 8 * (tb - 1))
                    for h in range(KT):
                        mm = pe.matmul(PS[:, 4 + (tb % 2) * 2 + h // 4, (h % 4) * P:(h % 4 + 1) * P], WS[:, h, :],
                                       Z[:, tb, D + h * P:D + (h + 1) * P], start=True, stop=True)
                    mm.then_inc(mix_done, 1)
                pe.wait_ge(mixed, 32)
                turn_pe()
                out_pe()

            return Stage(sync=sync, act=act_, dve=dve_, pe=pe_)

        u_full = [sem(f"u_full{s}") for s in range(RING)]
        v_full = [sem(f"v_full{s}") for s in range(RING)]
        u_used, v_used = Signal(sem("u_used"), RING), Signal(sem("v_used"), RING)
        keys_in, q_saved = Signal(sem("keys_in")), Signal(sem("q_saved"), 2)
        q_sums = Signal(sem("q_sums"))
        s_sums, s_saved = Signal(sem("s_sums")), Signal(sem("s_saved"), 2)
        ids_ready, top_shift, exp_done = Signal(sem("ids_ready")), Signal(sem("top_shift")), Signal(sem("exp_done"))
        gelu_done, w_ready, diag_ready = Signal(sem("gelu_done")), Signal(sem("w_ready")), Signal(sem("diag_ready"))
        y_taken = Signal(sem("y_taken"), 2)
        ring_use = [0]

        def peer(layer, ntb, ht_at):
            T = ntb * P
            UB = view(12288, RING, D)
            VB = [view(i * D, D) for i in range(4)] + [view((6 + i) * D, D) for i in range(4)]
            KEY = view(20480, HEADS, 4, KEYS)
            QT = view(24576, 4, TOK)
            S = view(26624, 4, 2, KEYS)
            CAND, CAND2 = view(27648, 2 * KEYS), view(27904, 2 * KEYS)
            S2 = view(28160, 2, KEYS)
            OH = view(28416, 2, TOPK, TOPK)
            DIAG = view(4 * D, 4, P)
            YG = view(10 * D, D)
            at = 64
            TV, IXF, TAB, K12 = (SM[:, at + 32 * i:at + 32 * (i + 1)].rearrange("p (h k) -> p h k", h=2) for i in range(4))
            TI = SM[:, 192:224].bitcast(U32).rearrange("p (h k) -> p h k", h=2)
            TABU = SM[:, 224:256].bitcast(U32).rearrange("p (h k) -> p h k", h=2)
            TS, EX = view(28928, 4, TOPK), view(28992, 4, TOPK)
            TC = SM[:, 272:288].bitcast(U32)
            NTOP, SUM = view(29056, 4), view(29060, 4)
            RSUM = SM[:, 306:307]
            EX2 = view(4 * D + 640, TOPK)
            ACTV = SM[:, 308:372].rearrange("p (t k) -> p t k", t=4)
            GELU = SM[:, 372:436].rearrange("p (t k) -> p t k", t=4)
            GATE = SM[:, 436:500].rearrange("p (t k) -> p t k", t=4)
            WGT = GELU
            IDS = view(4 * D + 512, 4, TOPK).bitcast(U32)
            IDP = view(4 * D + 576, 4, TOPK).bitcast(U32)

            n = HEADS * ntb
            rows_n = n * TOPK
            per_slot = ntb * TOPK // RING
            rb = ring_use[0]
            ring_use[0] += HEADS * per_slot
            uw = take([HEADS, HEADS, 0, 0])
            uu, vu = u_used.plan(rows_n), v_used.plan(rows_n)
            ki = keys_in.plan(16)
            qm, qs = q_sums.plan(HEADS * 2), q_saved.plan(HEADS * 4)
            sm_, sv = s_sums.plan(n), s_saved.plan(n)
            ir, tsh, ed = ids_ready.plan(n), top_shift.plan(n), exp_done.plan(n)
            gd, wr, dr = gelu_done.plan(n), w_ready.plan(n), diag_ready.plan(rows_n)
            yt = y_taken.plan(n)
            hh = n_h.total
            st = sums_taken.total
            xr = x_ready.plan(1)
            H_ROWS = ntb * TOPK

            def sync():
                sp.wait_ge(n_h.sem, hh)
                sp.dma_start(KEY, t["peer_keys"][layer].rearrange("p h a b k -> p h (a b) k")).then_inc(keys_in.sem, 16)
                with sp.Fori(0, HEADS) as h:
                    for s in range(2):
                        load(s, h + uw[s], wblock(t[f"peer_w_q{layer}"], h * 2 + s))

            def queries(h):
                for j in range(4):
                    if j % 2 == 0:
                        pe.wait_ge(w_full[j // 2], (h + uw[j // 2] + 1) * 16)
                    pe.wait_ge(q_saved.sem, h * 4 + (qs + j - 1))
                    for k in range(KT):
                        mm = pe.matmul(PS[:, j % 2, 0:T], W[:, j // 2, k * COLS + (j % 2) * P:k * COLS + (j % 2 + 1) * P],
                                       HT[:, k, 0:T], start=(k == 0), stop=(k == KT - 1))
                    mm.then_inc(w_used[j // 2] if j % 2 else q_sums.sem, 1)
                pe.wait_ge(q_saved.sem, h * 4 + (qs + 4))
                for tb in range(ntb):
                    pe.wait_ge(s_saved.sem, h * ntb + (sv + tb - 1))
                    for half in range(2):
                        for c in range(2):
                            mm = pe.matmul(PS[:, 2 + tb % 2, half * KEYS:(half + 1) * KEYS],
                                           QT[:, half * 2 + c, tb * P:(tb + 1) * P],
                                           KEY[:, ds(h, 1), half * 2 + c, :].rearrange("p a k -> p (a k)"),
                                           start=(c == 0), stop=(c == 1))
                    mm.then_inc(s_sums.sem, 1)

            def pe_head(h, more):
                if more:
                    queries(h + 1)
                for tb in range(ntb):
                    pe.wait_ge(y_taken.sem, h * ntb + (yt + tb - 1))
                    for k in range(TOPK):
                        i = tb * TOPK + k
                        pe.wait_ge(diag_ready.sem, h * H_ROWS + (dr + i + 1))
                        pe.wait_ge(v_full[i % RING], (h * per_slot + (rb + i // RING + 1)) * 16)
                        for c in range(2):
                            mm = pe.matmul(PS[:, 4 + (tb % 2) * 2 + c, :], DIAG[:, k % 4, :], VB[i % RING][:, c * 512:(c + 1) * 512],
                                           start=(k == 0), stop=(k == TOPK - 1))
                        mm.then_inc(v_used.sem, 1)

            def pe_():
                pe.wait_ge(n_ht.sem, ht_at)
                pe.wait_ge(sums_taken.sem, st)
                pe.wait_ge(keys_in.sem, ki + 16)
                queries(0)
                with pe.Fori(0, HEADS - 1) as h:
                    pe_head(h, True)
                pe_head(HEADS - 1, False)

            def save_queries(h):
                for j in range(4):
                    if j % 2:
                        a.wait_ge(w_used[j // 2], h + (uw[j // 2] + 2))
                    else:
                        a.wait_ge(q_sums.sem, h * 2 + (qm + j // 2 + 1))
                    a.copy(QT[:, j, 0:T], PS[:, j % 2, 0:T]).then_inc(q_saved.sem, 1)
                for tb in range(ntb):
                    a.wait_ge(s_sums.sem, h * ntb + (sm_ + tb + 1))
                    a.wait_ge(ids_ready.sem, h * ntb + (ir + tb + 1 - ntb) if not isinstance(h, int) else ir)
                    a.copy(S[:, tb], PS[:, 2 + tb % 2, 0:2 * KEYS].rearrange("p (h k) -> p h k", h=2)).then_inc(s_saved.sem, 1)

            def exps(h, tb):
                a.wait_ge(top_shift.sem, h * ntb + (tsh + tb + 1))
                a.activation(EX[:, tb, :], TS[:, tb, :], ACT.Exp, bias=NTOP[:, tb:tb + 1], accum_out=SUM[:, tb:tb + 1]).then_inc(exp_done.sem, 1)

            def act_head(h, more):
                if more:
                    save_queries(h + 1)
                for tb in range(ntb):
                    a.wait_ge(u_used.sem, h * H_ROWS + (uu + (tb + 1) * TOPK))
                    a.activation(GELU[:, tb, :], ACTV[:, tb, :], ACT.Gelu_apprx_tanh).then_inc(gelu_done.sem, 1)
                    a.wait_ge(w_ready.sem, h * ntb + (wr + tb + 1))
                    for k in range(TOPK):
                        a.wait_ge(v_used.sem, h * H_ROWS + (vu + tb * TOPK + k - 3))
                        a.mul(DIAG[:, k % 4, :], IDENT, WGT[:, tb, k:k + 1]).then_inc(diag_ready.sem, 1)
                    if more:
                        exps(h + 1, tb)

            def act_():
                a.wait_ge(n_h.sem, hh)
                save_queries(0)
                for tb in range(ntb):
                    exps(0, tb)
                with a.Fori(0, HEADS - 1) as h:
                    act_head(h, True)
                act_head(HEADS - 1, False)

            def best16(vals, ix, src, scratch):
                m = len(src)
                apart(v)
                for j in range(m):
                    last = v.max(vals[j][:, 0:8], src[j])
                dve.link(v, last)
                apart(v)
                for j in range(m):
                    v.max_index(ix[j][:, 0:8], vals[j][:, 0:8], src[j])
                    last = v.match_replace(scratch[j], vals[j][:, 0:8], src[j], NEG)
                dve.link(v, last)
                apart(v)
                for j in range(m):
                    last = v.max(vals[j][:, 8:16], scratch[j])
                dve.link(v, last)
                apart(v)
                for j in range(m):
                    last = v.max_index(ix[j][:, 8:16], vals[j][:, 8:16], scratch[j])
                dve.link(v, last)

            def choose(h, tb):
                v.wait_ge(s_saved.sem, h * ntb + (sv + tb + 1))
                best16([TV[:, 0, :], TV[:, 1, :]], [TI[:, 0, :], TI[:, 1, :]], [S[:, tb, 0, :], S[:, tb, 1, :]],
                       [S2[:, 0, :], S2[:, 1, :]])
                v.tensor_copy(IXF, TI)
                dve.link(v, v.tensor_tensor(CAND.rearrange("p (a b) -> p a b", a=TOPK),
                                            TV[:, 0, :].unsqueeze(2).to_broadcast([P, TOPK, TOPK]),
                                            TV[:, 1, :].unsqueeze(1).to_broadcast([P, TOPK, TOPK]), ALU.add))
                best16([TS[:, tb, :]], [TC], [CAND], [CAND2])
                v.tensor_scalar(NTOP[:, tb:tb + 1], TS[:, tb, 0:1], -1.0, None, ALU.mult).then_inc(top_shift.sem, 1)
                v.tensor_scalar(TABU[:, 0, :], TC, 4, None, ALU.logical_shift_right)
                dve.link(v, v.tensor_scalar(TABU[:, 1, :], TC, 15, None, ALU.bitwise_and))
                dve.link(v, v.tensor_copy(TAB, TABU))
                flat = OH.rearrange("p h k j -> p (h k) j")
                dve.link(v, v.tensor_tensor(flat, TAB.rearrange("p h k -> p (h k)").unsqueeze(2).to_broadcast([P, 2 * TOPK, TOPK]),
                                            IOTA.unsqueeze(1).to_broadcast([P, 2 * TOPK, TOPK]), ALU.is_equal))
                dve.link(v, v.tensor_tensor(OH, OH, IXF.unsqueeze(2).to_broadcast([P, 2, TOPK, TOPK]), ALU.mult))
                dve.link(v, v.tensor_reduce(K12.rearrange("p h k -> p (h k)"), flat, AX_X, ALU.add))
                dve.link(v, v.scalar_tensor_tensor(EX2, K12[:, 0, :], float(KEYS), K12[:, 1, :], ALU.mult, ALU.add))
                v.tensor_scalar(IDS[:, tb, :], EX2, float(layer * EXPERTS), None, ALU.add).then_inc(ids_ready.sem, 1)

            def gates(h, tb):
                v.wait_ge(exp_done.sem, h * ntb + (ed + tb + 1))
                dve.link(v, v.reciprocal(RSUM, SUM[:, tb:tb + 1]))
                dve.link(v, v.tensor_scalar(GATE[:, tb, :], EX[:, tb, :], RSUM, None, ALU.mult))

            def add_rows(m):
                h, tb = m
                v.wait_ge(v_used.sem, h * H_ROWS + (vu + (tb + 1) * TOPK))
                gate = MODX[5] if tb < 2 else MODC[5]
                sums = PS[:, 4 + (tb % 2) * 2:6 + (tb % 2) * 2, :].rearrange("p a b -> p (a b)")
                dve.link(v, v.tensor_tensor(YG, sums, gate, ALU.mult))
                v.tensor_tensor(XA[:, tb, :], XA[:, tb, :], YG, ALU.add).then_inc(y_taken.sem, 1)

            def dve_head(h, more, before=True):
                for tb in range(ntb):
                    for k in range(TOPK):
                        i = tb * TOPK + k
                        v.wait_ge(u_full[i % RING], (h * per_slot + (rb + i // RING + 1)) * 16)
                        v.tensor_tensor_reduce(UB[:, i % RING, :], UB[:, i % RING, :], H[:, tb, :], 1.0, 0.0,
                                               ALU.mult, ALU.add, ACTV[:, tb, k:k + 1]).then_inc(u_used.sem, 1)
                    if tb:
                        add_rows((h, tb - 1))
                    elif before:
                        add_rows((h - 1, ntb - 1))
                        gates(h, ntb - 1)
                    v.wait_ge(gelu_done.sem, h * ntb + (gd + tb + 1))
                    v.tensor_tensor(WGT[:, tb, :], GELU[:, tb, :], GATE[:, tb, :], ALU.mult).then_inc(w_ready.sem, 1)
                    if more:
                        if tb:
                            gates(h + 1, tb - 1)
                        choose(h + 1, tb)

            LINKS = 15

            def dve_():
                v.wait_ge(n_h.sem, hh)
                for tb in range(ntb):
                    choose(0, tb)
                    gates(0, tb)
                dve_head(0, True, before=False)
                with v.Fori(1, HEADS - 1) as h:
                    dve.enter(h - 1, ntb * (LINKS + 2 + 1))
                    dve_head(h, True)
                    dve.leave(HEADS - 2)
                dve_head(HEADS - 1, False)
                add_rows((HEADS - 1, ntb - 1))
                v.wait_ge(y_taken.sem, yt + n)
                v.memset(SM[:, 500:501], 0.0).then_inc(x_ready.sem, 1)

            def pool_head(h):
                def fetch(tb, k, table, ring, full, used):
                    i = tb * TOPK + k
                    g.wait_ge(used[0].sem, h * H_ROWS + (used[1] + i + 1 - RING))
                    apart(g)
                    g.indirect_dma_start(out=ring[i % RING], out_offset=None, in_=table,
                                         in_offset=bass.IndirectOffsetOnAxis(ap=IDP[:, tb, k:k + 1], axis=0)).then_inc(full[i % RING], 16)

                ub = [UB[:, i, :] for i in range(RING)]
                for tb in range(ntb + 1):
                    if tb < ntb:
                        g.wait_ge(ids_ready.sem, h * ntb + (ir + tb + 1))
                        apart(g)
                        pool.link(g, g.tensor_copy(IDP[:, tb, :], IDS[:, tb, :]))
                    for k in range(TOPK):
                        if tb < ntb:
                            fetch(tb, k, t["peer_u"], ub, u_full, (u_used, uu))
                        if tb:
                            fetch(tb - 1, k, t["peer_v"], VB, v_full, (v_used, vu))

            def pool_():
                with g.Fori(0, HEADS) as h:
                    pool.enter(h, ntb)
                    pool_head(h)
                    pool.leave(HEADS)

            return Stage(sync=sync, pe=pe_, act=act_, dve=dve_, pool=pool_)

        NCH = GROUPS // CG
        A8R = SM[:, 64:192].rearrange("p (r g) -> p r g", r=2)
        A8S = SM[:, 192:320].rearrange("p (r g) -> p r g", r=2)
        mats_stored = Signal(sem("mats_stored"))

        def ssm_matrices():
            at = [6144]

            def new(*dims):
                ap = view(at[0], *dims)
                at[0] += int(np.prod(dims))
                return ap

            G_ = GROUPS
            LR, LI, LOGS, STEP, E, MAG, TH, K, RED, SN, CS_, A_R, A_I, DEN, X1, X2, CO_R, CO_I = (new(1, G_) for _ in range(18))
            BR, BI, CR, CI, BBR, BBI = (new(G_, GDIM) for _ in range(6))
            T1, T2 = new(G_, GDIM), new(G_, GDIM)
            PR, PI = new(T8 + 1, G_), new(T8 + 1, G_)
            INR, INI, OUTR, OUTI = (new(T8, G_) for _ in range(4))
            MIN = new(2, CG, T8 * GDIM)
            MOUT = new(2, CG, T8 * GDIM)
            CST = new(2, CG, GDIM)
            MT = new(CG * 2, P)
            KS = new(CG, 2, GDIM)
            ZERO = view(0, GDIM * (2 * T8 - 1) * GDIM)[0:GROUPS]
            par_in, zero_done = sem("ssm_par_in"), sem("ssm_zero")
            lr_done, e_done, mag_done, th_done, sin_done = (sem("ssm_" + n) for n in ("lr", "step", "mag", "theta", "sin"))
            min_done, mout_done = sem("ssm_min"), sem("ssm_mout")
            mt_sums, k_sums = primed("ssm_turned"), primed("ssm_lags")
            mt_saved, k_saved = primed("ssm_min_saved"), primed("ssm_lags_saved")
            mt_out, mout_out, k_out = primed("ssm_min_out"), primed("ssm_mout_out"), primed("ssm_lags_out")
            zero_out = sem("ssm_zero_out")
            N_K = 2 * T8 * 16
            xr = x_ready.total

            def sync():
                sp.wait_ge(x_ready.sem, xr)
                for dst, name in ((LR[:, 0], "ssm_lr"), (LI[:, 0], "ssm_li"), (LOGS[:, 0], "ssm_ls"), (BR, "ssm_br"), (BI, "ssm_bi"),
                                  (CR, "ssm_cr"), (CI, "ssm_ci")):
                    sp.dma_start(dst, t[name]).then_inc(par_in, 16)
                sp.wait_ge(zero_done, 1)
                for d in range(2):
                    sp.dma_start(lag_scr[d].rearrange("g c l -> g (c l)"), ZERO).then_inc(zero_out, 16)
                sp.wait_ge(zero_out, 32)
                with sp.Fori(0, NCH) as c:
                    sp.wait_ge(mout_done, c + 1)
                    sp.dma_start(wblock(mout_scr, c), MOUT.rearrange("p r g x -> p (r g x)")).then_inc(mout_out, 16)
                    sp.wait_ge(mt_saved, 1 + c + 1)
                    sp.dma_start(wblock(min_scr, c), MT.rearrange("p g x -> p (g x)")).then_inc(mt_out, 16)
                    sp.wait_ge(k_saved, 1 + c * 2 + 2)
                    for d in range(2):
                        for s in range(T8):
                            j = s + d * (T8 - 1)
                            sp.dma_start(lag_scr[d, ds(c * CG, CG), :, j * GDIM:(j + 1) * GDIM].rearrange("g c x -> c g x"),
                                         KS[s * GDIM:(s + 1) * GDIM, :, d, :]).then_inc(k_out, 16)
                sp.wait_ge(mt_out, 1 + 16 * NCH)
                sp.wait_ge(mout_out, 1 + 16 * NCH)
                sp.wait_ge(k_out, 1 + N_K * NCH)

            def act_():
                a.wait_ge(par_in, 112)
                a.activation(STEP[:, 0], LOGS[:, 0], ACT.Exp).then_inc(lr_done, 1)
                a.wait_ge(e_done, 1)
                a.activation(MAG[:, 0], E[:, 0], ACT.Exp).then_inc(mag_done, 1)
                a.wait_ge(th_done, 1)
                a.activation(SN[:, 0], RED[:, 0], ACT.Sin).then_inc(sin_done, 1)
                a.wait_ge(th_done, 2)
                a.activation(CS_[:, 0], X1[:, 0], ACT.Sin).then_inc(sin_done, 1)
                with a.Fori(0, NCH) as c:
                    a.wait_ge(mt_sums, 1 + c + 1)
                    a.wait_ge(mt_out, 1 + c * 16)
                    a.copy(MT.rearrange("p (b g) x -> p b (g x)", b=4), PS[:, 0:4, :]).then_inc(mt_saved, 1)
                    a.wait_ge(k_sums, 1 + c + 1)
                    a.wait_ge(k_out, 1 + c * N_K)
                    for d in range(2):
                        a.copy(KS[:, :, d, :], PS[:, 4 + d, 0:P].rearrange("p (g x) -> p g x", g=CG)).then_inc(k_saved, 1)

            def dve_():
                L = lambda ins: dve.link(v, ins)
                tt = lambda o, x, y, op: L(v.tensor_tensor(o, x, y, op))
                ts = lambda o, x, s1, s2, op0, op1=ALU.bypass: L(v.tensor_scalar(o, x, s1, s2, op0, op1) if s2 is not None else v.tensor_scalar(o, x, s1, None, op0))
                stt = lambda o, x, s, y, op0, op1: L(v.scalar_tensor_tensor(o, x, s, y, op0, op1))
                v.wait_ge(x_ready.sem, xr)
                v.memset(ZERO, 0.0).then_inc(zero_done, 1)
                v.wait_ge(par_in, 112)
                v.wait_ge(lr_done, 1)
                v.tensor_tensor(E, LR, STEP, ALU.mult).then_inc(e_done, 1)
                tt(TH, LI, STEP, ALU.mult)
                ts(K, TH, 1.0 / TWO_PI, ROUND, ALU.mult, ALU.add)
                ts(K, K, -ROUND, None, ALU.add)
                stt(RED, K, -PI_A, TH, ALU.mult, ALU.add)
                stt(RED, K, -PI_B, RED, ALU.mult, ALU.add)
                stt(RED, K, -PI_C, RED, ALU.mult, ALU.add)
                ts(RED, RED, PI_F, -PI_F, ALU.min, ALU.max)
                ts(X1, RED, math.pi / 2, None, ALU.add)
                v.memset(SM[:, 502:503], 0.0).then_inc(th_done, 1)
                ts(X2, X1, PI_F, None, ALU.is_gt)
                stt(X1, X2, -TWO_PI, X1, ALU.mult, ALU.add)
                ts(X1, X1, PI_F, -PI_F, ALU.min, ALU.max)
                v.memset(SM[:, 502:503], 0.0).then_inc(th_done, 1)
                v.wait_ge(mag_done, 1)
                v.wait_ge(sin_done, 2)
                tt(A_R, MAG, CS_, ALU.mult)
                tt(A_I, MAG, SN, ALU.mult)
                tt(DEN, LR, LR, ALU.mult)
                tt(X1, LI, LI, ALU.mult)
                tt(DEN, DEN, X1, ALU.add)
                L(v.reciprocal(DEN, DEN))
                ts(K, A_R, -1.0, None, ALU.add)
                tt(X1, K, LR, ALU.mult)
                tt(X2, A_I, LI, ALU.mult)
                tt(X1, X1, X2, ALU.add)
                tt(CO_R, X1, DEN, ALU.mult)
                tt(X1, A_I, LR, ALU.mult)
                tt(X2, K, LI, ALU.mult)
                tt(X1, X1, X2, ALU.subtract)
                tt(CO_I, X1, DEN, ALU.mult)

                def over_c(x):
                    return x[:, 0, :].unsqueeze(2).to_broadcast([P, G_, GDIM])

                def cmul(o_r, o_i, xr_, xi_, yr, yi, t1, t2):
                    v.tensor_tensor(t1, xr_, yr, ALU.mult)
                    tt(t2, xi_, yi, ALU.mult)
                    tt(o_r, t1, t2, ALU.subtract)
                    v.tensor_tensor(t1, xr_, yi, ALU.mult)
                    tt(t2, xi_, yr, ALU.mult)
                    tt(o_i, t1, t2, ALU.add)

                cmul(BBR, BBI, over_c(CO_R), over_c(CO_I), BR, BI, T1, T2)
                L(v.memset(PR[:, 0], 1.0))
                L(v.memset(PI[:, 0], 0.0))
                L(v.tensor_copy(PR[:, 1], A_R[:, 0]))
                L(v.tensor_copy(PI[:, 1], A_I[:, 0]))
                for n in range(2, T8 + 1):
                    cmul(PR[:, n], PI[:, n], PR[:, n - 1], PI[:, n - 1], A_R[:, 0], A_I[:, 0], X1[:, 0], X2[:, 0])
                for src, i_, o_ in ((PR, INR, OUTR), (PI, INI, OUTI)):
                    v.tensor_copy(i_[0:64], src[0:64, T8 - 1::-1, :])
                    v.tensor_copy(o_[0:64], src[0:64, T8:0:-1, :])
                    v.tensor_copy(i_[64:P], src[64:P, 0:T8, :])
                    L(v.tensor_copy(o_[64:P], src[64:P, 1:T8 + 1, :]))
                for r in range(2):
                    L(v.tensor_copy(A8R[:, r, :], PR[:, T8]))
                L(v.tensor_copy(A8S[:, 1, :], PI[:, T8]))
                ts(A8S[:, 0, :], PI[:, T8], -1.0, None, ALU.mult)
                shape = [P, CG, T8, GDIM]

                def by_step(x, c):
                    return x[:, :, ds(c * CG, CG)].rearrange("p s g -> p g s").unsqueeze(3).to_broadcast(shape)

                def by_group(x, c):
                    return x[:, ds(c * CG, CG), :].unsqueeze(2).to_broadcast(shape)

                def tile(x):
                    return x.rearrange("p g (s c) -> p g s c", s=T8)

                t1, t2 = (x.rearrange("p (g s) c -> p g s c", g=CG) for x in (T1, T2))
                with v.Fori(0, NCH) as c:
                    dve.enter(c, 10)
                    v.wait_ge(k_sums, 1 + c)
                    v.wait_ge(mt_sums, 1 + c)
                    i_r, i_i, b_r, b_i = by_step(INR, c), by_step(INI, c), by_group(BBR, c), by_group(BBI, c)
                    cmul(tile(MIN[:, 0]), tile(MIN[:, 1]), i_r, i_i, b_r, b_i, t1, t2)
                    L(v.tensor_copy(CST[:, 0], CR[:, ds(c * CG, CG), :]))
                    v.tensor_scalar(CST[:, 1], CI[:, ds(c * CG, CG), :], -1.0, None, ALU.mult).then_inc(min_done, 1)
                    v.wait_ge(mout_out, 1 + c * 16)
                    o_r, o_i, c_r, c_i = by_step(OUTR, c), by_step(OUTI, c), by_group(CR, c), by_group(CI, c)
                    v.tensor_tensor(t1, o_r, c_r, ALU.mult)
                    tt(t2, o_i, c_i, ALU.mult)
                    tt(tile(MOUT[:, 0]), t1, t2, ALU.subtract)
                    v.tensor_scalar(t1, c_i, -1.0, None, ALU.mult)
                    tt(t2, o_i, c_r, ALU.mult)
                    tt(t1, t1, o_r, ALU.mult)
                    tt(tile(MOUT[:, 1]), t1, t2, ALU.subtract)
                    v.memset(SM[:, 502:503], 0.0).then_inc(mout_done, 1)
                    dve.leave(NCH)

            def pe_():
                pe.wait_ge(sums_taken.sem, st)
                with pe.Fori(0, NCH) as c:
                    pe.wait_ge(min_done, c + 1)
                    pe.wait_ge(mt_saved, 1 + c)
                    for i in range(CG):
                        for r in range(2):
                            b = i * 2 + r
                            mm = pe.transpose(PS[:, b // 4, (b % 4) * P:(b % 4 + 1) * P], MIN[:, r, i, :], IDENT)
                    mm.then_inc(mt_sums, 1)
                    pe.wait_ge(k_saved, 1 + c * 2)
                    for i in range(CG):
                        for d in range(2):
                            half = slice(d * STATE, (d + 1) * STATE)
                            for r in range(2):
                                mm = pe.matmul(PS[:, 4 + d, i * GDIM:(i + 1) * GDIM], MIN[half, r, i, :], CST[half, r, i, :],
                                               start=(r == 0), stop=(r == 1))
                    mm.then_inc(k_sums, 1)

            st = sums_taken.total
            return Stage(sync=sync, pe=pe_, act=act_, dve=dve_)

        def ssm(ht_at):
            V = view(6144, NBLK, 2, GROUPS)
            UTL = view(14336, GROUPS, LATB)
            SLM = view(16384, CG, 2, P)
            SLO = view(18432, 2, CG, P)
            DF, DB = view(20480, CG, P), view(21504, CG, P)
            UC = view(22528, T8, P)[0:NBLK]
            YC = view(23552, T8, P)[0:LATB]
            HST = view(24576, 2, CG, LATB)
            UTST = view(25088, CG, NBLK)
            UTLS = view(25600, CG, LATB)
            TA, TB_ = view(25856, 2, GROUPS), view(25984, 2, GROUPS)
            UCG = view(27136, CG, P)[0:NBLK]
            Y = view(6144, 2, D)
            DROW = view(8192, D)
            VAL = view(12288, 2, D)
            TMP = view(26112, 2, COLS)
            SG = view(26624, 2, COLS)
            u_out, slm_in, uc_in, uc_cut = sem("u_out"), sem("slm_in"), sem("uc_in"), sem("uc_cut")
            ut_sums, ut_saved, v_sums, v_saved = primed("ut_sums"), primed("ut_saved"), primed("v_sums"), primed("v_saved")
            scanned = sem("scanned")
            slo_in, d_in, d_sum, hst_done, y_in = (sem("ssm_" + n) for n in ("slo_in", "d_in", "d_sum", "hst", "y_in"))
            y_sums, y_saved, y_out = (primed("ssm_" + n) for n in ("y_sums", "y_saved", "y_out"))
            y_done, z_done, sg_done = sem("ssm_y"), sem("ssm_z"), sem("ssm_gate")
            xr = x_ready.total

            def to_h(blk, tb, sums):
                return a.copy(H[:, tb, ds(blk * COLS, COLS)], sums)

            in_sync, in_pe, in_take, in_end = linear(t["ssm_w_in"], 4, 4, lambda k, tb: HT[:, k, tb * P:(tb + 1) * P], to_h, ht_at=ht_at)
            turn_pe, turn_act, turn_end = turn(lambda tb: VAL[:, tb, :], range(2), KT, z_done, lambda i: i + 1,
                                               lambda q, i: HT[:, 4 * q:4 * q + 4, i * P:(i + 1) * P])
            NW = 8
            uw = take([NW // 4] * SLOTS)
            st = sums_taken.plan(NW * 2)
            N_D = 2 * T8 * 16

            def sync():
                in_sync()
                sp.wait_ge(sums_taken.sem, in_end)
                for tb, at in ((2, 0), (3, P), (0, 2 * P), (1, 3 * P)):
                    sp.dma_start(u_scr[at:at + P, :], H[:, tb, :]).then_inc(u_out, 16)
                sp.wait_ge(u_out, 64)
                u_steps = u_scr.rearrange("(k s) d -> k s d", s=T8)
                with sp.Fori(0, NCH) as c:
                    sp.wait_ge(v_sums, 1 + c)
                    sp.dma_start(SLM.rearrange("p g r x -> p (g r x)"), wblock(min_scr, c)).then_inc(slm_in, 16)
                    sp.dma_start(UC, u_steps[:, :, ds(c * P, P)]).then_inc(uc_in, 16)
                with sp.Fori(0, NCH) as c:
                    sp.wait_ge(y_sums, 1 + c)
                    sp.dma_start(SLO.rearrange("p r g x -> p (r g x)"), wblock(mout_scr, c)).then_inc(slo_in, 16)
                    for d, dst in enumerate((DF, DB)):
                        for s in range(T8):
                            sp.dma_start(dst[s * GDIM:(s + 1) * GDIM],
                                         lag_scr[d, ds(c * CG, CG), :, s * GDIM:s * GDIM + P].rearrange("g c x -> c g x")).then_inc(d_in, 16)
                    sp.wait_ge(y_saved, 1 + c + 1)
                    sp.dma_start(y_scr.rearrange("(k s) d -> k s d", s=T8)[:, :, ds(c * P, P)], YC).then_inc(y_out, 16)
                sp.wait_ge(y_out, 1 + 16 * NCH)
                sp.dma_start(Y, y_scr.rearrange("(t p) d -> p t d", p=P)).then_inc(y_in, 16)
                sp.dma_start(DROW, row(t["ssm_d"])).then_inc(y_in, 16)
                with sp.Fori(0, NW // 4) as r:
                    for s in range(SLOTS):
                        load(s, r + uw[s], wblock(t["ssm_w_out"], r * 4 + s))

            def pe_():
                in_pe()
                with pe.Fori(0, NCH) as c:
                    pe.wait_ge(uc_cut, c + 1)
                    pe.wait_ge(ut_saved, 1 + c * 2)
                    apart(pe)
                    for i in range(CG):
                        mm = pe.transpose(PS[:, 4, i * NBLK:(i + 1) * NBLK], UCG[:, i, :], IDENT[0:NBLK, 0:NBLK])
                    mm.then_inc(ut_sums, 1)
                    pe.wait_ge(slm_in, c * 16 + 16)
                    pe.wait_ge(ut_saved, 1 + c * 2 + 1)
                    pe.wait_ge(v_saved, 1 + c * 3)
                    for i in range(CG):
                        for r in range(2):
                            mm = pe.matmul(PS[:, 5 + i // 4, ((i % 4) * 2 + r) * NBLK:((i % 4) * 2 + r + 1) * NBLK],
                                           SLM[:, i, r, :], UTST[:, i, :], start=True, stop=True)
                    mm.then_inc(v_sums, 1)
                with pe.Fori(0, NCH) as c:
                    pe.wait_ge(slo_in, c * 16 + 16)
                    pe.wait_ge(d_sum, c + 1)
                    pe.wait_ge(hst_done, c * 3 + 3)
                    pe.wait_ge(y_saved, 1 + c)
                    for i in range(CG):
                        out = PS[0:LATB, i // 4, (i % 4) * P:(i % 4 + 1) * P]
                        pe.matmul(out, UTLS[:, i, :], DF[:, i, :], start=True, stop=False)
                        pe.matmul(out, HST[:, 0, i, :], SLO[:, 0, i, :], start=False, stop=False)
                        mm = pe.matmul(out, HST[:, 1, i, :], SLO[:, 1, i, :], start=False, stop=True)
                    mm.then_inc(y_sums, 1)
                turn_pe()
                pe.wait_ge(n_ht.sem, turn_end)
                pe.wait_ge(y_saved, 1 + NCH)
                with pe.Fori(0, NW // 4) as r:
                    for s in range(4):
                        pe.wait_ge(w_full[s], (r + uw[s] + 1) * 16)
                        pe.wait_ge(sums_taken.sem, r * 8 + (st + (s // 2 - 1) * 4))
                        for tb in range(2):
                            for k in range(KT):
                                mm = pe.matmul(PS[:, s, tb * COLS:(tb + 1) * COLS], HT[:, k, tb * P:(tb + 1) * P],
                                               W[:, s, k * COLS:(k + 1) * COLS], start=(k == 0), stop=(k == KT - 1))
                        mm.then_inc(w_used[s], 1)

            def act_():
                in_take(a)
                with a.Fori(0, NCH) as c:
                    a.wait_ge(uc_in, c * 16 + 16)
                    a.wait_ge(ut_sums, 1 + c)
                    a.copy(UCG.rearrange("k g (s c) -> k g s c", s=T8), UC.rearrange("k s (g c) -> k g s c", g=CG)).then_inc(uc_cut, 1)
                    a.wait_ge(ut_sums, 1 + c + 1)
                    a.wait_ge(v_sums, 1 + c)
                    turned = PS[:, 4, :].rearrange("p (g k) -> p g k", g=CG)
                    a.copy(UTST, turned).then_inc(ut_saved, 1)
                    a.copy(UTL[:, ds(c * CG, CG), :], turned[:, :, NBLK - LATB:NBLK]).then_inc(ut_saved, 1)
                    a.wait_ge(v_sums, 1 + c + 1)
                    parts = PS[:, 5:7, :].rearrange("p b (g r k) -> p (b g) r k", g=4, r=2)
                    for rows_, lo, hi, back in ((slice(0, 64), 0, NBLK, 0), (slice(64, P), 0, NBLK - LATB, 1), (slice(64, P), NBLK - LATB, NBLK, 1)):
                        for r in range(2):
                            dst = V[rows_, lo:hi, r, ds(c * CG, CG)].rearrange("p k g -> p g k")
                            src = parts[rows_, :, r, lo:hi]
                            if back:
                                src = src[:, :, ::-1]
                            ins = a.copy(dst, src)
                        ins.then_inc(v_saved, 1)
                with a.Fori(0, NCH) as c:
                    a.wait_ge(scanned, 1)
                    a.wait_ge(y_sums, 1 + c)
                    a.copy(UTLS, UTL[:, ds(c * CG, CG), :]).then_inc(hst_done, 1)
                    first = NBLK - LATB - 1
                    fwd = V[0:64, first:NBLK - 1, :, ds(c * CG, CG)].rearrange("p k r g -> p r g k")
                    bwd = V[64:P, first:NBLK - 1, :, ds(c * CG, CG)].rearrange("p k r g -> p r g k")
                    a.copy(HST[0:64], fwd).then_inc(hst_done, 1)
                    a.copy(HST[64:P][:, :, :, ::-1], bwd).then_inc(hst_done, 1)
                    a.wait_ge(y_sums, 1 + c + 1)
                    a.wait_ge(y_out, 1 + c * 16)
                    a.copy(YC.rearrange("k t (g x) -> k g t x", g=CG)[:, :, ::-1, :],
                           PS[0:LATB, 0:2, :].rearrange("k b (g t x) -> k (b g) t x", g=4, t=T8)).then_inc(y_saved, 1)
                for tb in range(2):
                    a.wait_ge(y_done, tb + 1)
                    a.activation(VAL[:, tb, :], Y[:, tb, :], ACT.Gelu_apprx_tanh).then_inc(z_done, 1)
                turn_act()
                with a.Fori(0, NW // 4) as r:
                    for s in (1, 3):
                        a.wait_ge(w_used[s], r + uw[s] + 2)
                        a.wait_ge(sums_taken.sem, r * 8 + (st + (s // 2) * 4))
                        a.activation(SG, PS[:, s, :].rearrange("p (t c) -> p t c", t=2), ACT.Sigmoid).then_inc(sg_done, 1)

            def dve_():
                v.wait_ge(v_saved, 1 + 3 * NCH)
                with v.Fori(1, NBLK - 1) as j:
                    dve.enter(j - 1, 3)
                    last, cur = (V[:, ds(j - o, 1)].rearrange("p a r g -> p (a r) g") for o in (1, 0))
                    v.tensor_tensor(TA, A8R, last, ALU.mult)
                    dve.link(v, v.tensor_tensor(TB_[:, ::-1, :], A8S[:, ::-1, :], last, ALU.mult))
                    dve.link(v, v.tensor_tensor(TA, TA, TB_, ALU.add))
                    dve.link(v, v.tensor_tensor(cur, cur, TA, ALU.add))
                    dve.leave(NBLK - 2)
                v.memset(SM[:, 501:502], 0.0).then_inc(scanned, 1)
                with v.Fori(0, NCH) as c:
                    v.wait_ge(d_in, c * N_D + N_D)
                    v.tensor_tensor(DF, DF, DB, ALU.add).then_inc(d_sum, 1)
                v.wait_ge(y_in, 32)
                for tb in range(2):
                    dve.link(v, v.tensor_tensor(H[:, tb, :], H[:, tb, :], DROW, ALU.mult))
                    v.tensor_tensor(Y[:, tb, :], Y[:, tb, :], H[:, tb, :], ALU.add).then_inc(y_done, 1)
                with v.Fori(0, NW // 4) as r:
                    dve.enter(r, 8)
                    for s in (1, 3):
                        v.wait_ge(sg_done, r * 2 + (s // 2 + 1))
                        v.wait_ge(w_used[s - 1], r + uw[s - 1] + 2)
                        for tb in range(2):
                            col = r * (2 * COLS) + (s // 2) * COLS
                            dst = XA[:, tb, ds(col, COLS)]
                            x = TMP[:, tb, :]
                            dve.link(v, v.tensor_tensor(x, PS[:, s - 1, tb * COLS:(tb + 1) * COLS], SG[:, tb, :], ALU.mult))
                            dve.link(v, v.tensor_tensor(x, x, AR[:, ds(col + 2 * D, COLS)], ALU.mult))
                            v.tensor_tensor(dst, dst, x, ALU.add).then_inc(sums_taken.sem, 2)
                    dve.leave(NW // 4)
                mark()

            mark = mark_x()
            return Stage(sync=sync, pe=pe_, act=act_, dve=dve_)

        PIECES = ((0, P), (P, 3 * P))
        SCORES = 3 * P

        def fox(ht_at):
            O = view(0, 2, D)
            VT = view(2048, 2, D)
            QP, KP = view(4096, 2, SEQ), view(4608, 2, SEQ)
            LT = view(5120, 2, SCORES)
            SB = view(5888, 2, SCORES)
            PB = view(6656, 2, SCORES)
            PTB = view(7424, 2, SCORES)
            FW = view(8192, KT, FOX_H)
            BF = view(8320, FOX_H)
            ZF, AF, LF = view(8336, 2, FOX_H), view(8368, 2, FOX_H), view(8400, 2, FOX_H)
            NM, SUMS, RS = view(8432, 4), view(8436, 4), view(8440, 4)
            TMPM = view(8444, 4)
            SUF = view(8448, 2, SEQ)
            PAIRS = FOX_H // 2
            ROUNDS = PAIRS // 2
            par_in, f_sums, f_z, f_exp, f_one, f_log = (sem("fox_" + n) for n in ("par_in", "f_sums", "f_abs", "f_exp", "f_one", "f_log"))
            lt_ready, s_sums, neg_ready, pv_sums = (sem("fox_" + n) for n in ("gates", "s_sums", "negmax", "pv_sums"))
            s_taken, exp_done, pt_sums, pt_saved, o_taken = (primed("fox_" + n) for n in ("s_taken", "exp", "turned", "pt_saved", "o_taken"))
            qk_saved, v_saved = sem("fox_qk_saved"), sem("fox_v_saved")
            uw = take([ROUNDS, ROUNDS, ROUNDS, 0])
            turn_pe, turn_act, turn_end = turn(lambda tb: O[:, tb, :], range(2), KT, o_taken, lambda i: 1 + 4 * PAIRS,
                                               lambda q, i: HT[:, 4 * q:4 * q + 4, i * P:(i + 1) * P])
            out_sync, out_pe, out_take, out_end = linear(t["fox_out"], 4, 2, lambda k, tb: HT[:, k, tb * P:(tb + 1) * P],
                                                         add_gated(None, 2, None), ht_at=turn_end)
            mark = mark_x()
            st = sums_taken.total - 8

            def sync():
                sp.wait_ge(n_ht.sem, ht_at)
                sp.sem_inc(qk_saved, 4)
                sp.dma_start(FW, t["fox_f"]).then_inc(par_in, 16)
                sp.dma_start(BF, row(t["fox_b"])).then_inc(par_in, 16)
                sp.dma_start(SUF.rearrange("p b k -> p (b k)"), t["consts"][:, C_SUF:C_SUF + 2 * SEQ]).then_inc(par_in, 16)
                with sp.Fori(0, ROUNDS) as r:
                    load(0, r + uw[0], wblock(t["fox_qk"], r * 2))
                    load(2, r + uw[2], wblock(t["fox_v"], r))
                    load(1, r + uw[1], wblock(t["fox_qk"], r * 2 + 1))
                out_sync()

            def pe_():
                def project(r, s):
                    j = r * 2 + s
                    pe.wait_ge(w_full[s], (r + uw[s] + 1) * 16)
                    pe.wait_ge(qk_saved, j * 2 + 2)
                    for part in range(2):
                        for k in range(KT):
                            mm = pe.matmul(PS[:, s, part * SEQ:(part + 1) * SEQ], W[:, s, k * COLS + part * P:k * COLS + (part + 1) * P],
                                           HT[:, k, 0:SEQ], start=(k == 0), stop=(k == KT - 1))
                    mm.then_inc(w_used[s], 1)
                    if s == 0:
                        pe.wait_ge(w_full[2], (r + uw[2] + 1) * 16)
                        pe.wait_ge(v_saved, r)
                        for tb in range(2):
                            for k in range(KT):
                                mm = pe.matmul(PS[:, 2, tb * COLS:(tb + 1) * COLS], HT[:, k, tb * P:(tb + 1) * P],
                                               W[:, 2, k * COLS:(k + 1) * COLS], start=(k == 0), stop=(k == KT - 1))
                        mm.then_inc(w_used[2], 1)

                def scores(r, s):
                    j = r * 2 + s
                    pe.wait_ge(qk_saved, j * 2 + 6)
                    pe.wait_ge(lt_ready, j * 2 + 2)
                    pe.wait_ge(s_taken, 1 + j * 2)
                    for i in range(2):
                        h = slice(i * FOX_D, (i + 1) * FOX_D)
                        first, second = PS[:, 3 + i, 0:P], PS[:, 3 + i, P:SCORES]
                        pe.matmul(first, QP[h, s, 0:P], KP[h, s, 0:P], start=True, stop=False)
                        pe.matmul(first, LT[:, i, 0:P], SUF[:, 0, 0:P], start=False, stop=True)
                        pe.matmul(second, QP[h, s, P:SEQ], KP[h, s, :], start=True, stop=False)
                        pe.matmul(second, LT[:, i, P:SEQ], SUF[:, 0, :], start=False, stop=False)
                        mm = pe.matmul(second, LT[:, i, SEQ:SCORES], SUF[:, 1, :], start=False, stop=True)
                    mm.then_inc(s_sums, 1)

                def values(r, s):
                    j = r * 2 + s
                    for i in range(2):
                        pe.wait_ge(exp_done, 1 + j * 4 + (2 * i + 2))
                        pe.wait_ge(pt_saved, 1 + j * 2)
                        for k in range(3):
                            mm = pe.transpose(PS[:, 5 + i, k * P:(k + 1) * P], PB[:, i, k * P:(k + 1) * P], IDENT)
                        mm.then_inc(pt_sums, 1)
                    pe.wait_ge(v_saved, r + 1)
                    pe.wait_ge(o_taken, 1 + j * 4)
                    for i in range(2):
                        pe.wait_ge(pt_saved, 1 + j * 2 + (i + 1))
                        vh = [VT[:, kb, ds(r * COLS + (s * 2 + i) * FOX_D, FOX_D)] for kb in range(2)]
                        outs = [PS[:, 7, (2 * i + q) * FOX_D:(2 * i + q + 1) * FOX_D] for q in range(2)]
                        pe.matmul(outs[0], PTB[:, i, 0:P], vh[0], start=True, stop=True)
                        pe.matmul(outs[1], PTB[:, i, P:SEQ], vh[0], start=True, stop=False)
                        pe.matmul(outs[1], PTB[:, i, SEQ:SCORES], vh[1], start=False, stop=True).then_inc(pv_sums, 1)

                def pe_round(r, more):
                    for s in range(2):
                        scores(r, s)
                        if s == 0:
                            project(r, 1)
                        elif more:
                            project(r + 1, 0)
                        values(r, s)

                pe.wait_ge(n_ht.sem, ht_at)
                pe.wait_ge(par_in, 48)
                pe.wait_ge(sums_taken.sem, st)
                for tb in range(2):
                    for k in range(KT):
                        mm = pe.matmul(PS[:, 7, tb * FOX_H:(tb + 1) * FOX_H], HT[:, k, tb * P:(tb + 1) * P], FW[:, k, :],
                                       start=(k == 0), stop=(k == KT - 1))
                mm.then_inc(f_sums, 1)
                project(0, 0)
                with pe.Fori(0, ROUNDS - 1) as r:
                    pe_round(r, True)
                pe_round(ROUNDS - 1, False)
                turn_pe()
                out_pe()

            def act_():
                def save(r, s):
                    a.wait_ge(w_used[s], r + uw[s] + 2)
                    a.activation(QP[:, s, :], PS[:, s, 0:SEQ], ACT.Copy, scale=FOX_D ** -0.5).then_inc(qk_saved, 1)
                    a.copy(KP[:, s, :], PS[:, s, SEQ:2 * SEQ]).then_inc(qk_saved, 1)
                    if s == 0:
                        a.wait_ge(w_used[2], r + uw[2] + 2)
                        a.copy(VT[:, :, ds(r * COLS, COLS)], PS[:, 2, :].rearrange("p (t c) -> p t c", t=2)).then_inc(v_saved, 1)

                def soft(r, s):
                    j = r * 2 + s
                    a.wait_ge(neg_ready, j + 1)
                    a.wait_ge(pt_sums, 1 + j * 2)
                    for i in range(2):
                        for q, (lo, hi) in enumerate(PIECES):
                            c = 2 * i + q
                            a.activation(PB[:, i, lo:hi], SB[:, i, lo:hi], ACT.Exp, bias=NM[:, c:c + 1],
                                         accum_out=SUMS[:, c:c + 1]).then_inc(exp_done, 1)

                def save_turned(r, s):
                    j = r * 2 + s
                    for i in range(2):
                        a.wait_ge(pt_sums, 1 + j * 2 + (i + 1))
                        a.copy(PTB[:, i, :], PS[:, 5 + i, 0:SCORES]).then_inc(pt_saved, 1)

                def act_round(r, more):
                    for s in range(2):
                        soft(r, s)
                        if s == 0:
                            save(r, 1)
                        elif more:
                            save(r + 1, 0)
                        save_turned(r, s)

                a.wait_ge(f_z, 1)
                a.activation(AF, AF, ACT.Exp, scale=-1.0).then_inc(f_exp, 1)
                a.wait_ge(f_one, 1)
                a.activation(AF, AF, ACT.Ln).then_inc(f_log, 1)
                save(0, 0)
                with a.Fori(0, ROUNDS - 1) as r:
                    act_round(r, True)
                act_round(ROUNDS - 1, False)
                turn_act()

            def dve_():
                def gates(j):
                    v.wait_ge(s_sums, j)
                    for i in range(2):
                        for lo, hi, tb in ((0, SEQ, 0), (SEQ, SCORES, 1)):
                            one = v.tensor_tensor(LT[:, i, lo:hi], TRI[:, lo:hi], LF[:, tb, ds(j * 2 + i, 1)].to_broadcast([P, hi - lo]), ALU.mult)
                        one.then_inc(lt_ready, 1)

                def pair(j, more):
                    v.wait_ge(s_sums, j + 1)
                    v.wait_ge(exp_done, 1 + j * 4)
                    for i in range(2):
                        last = v.tensor_tensor(SB[:, i, :], PS[:, 3 + i, 0:SCORES], FOX_MASK, ALU.add)
                        last.then_inc(s_taken, 1)
                    v.wait_ge(s_taken, 1 + j * 2 + 2)
                    for i in range(2):
                        for q, (lo, hi) in enumerate(PIECES):
                            last = v.tensor_reduce(TMPM[:, 2 * i + q:2 * i + q + 1], SB[:, i, lo:hi], AX_X, ALU.max)
                    dve.link(v, last)
                    v.tensor_scalar(NM, TMPM, -1.0, None, ALU.mult).then_inc(neg_ready, 1)
                    if more:
                        gates(j + 1)
                    v.wait_ge(exp_done, 1 + j * 4 + 4)
                    dve.link(v, v.reciprocal(RS, SUMS))
                    v.wait_ge(pv_sums, j * 2 + 2)
                    for i in range(2):
                        for q in range(2):
                            c = 2 * i + q
                            v.tensor_scalar(O[:, q, ds(j * P + i * FOX_D, FOX_D)], PS[:, 7, c * FOX_D:(c + 1) * FOX_D],
                                            RS[:, c:c + 1], None, ALU.mult).then_inc(o_taken, 1)

                v.wait_ge(par_in, 48)
                v.wait_ge(f_sums, 1)
                sums = PS[:, 7, 0:2 * FOX_H].rearrange("p (t h) -> p t h", t=2)
                dve.link(v, v.tensor_tensor(ZF, sums, BF.unsqueeze(1).to_broadcast([P, 2, FOX_H]), ALU.add))
                v.scalar_tensor_tensor(AF, ZF, -1.0, ZF, ALU.mult, ALU.max).then_inc(f_z, 1)
                v.wait_ge(f_exp, 1)
                v.tensor_scalar(AF, AF, 1.0, None, ALU.add).then_inc(f_one, 1)
                v.wait_ge(f_log, 1)
                dve.link(v, v.scalar_tensor_tensor(LF, ZF, 0.0, AF, ALU.min, ALU.subtract))
                gates(0)
                with v.Fori(0, PAIRS - 1) as j:
                    dve.enter(j, 2)
                    pair(j, True)
                    dve.leave(PAIRS - 1)
                pair(PAIRS - 1, False)
                out_take(v)
                mark()

            return Stage(sync=sync, pe=pe_, act=act_, dve=dve_)

        def ffn(layer, ht_at):
            U = view(0, 4, SEQ + 2)
            CT = view(1040, 4, SEQ)
            SIL = view(2064, 2, SEQ)
            GV = view(2576, 2, SEQ)
            CW = view(3088, FFC, 16)
            CWC = view(3088 + 16 * FFC, 4, 4)
            uw = take([FFC, FFC, FFC, 0])
            nm = f"ffn{layer}_"
            cw_in, pad_done, cw_ready, silu_done = (sem(nm + n) for n in ("taps_in", "pad", "taps_cut", "silu"))
            u_saved, conv_done, gv_ready = (primed(nm + n) for n in ("u_saved", "conv", "gated"))
            st = sums_taken.plan(4)
            xr = x_ready.total

            def sync():
                sp.wait_ge(x_ready.sem, xr)
                sp.dma_start(CW, t["ffn_conv"][layer]).then_inc(cw_in, 16)
                with sp.Fori(0, FFC) as c:
                    load(0, c + uw[0], wblock(t[f"ffn_gate{layer}"], c))
                    load(1, c + uw[1], wblock(t[f"ffn_val{layer}"], c))
                    load(2, c + uw[2], wblock(t[f"ffn_out{layer}"], c))

            def pe_():
                def project(c):
                    for s in range(2):
                        pe.wait_ge(w_full[s], (c + uw[s] + 1) * 16)
                        pe.wait_ge(u_saved, 1 + c * 8)
                        for m in range(2):
                            for k in range(KT):
                                mm = pe.matmul(PS[:, 4 + s, m * SEQ:(m + 1) * SEQ], W[:, s, k * COLS + m * P:k * COLS + (m + 1) * P],
                                               HT[:, k, 0:SEQ], start=(k == 0), stop=(k == KT - 1))
                        mm.then_inc(w_used[s], 1)

                def output(c, start, stop):
                    pe.wait_ge(w_full[2], (c + uw[2] + 1) * 16)
                    pe.wait_ge(gv_ready, 1 + c + 1)
                    for tb in range(2):
                        for half in range(2):
                            for k in range(2):
                                mm = pe.matmul(PS[:, tb * 2 + half, :], GV[:, k, tb * P:(tb + 1) * P],
                                               W[:, 2, k * D + half * 512:k * D + (half + 1) * 512],
                                               start=(start and k == 0), stop=(stop and k == 1))
                    mm.then_inc(w_used[2], 1)

                pe.wait_ge(n_ht.sem, ht_at)
                pe.wait_ge(sums_taken.sem, st)
                project(0)
                project(1)
                output(0, True, False)
                with pe.Fori(1, FFC - 1) as c:
                    project(c + 1)
                    output(c, False, False)
                output(FFC - 1, False, True)

            def act_():
                a.wait_ge(pad_done, 1)
                with a.Fori(0, FFC) as c:
                    a.wait_ge(cw_ready, c + 1)
                    a.wait_ge(conv_done, 1 + c)
                    for s in range(2):
                        a.wait_ge(w_used[s], c + uw[s] + 2)
                        for m in range(2):
                            i = s * 2 + m
                            src = PS[:, 4 + s, m * SEQ:(m + 1) * SEQ]
                            a.copy(U[:, i, 2:SEQ + 2], src).then_inc(u_saved, 1)
                            a.activation(CT[:, i, :], src, ACT.Identity, scale=CWC[:, i, 2:3], bias=CWC[:, i, 3:4]).then_inc(u_saved, 1)
                    a.wait_ge(conv_done, 1 + c + 1)
                    a.wait_ge(gv_ready, 1 + c)
                    a.activation(SIL, CT[:, 0:2, :], ACT.Silu).then_inc(silu_done, 1)

            def dve_():
                v.wait_ge(x_ready.sem, xr)
                v.memset(U[:, :, 0:2], 0.0).then_inc(pad_done, 1)
                v.wait_ge(pad_done, 1)
                v.wait_ge(cw_in, 16)
                with v.Fori(0, FFC) as c:
                    dve.enter(c, 1)
                    v.wait_ge(u_saved, 1 + c * 8)
                    v.wait_ge(conv_done, 1 + c)
                    v.tensor_copy(CWC.rearrange("p i j -> p (i j)"), CW[:, ds(c, 1), :].rearrange("p a j -> p (a j)")).then_inc(cw_ready, 1)
                    v.wait_ge(u_saved, 1 + c * 8 + 8)
                    for i in range(4):
                        last = v.scalar_tensor_tensor(CT[:, i, :], U[:, i, 1:SEQ + 1], CWC[:, i, 1:2], CT[:, i, :], ALU.mult, ALU.add)
                    dve.link(v, last)
                    for i in range(4):
                        last = v.scalar_tensor_tensor(CT[:, i, :], U[:, i, 0:SEQ], CWC[:, i, 0:1], CT[:, i, :], ALU.mult, ALU.add)
                    last.then_inc(conv_done, 1)
                    v.wait_ge(silu_done, c + 1)
                    v.wait_ge(w_used[2], c + (uw[2] + 1))
                    v.tensor_tensor(GV, SIL, CT[:, 2:4, :], ALU.mult).then_inc(gv_ready, 1)
                    dve.leave(FFC)
                v.wait_ge(w_used[2], uw[2] + FFC + 1)
                for tb in range(2):
                    for half in range(2):
                        dst = XA[:, tb, half * 512:(half + 1) * 512]
                        v.tensor_tensor(dst, dst, PS[:, tb * 2 + half, :], ALU.add).then_inc(sums_taken.sem, 1)
                mark()

            mark = mark_x()
            return Stage(sync=sync, pe=pe_, act=act_, dve=dve_)

        KR = view(28160, 2, SEQ)
        QD = lambda tb: H[:, tb, 0:QL]
        CKV = lambda tb: H[:, 2 + tb, 0:KVL]

        def rope(dst, src, t1, t2, done):
            x1, x2 = src[:, 0, :], src[:, 1, :]
            v.tensor_tensor(t1[:, 0, :], x1, COS, ALU.mult)
            v.tensor_tensor(t2[:, 0, :], x2, SIN, ALU.mult)
            v.tensor_tensor(t1[:, 1, :], x1, SIN, ALU.mult)
            dve.link(v, v.tensor_tensor(t2[:, 1, :], x2, COS, ALU.mult))
            v.tensor_tensor(dst[:, 0, :], t1[:, 0, :], t2[:, 0, :], ALU.subtract)
            return v.tensor_tensor(dst[:, 1, :], t1[:, 1, :], t2[:, 1, :], ALU.add).then_inc(done, 1)

        def mla_down(ht_at):
            RAW, T1, T2 = view(0, 2, SEQ), view(512, 2, SEQ), view(1024, 2, SEQ)
            n_blk = QL // COLS + 2
            uw = take([2, 1, 1, 1])
            saved, roped = sem("mla_down_saved"), sem("mla_key_roped")
            st = sums_taken.total
            x_ready.plan(1)

            def sync():
                for b in range(n_blk):
                    load(b % SLOTS, uw[b % SLOTS] + b // SLOTS, t["mla_down"][b])

            def pe_():
                pe.wait_ge(n_ht.sem, ht_at)
                pe.wait_ge(sums_taken.sem, st)
                for b in range(n_blk):
                    s = b % SLOTS
                    pe.wait_ge(w_full[s], (uw[s] + b // SLOTS + 1) * 16)
                    for half in range(2):
                        for k in range(KT):
                            if b < n_blk - 1:
                                at = half * P + (SEQ if b == n_blk - 2 else 0)
                                ops = HT[:, k, at:at + P], W[:, s, k * COLS:(k + 1) * COLS]
                            else:
                                ops = W[:, s, k * COLS + half * P:k * COLS + (half + 1) * P], HT[:, k, SEQ:2 * SEQ]
                            mm = pe.matmul(PS[:, b, half * COLS:(half + 1) * COLS], *ops, start=(k == 0), stop=(k == KT - 1))
                    mm.then_inc(w_used[s], 1)

            def act_():
                for b in range(n_blk):
                    s = b % SLOTS
                    a.wait_ge(w_used[s], uw[s] + b // SLOTS + 2)
                    sums = PS[:, b, :].rearrange("p (t c) -> p t c", t=2)
                    dst = H[:, 0:2, b * COLS:(b + 1) * COLS] if b < n_blk - 2 else H[:, 2:4, 0:KVL] if b == n_blk - 2 else RAW
                    a.copy(dst, sums).then_inc(saved, 1)

            def dve_():
                v.wait_ge(saved, n_blk)
                rope(KR, RAW, T1, T2, roped)
                v.memset(SM[:, 500:501], 0.0).then_inc(x_ready.sem, 1)

            return Stage(sync=sync, pe=pe_, act=act_, dve=dve_)

        def mla(ht_at):
            G4 = 4
            ROUNDS = MLA_H // G4
            HV = MLA_H * VD
            O = view(0, 2, HV)
            VT = view(4096, 2, HV)
            QN, KN = view(8192, G4, SEQ), view(9216, G4, SEQ)
            RAW, T1, T2, QR = view(10240, 2, SEQ), view(10752, 2, SEQ), view(11264, 2, SEQ), view(11776, 2, SEQ)
            SB, PB, PTB = view(12288, G4, SCORES), view(13824, G4, SCORES), view(15360, G4, SCORES)
            NM, SUMS, RS, TMPM = (view(16896 + 8 * i, 8) for i in range(4))
            QK, LK = QL // P, KVL // P
            OT = HT[:, :, :].rearrange("p k (a t) -> p (k a) t", a=2)
            UNITS = 7
            scale = (NOPE + ROPE) ** -0.5
            p_sums, p_taken, roped = sem("mla_p_sums"), sem("mla_p_taken"), sem("mla_q_roped")
            s_sums, s_taken, neg_ready, pt_saved, pv_sums = (sem("mla_" + n) for n in ("s_sums", "s_taken", "negmax", "pt_saved", "pv_sums"))
            exp_done, pt_sums, o_taken = (primed("mla_" + n) for n in ("exp", "turned", "o_taken"))
            uw = take([ROUNDS] * SLOTS)
            turn_pe, turn_act, turn_end = turn(lambda tb: O[:, tb, :], range(2), HV // P, o_taken, lambda i: 1 + 2 * MLA_H,
                                               lambda q, i: OT[:, 4 * q:4 * q + 4, i * P:(i + 1) * P])
            out_sync, out_pe, out_take, out_end = linear(t["mla_out"], 8, 2, lambda k, tb: OT[:, k, tb * P:(tb + 1) * P],
                                                         add_gated(None, 2, None, cols=P), ht_at=turn_end, kt=HV // P)
            mark = mark_x()
            n_h_at = n_h.total

            def sync():
                with sp.Fori(0, ROUNDS) as r:
                    for s in range(3):
                        load(s, r + uw[s], wblock(t["mla_uq"], r * 3 + s), cols=QK * COLS)
                    load(3, r + uw[3], wblock(t["mla_ukv"], r))
                out_sync()

            def pe_():
                def project(r):
                    for u in range(UNITS):
                        s = min(u, 3)
                        if u <= 3:
                            pe.wait_ge(w_full[s], (r + uw[s] + 1) * 16)
                        pe.wait_ge(p_taken, r * UNITS + max(0, u - 3))
                        bank = PS[:, 4 + u % 4, :]
                        if u < 3:
                            for m in range(2):
                                for k in range(QK):
                                    mm = pe.matmul(bank[:, m * SEQ:(m + 1) * SEQ], W[:, s, k * COLS + m * P:k * COLS + (m + 1) * P],
                                                   HT[:, k, 0:SEQ], start=(k == 0), stop=(k == QK - 1))
                            mm.then_inc(w_used[s], 1)
                        elif u < 5:
                            for m in range(2):
                                col = ((u - 3) * 2 + m) * P
                                for k in range(LK):
                                    mm = pe.matmul(bank[:, m * SEQ:(m + 1) * SEQ], W[:, s, k * 512 + col:k * 512 + col + P],
                                                   HT[:, k, SEQ:2 * SEQ], start=(k == 0), stop=(k == LK - 1))
                            mm.then_inc(p_sums, 1)
                        else:
                            tb = u - 5
                            for k in range(LK):
                                mm = pe.matmul(bank, HT[:, k, SEQ + tb * P:SEQ + (tb + 1) * P], W[:, s, 1024 + k * 512:1024 + (k + 1) * 512],
                                               start=(k == 0), stop=(k == LK - 1))
                            mm.then_inc(p_sums if tb == 0 else w_used[s], 1)

                def scores(r):
                    pe.wait_ge(p_taken, r * UNITS + 5)
                    pe.wait_ge(roped, r + 1)
                    for i in range(G4):
                        pe.wait_ge(o_taken, 1 + r * (2 * G4))
                        b = slice(i * 32, (i + 1) * 32)
                        for (lo, hi), q in zip(PIECES, (slice(0, P), slice(P, SEQ))):
                            keys = slice(0, hi - lo)
                            out = PS[:, i, lo:hi]
                            pe.matmul(out, QN[:, i, q], KN[:, i, keys], start=True, stop=False)
                            for x in range(2):
                                mm = pe.matmul(out, QR[b, x, q], KR[b, x, keys], start=False, stop=(x == 1))
                        mm.then_inc(s_sums, 1)

                def values(r):
                    for i in range(G4):
                        pe.wait_ge(exp_done, 1 + r * (2 * G4) + (2 * i + 2))
                        for k in range(3):
                            mm = pe.transpose(PS[:, i, k * P:(k + 1) * P], PB[:, i, k * P:(k + 1) * P], IDENT)
                        mm.then_inc(pt_sums, 1)
                    pe.wait_ge(p_taken, r * UNITS + UNITS)
                    for i in range(G4):
                        pe.wait_ge(pt_saved, r * G4 + (i + 1))
                        vh = [VT[:, kb, ds(r * (G4 * VD) + i * VD, VD)] for kb in range(2)]
                        pe.matmul(PS[:, i, 0:VD], PTB[:, i, 0:P], vh[0], start=True, stop=True)
                        pe.matmul(PS[:, i, VD:2 * VD], PTB[:, i, P:SEQ], vh[0], start=True, stop=False)
                        pe.matmul(PS[:, i, VD:2 * VD], PTB[:, i, SEQ:SCORES], vh[1], start=False, stop=True).then_inc(pv_sums, 1)

                pe.wait_ge(n_ht.sem, ht_at)
                project(0)
                with pe.Fori(0, ROUNDS - 1) as r:
                    scores(r)
                    project(r + 1)
                    values(r)
                scores(ROUNDS - 1)
                values(ROUNDS - 1)
                turn_pe()
                out_pe()

            def act_():
                def save(r):
                    for u in range(UNITS):
                        if u < 3:
                            a.wait_ge(w_used[u], r + (uw[u] + 2))
                        elif u < 6:
                            a.wait_ge(p_sums, r * 3 + (u - 2))
                        else:
                            a.wait_ge(w_used[3], r + (uw[3] + 2))
                        sums = PS[:, 4 + u % 4, :]
                        two = sums.rearrange("p (m t) -> p m t", m=2)
                        if u < 2:
                            one = a.activation(QN[:, 2 * u:2 * u + 2, :], two, ACT.Copy, scale=scale)
                        elif u == 2:
                            a.wait_ge(roped, r)
                            one = a.activation(RAW, two, ACT.Copy, scale=scale)
                        elif u < 5:
                            one = a.copy(KN[:, 2 * (u - 3):2 * (u - 3) + 2, :], two)
                        else:
                            one = a.copy(VT[:, u - 5, ds(r * (G4 * VD), G4 * VD)], sums)
                        one.then_inc(p_taken, 1)

                def soft(r):
                    for i in range(G4):
                        a.wait_ge(neg_ready, r * G4 + (i + 1))
                        a.wait_ge(pt_sums, 1 + r * G4)
                        for q, (lo, hi) in enumerate(PIECES):
                            c = 2 * i + q
                            a.activation(PB[:, i, lo:hi], SB[:, i, lo:hi], ACT.Exp, bias=NM[:, c:c + 1],
                                         accum_out=SUMS[:, c:c + 1]).then_inc(exp_done, 1)

                def save_turned(r):
                    for i in range(G4):
                        a.wait_ge(pt_sums, 1 + r * G4 + (i + 1))
                        a.copy(PTB[:, i, :], PS[:, i, 0:SCORES]).then_inc(pt_saved, 1)

                a.wait_ge(n_ht.sem, ht_at)
                save(0)
                with a.Fori(0, ROUNDS - 1) as r:
                    soft(r)
                    save(r + 1)
                    save_turned(r)
                soft(ROUNDS - 1)
                save_turned(ROUNDS - 1)
                turn_act()

            def dve_():
                def turn_queries(r):
                    v.wait_ge(p_taken, r * UNITS + 3)
                    v.wait_ge(s_sums, r * G4)
                    rope(QR, RAW, T1, T2, roped)

                def four(r, more):
                    v.wait_ge(exp_done, 1 + r * (2 * G4))
                    for i in range(G4):
                        v.wait_ge(s_sums, r * G4 + (i + 1))
                        v.tensor_tensor(SB[:, i, :], PS[:, i, 0:SCORES], MLA_MASK, ALU.add).then_inc(s_taken, 1)
                    for i in range(G4):
                        v.wait_ge(s_taken, r * G4 + (i + 1))
                        for q, (lo, hi) in enumerate(PIECES):
                            c = 2 * i + q
                            last = v.tensor_reduce(TMPM[:, c:c + 1], SB[:, i, lo:hi], AX_X, ALU.max)
                        dve.link(v, last)
                        v.tensor_scalar(NM[:, 2 * i:2 * i + 2], TMPM[:, 2 * i:2 * i + 2], -1.0, None, ALU.mult).then_inc(neg_ready, 1)
                    if more:
                        turn_queries(r + 1)
                    v.wait_ge(exp_done, 1 + r * (2 * G4) + 2 * G4)
                    dve.link(v, v.reciprocal(RS, SUMS))
                    for i in range(G4):
                        v.wait_ge(pv_sums, r * G4 + (i + 1))
                        for q in range(2):
                            c = 2 * i + q
                            v.tensor_scalar(O[:, q, ds(r * (G4 * VD) + i * VD, VD)], PS[:, i, q * VD:(q + 1) * VD],
                                            RS[:, c:c + 1], None, ALU.mult).then_inc(o_taken, 1)

                v.wait_ge(n_h.sem, n_h_at)
                turn_queries(0)
                with v.Fori(0, ROUNDS - 1) as r:
                    dve.enter(r, G4 + 2)
                    four(r, True)
                    dve.leave(ROUNDS - 1)
                four(ROUNDS - 1, False)
                out_take(v)
                mark()

            return Stage(sync=sync, pe=pe_, act=act_, dve=dve_)

        def mark_norm():
            x_ready.plan(1)
            at = n_h.total

            def dve_():
                v.wait_ge(n_h.sem, at)
                v.memset(SM[:, 500:501], 0.0).then_inc(x_ready.sem, 1)
            return Stage(dve=dve_)

        def write_out():
            at, out_done = n_h.total, sem("out_done")

            def sync():
                sp.wait_ge(n_h.sem, at)
                sp.dma_start(t["out"].rearrange("(t p) d -> p t d", p=P), H[:, 0:2, :]).then_inc(out_done, 16)
                sp.wait_ge(out_done, 16)
            return Stage(sync=sync)

        stages = []
        first, cs_done, CS = setup()
        stages.append(first)
        stages.append(ada(0, N_MOD, cs_done, CS))
        mod1 = [(0, D)] * 2 + [(6 * D, 7 * D)] * 2
        stages.append(norm(None, range(4), gain=t["norm1_g"][0], mod=mod1))
        stages.append(chunk_mixer(n_ht.total))
        mod2 = [(3 * D, 4 * D)] * 2 + [(9 * D, 10 * D)] * 2
        stages.append(norm(None, range(4), gain=t["norm2_g"][0], mod=mod2))
        stages.append(peer(0, 4, n_ht.total))
        stages.append(ssm_matrices())
        stages.append(ada(1, 2, cs_done, CS))
        stages.append(norm(None, range(4), gain=t["norm1_g"][1], mod=mod1))
        stages.append(ssm(n_ht.total))
        stages.append(norm(None, range(2), gain=t["norm2_g"][1], mod=mod2[:2]))
        stages.append(peer(1, 2, n_ht.total))
        stages.append(norm(None, range(2), gain=t["final_g"], dst=lambda tb: XA[:, tb, :], junk=lambda tb: H[:, tb, :], out_ht=False))
        stages.append(mark_norm())
        stages.append(norm(None, range(2), gain=t["fox_norm"]))
        stages.append(fox(n_ht.total))
        stages.append(norm(None, range(2), gain=t["ffn_norm"][0]))
        stages.append(ffn(0, n_ht.total))
        stages.append(norm(None, range(2), gain=t["kv_in_norm"], ht_off=SEQ))
        stages.append(norm(None, range(2), gain=t["mla_norm"]))
        stages.append(mla_down(n_ht.total))
        stages.append(norm(CKV, range(2), gain=t["kv_norm"], width=KVL, dst=CKV, junk=lambda tb: view(2048 + tb * D, KVL), ht_off=SEQ))
        stages.append(norm(QD, range(2), gain=t["q_norm"], width=QL, dst=QD, junk=lambda tb: view(2048 + tb * D, QL)))
        stages.append(mla(n_ht.total))
        stages.append(norm(None, range(2), gain=t["ffn_norm"][1]))
        stages.append(ffn(1, n_ht.total))
        stages.append(norm(None, range(2), gain=t["final_norm"], out_ht=False))
        stages.append(write_out())
        block = ctx.enter_context(nc.Block())

        @block.sync
        def _(eng):
            for s in stages:
                if s.sync:
                    s.sync()

        @block.tensor
        def _(eng):
            for s in stages:
                if s.pe:
                    s.pe()

        @block.scalar
        def _(eng):
            for s in stages:
                if s.act:
                    s.act()

        @block.vector
        def _(eng):
            for s in stages:
                if s.dve:
                    s.dve()

        @block.gpsimd
        def _(eng):
            for s in stages:
                if s.pool:
                    s.pool()


def blocks(w):
    k, n = w.shape
    return np.ascontiguousarray(w.reshape(k // P, P, n // COLS, COLS).transpose(2, 1, 0, 3).reshape(n // COLS, P, -1))


def sincos(pos, dim):
    omega = 1.0 / (10000.0 ** (np.arange(dim // 2, dtype=np.float32) / np.float32(dim // 2)))
    ang = (pos[:, None] * omega[None, :].astype(np.float32)).astype(np.float32)
    return np.concatenate([np.sin(ang), np.cos(ang)], axis=-1)


def constants():
    rows = np.repeat(np.arange(SEQ // GRID_W, dtype=np.float32), GRID_W)
    cols = np.tile(np.arange(GRID_W, dtype=np.float32), SEQ // GRID_W)
    pos = np.concatenate([sincos(rows, D // 2), sincos(cols, D // 2)], axis=-1).astype(np.float32)
    c = np.zeros((P, C_SUF + 2 * SEQ), np.float32)
    c[:, C_ID:C_ID + P] = np.eye(P)
    s, tt = np.arange(SEQ)[:, None], np.arange(SEQ)[None, :]
    tri = (s <= tt).astype(np.float32)
    c[:, C_TRI:C_TRI + SEQ], c[:, C_TRI + SEQ:C_TRI + 3 * P] = tri[:P], tri[P:, P:]
    c[:, C_SUF:C_SUF + SEQ], c[:, C_SUF + SEQ:C_SUF + 2 * SEQ] = 1 - tri[:P], 1 - tri[P:]
    q, k = np.arange(P)[:, None], np.arange(P)[None, :]
    for at, seen in ((C_FOX, k <= q), (C_MLA, k // 64 <= q // 64)):
        m = np.where(seen, 0.0, MASKED)
        c[:, at:at + P] = m
        c[:, at + 2 * P:at + 3 * P] = m
    inv = (np.float32(10000.0) ** (-np.arange(0, ROPE, 2, dtype=np.float32) / np.float32(ROPE))).astype(np.float32)
    ang = (np.arange(SEQ, dtype=np.float32)[:, None] * inv[None, :]).astype(np.float32)
    c[:, C_COS:C_COS + SEQ] = np.tile(np.cos(ang).T, (4, 1))
    c[:, C_SIN:C_SIN + SEQ] = np.tile(np.sin(ang).T, (4, 1))
    c[:, C_IOTA:C_IOTA + TOPK] = np.arange(TOPK)
    return pos, c


def layout(i):
    i = {k: np.asarray(x) for k, x in i.items()}
    pos, consts = constants()
    o = {
        "x": i["x"][0], "ctx": i["ctx"][0], "pos": pos, "consts": consts,
        "cond": np.stack([i["c"][0], i["c_ctx"]], -1).reshape(KT, P, 2).transpose(1, 0, 2),
        "ada_b": i["ada_b"], "norm1_g": i["norm1_g"], "norm2_g": i["norm2_g"], "final_g": i["final_g"],
        "cm_w_in": blocks(i["cm_w_in"][0]), "cm_w_out": blocks(i["cm_w_out"][0]),
        "cm_ws": i["cm_w_s"][0].transpose(2, 0, 1), "cm_bs": i["cm_b_s"][0].T,
        "cm_ln_g": i["cm_ln_g"][0], "cm_ln_b": i["cm_ln_b"][0],
        "peer_u": i["peer_u"].reshape(-1, D), "peer_v": i["peer_v"].reshape(-1, D),
        "peer_keys": i["peer_keys"].transpose(0, 4, 1, 2, 3).reshape(DEPTH, 2, P, HEADS, 2, KEYS).transpose(0, 2, 3, 4, 1, 5),
    }
    for l in range(DEPTH):
        o[f"ada_w{l}"] = blocks(i["ada_w"][l])
        o[f"peer_w_q{l}"] = blocks(i["peer_w_q"][l])
    pairs = np.stack(np.split(i["ssm_w_out"][0].reshape(D, 2 * D // COLS, COLS), 2, axis=1), 2).reshape(D, 2 * D)
    both = lambda x: x[0].transpose(0, 2, 1).reshape(P, GROUPS)
    o |= {
        "ssm_w_in": blocks(i["ssm_w_in"][0]), "ssm_w_out": blocks(pairs), "ssm_d": i["ssm_d"][0],
        "ssm_lr": both(i["ssm_lam_re"]), "ssm_li": both(i["ssm_lam_im"]),
        "ssm_ls": np.repeat(i["ssm_log_step"][0], STATE, axis=0),
    }
    for n in ("re", "im"):
        o["ssm_b" + n[0]] = i["ssm_b_" + n][0].transpose(0, 2, 1, 3).reshape(P, GROUPS, GDIM)
        o["ssm_c" + n[0]] = i["ssm_c_" + n][0].transpose(0, 3, 1, 2).reshape(P, GROUPS, GDIM)
    w, h3 = i["w_fox_in_2"][0], FOX_H * FOX_D
    q, k, v = (w[:, n * h3:(n + 1) * h3].reshape(D, FOX_H // 2, P) for n in range(3))
    down, uq = i["w_dkv_2"], i["w_uq_2"][0].reshape(QL, MLA_H // 4, 4, NOPE + ROPE)
    half = ROPE // 2
    uq = np.concatenate([uq[..., :NOPE].reshape(QL, 4, -1), uq[..., NOPE:NOPE + half].reshape(QL, 4, -1),
                         uq[..., NOPE + half:].reshape(QL, 4, -1)], -1).reshape(QL, -1)
    fours = lambda m: m.reshape(KVL // P, P, MLA_H // 4, 4 * P).transpose(2, 1, 0, 3).reshape(MLA_H // 4, P, -1)
    o |= {
        "fox_norm": i["fox_norm_2"][0], "fox_b": i["b_fox_f_2"][0], "fox_out": blocks(i["w_fox_out_2"][0]),
        "fox_qk": blocks(np.concatenate([q, k], -1).reshape(D, -1)), "fox_v": blocks(v.reshape(D, -1)),
        "fox_f": w[:, 3 * h3:].reshape(KT, P, FOX_H).transpose(1, 0, 2),
        "ffn_norm": i["ffn_norm_2"], "kv_in_norm": i["kv_in_norm_2"], "kv_norm": i["kv_norm_2"],
        "mla_norm": i["mla_norm_2"][0], "q_norm": i["q_norm_2"][0], "final_norm": i["final_norm_2"],
        "mla_down": blocks(np.concatenate([i["w_dq_2"][0], down[:, :KVL]] + [down[:, KVL:KVL + half]] * 4
                                          + [down[:, KVL + half:]] * 4, -1)),
        "mla_uq": blocks(uq), "mla_ukv": np.concatenate([fours(i["w_uk_2"]), fours(i["w_uv_2"])], -1),
        "mla_out": i["w_mla_out_2"][0].reshape(-1, P, KT, P).transpose(2, 1, 0, 3).reshape(KT, P, -1),
    }
    taps = np.concatenate([i["ffn_conv_w_2"], i["ffn_conv_b_2"][:, None]], 1)
    o["ffn_conv"] = taps.reshape(DEPTH, 4, 2, FFC, 2, P).transpose(0, 5, 3, 2, 4, 1).reshape(DEPTH, P, FFC, 16)
    for l in range(DEPTH):
        o[f"ffn_gate{l}"], o[f"ffn_val{l}"] = (blocks(m) for m in np.split(i["w_ffn_in_2"][l], 2, axis=1))
        o[f"ffn_out{l}"] = i["w_ffn_out_2"][l].reshape(FFC, 2, P, D).transpose(0, 2, 1, 3).reshape(FFC, P, -1)
    return {k: np.ascontiguousarray(x) for k, x in o.items()}


def kernel(**inputs):
    import concourse.bacc as bacc
    from concourse.bass_utils import run_bass_kernel_spmd as run

    nc = bacc.Bacc("TRN2", target_bir_lowering=False, num_devices=1)
    arrays = {f"in_{n}": x for n, x in layout(inputs).items()}
    t = {n[3:]: nc.dram_tensor(n, x.shape, mybir.dt.from_np(x.dtype), kind="ExternalInput").ap() for n, x in arrays.items()}
    t["out"] = nc.dram_tensor("out", [SEQ, D], F32, kind="ExternalOutput").ap()
    program(nc, t)
    return run(nc, [arrays], core_ids=[0]).results[0]["out"].reshape(1, SEQ, D)
```

```python
import math
from contextlib import ExitStack

import numpy as np

import concourse.bass as bass
from concourse import mybir

ALU = mybir.AluOpType
ACT = mybir.ActivationFunctionType
F32 = mybir.dt.float32
U32 = mybir.dt.uint32
AX_X = mybir.AxisListType.X
ds = bass.ds

P = 128
D = 1024
KT = D // P
SEQ = 256
TOK = 2 * SEQ
DEPTH = 2
N_MOD = 6
EPS = 1e-6
GRID_W = 64
BLK = 2048
COLS = BLK // KT
SLOTS = 4
HEADS, KEYS, TOPK, DHALF = 8, 128, 16, 256
EXPERTS = KEYS * KEYS
RING = 8
GROUPS, GDIM, STATE = 64, 16, 64
T8 = 8
NBLK = TOK // T8
LATB = SEQ // T8
CG = 8
FOX_H, FOX_D = 16, 64
MLA_H, NOPE, ROPE, VD = 16, 128, 64, 128
KVL, QL = 256, 768
D_FF = 2816
FFC = D_FF // 256
NEG = -3.0e38
MASKED = -1.0e30
TWO_PI = 2.0 * math.pi
PI_A = 6.28125
PI_B = float(np.float32(round((TWO_PI - PI_A) * 2.0 ** 21) / 2.0 ** 21))
PI_C = TWO_PI - PI_A - PI_B
ROUND = 1.5 * 2.0 ** 23
PI_F = 3.1415925

C_ID, C_TRI, C_FOX, C_MLA, C_COS, C_SIN, C_IOTA = 0, 128, 512, 896, 1280, 1536, 1792
C_ALL = 1808
C_SUF = C_ALL


class Signal:

    def __init__(self, sem, credit=0):
        self.sem, self.total, self.credit = sem, credit, credit

    def plan(self, n):
        base = self.total
        self.total += n
        return base


class Chain:

    def __init__(self, sem):
        self.sem, self.n, self.it, self.per = sem, 0, None, 0

    def link(self, eng, ins):
        self.n += 1
        ins.then_inc(self.sem, 1)
        eng.wait_ge(self.sem, self.n if self.it is None else self.it * self.per + self.n)

    def enter(self, it, per):
        self.it, self.per, self.start = it, per, self.n

    def leave(self, rounds):
        assert self.n - self.start == self.per, (self.n - self.start, self.per)
        self.n = self.start + self.per * rounds
        self.it = None


class Stage:
    def __init__(self, sync=None, pe=None, act=None, dve=None, pool=None):
        self.sync, self.pe, self.act, self.dve, self.pool = sync, pe, act, dve, pool


def program(nc, t):
    with ExitStack() as ctx:
        def sb(name, shape, dt=F32):
            return ctx.enter_context(nc.sbuf_tensor(name, shape, dt))

        def sem(name):
            return ctx.enter_context(nc.semaphore(name))

        primed_sems = []

        def primed(name, n=1):
            primed_sems.append((sem(name), n))
            return primed_sems[-1][0]

        def dram(name, shape):
            return nc.dram_tensor(name, shape, F32, kind="Internal").ap()

        XA = sb("XA", [P, 4, D])
        H = sb("H", [P, 4, D])
        HT = sb("HT", [P, KT, TOK])
        W = sb("W", [P, SLOTS, BLK])
        CON = sb("CON", [P, C_ALL])
        AR = sb("AR", [P, 30208])
        SM = sb("SM", [P, 512])
        PS = ctx.enter_context(nc.psum_tensor("PS", [P, 8, 512], F32))

        u_scr = dram("u_scr", [TOK, D])
        y_scr = dram("y_scr", [SEQ, D])
        min_scr = dram("min_scr", [GROUPS // CG, P, CG * 2 * P])
        mout_scr = dram("mout_scr", [GROUPS // CG, P, 2 * CG * P])
        mod_scr = dram("mod_scr", [DEPTH, 2, N_MOD * D])
        step_scr = dram("step_scr", [P, 4 * GROUPS])
        LAGS = (2 * T8 - 1) * GDIM
        LAG_STEP = LAGS + (T8 - 1) * GDIM
        lag_scr = dram("lag_scr", [GDIM, GROUPS, 2 * LAG_STEP])

        def view(off, *dims):
            n = int(np.prod(dims))
            assert off + n <= 30208
            ap = AR[:, off:off + n]
            if len(dims) == 2:
                return ap.rearrange("p (a b) -> p a b", a=dims[0])
            if len(dims) == 3:
                return ap.rearrange("p (a b c) -> p a b c", a=dims[0], b=dims[1])
            if len(dims) == 4:
                return ap.rearrange("p (a b c d) -> p a b c d", a=dims[0], b=dims[1], c=dims[2])
            return ap

        IDENT = CON[:, C_ID:C_ID + P]
        TRI = CON[:, C_TRI:C_TRI + 3 * P]
        FOX_MASK, MLA_MASK = CON[:, C_FOX:C_FOX + 3 * P], CON[:, C_MLA:C_MLA + 3 * P]
        COS, SIN = CON[:, C_COS:C_COS + SEQ], CON[:, C_SIN:C_SIN + SEQ]
        IOTA = CON[:, C_IOTA:C_IOTA + TOPK]
        MODX = [view(r * D, D) for r in range(N_MOD)]
        MODC = [view((N_MOD + r) * D, D) for r in range(N_MOD)]
        GAIN = view(29184, D)

        w_full = [sem(f"w_full{s}") for s in range(SLOTS)]
        w_used = [sem(f"w_used{s}") for s in range(SLOTS)]
        uses = [0] * SLOTS
        sums_taken = Signal(sem("sums_taken"), 64)
        x_ready = Signal(sem("x_ready"))
        n_sumsq = Signal(sem("n_sumsq"))
        n_var = Signal(sem("n_var"))
        n_std = Signal(sem("n_std"))
        n_h = Signal(sem("n_h"))
        n_turned = Signal(sem("n_turned"))
        n_ht = Signal(sem("n_ht"))
        gain_in = Signal(sem("gain_in"))
        parted = sem("parted")
        load_in = Signal(sem("load_in"))
        dve = Chain(sem("dve_chain"))
        act = Chain(sem("act_chain"))
        pool = Chain(sem("pool_chain"))
        v, a, g, pe, sp = nc.vector, nc.scalar, nc.gpsimd, nc.tensor, nc.sync

        def take(counts):
            base = list(uses)
            for s, n in enumerate(counts):
                uses[s] += n
            return base

        def load(slot, n, src, cols=BLK):
            sp.wait_ge(w_used[slot], n + 1)
            sp.dma_start(W[:, slot, 0:cols], src).then_inc(w_full[slot], 16)

        def wblock(w, i):
            return w[ds(i, 1)].rearrange("a p c -> (a p) c")

        def apart(eng):
            eng.sem_inc(parted, 1)

        def row(ap):
            return ap.partition_broadcast(P)

        def setup():
            in_sem, cs_done = sem("inputs_in"), sem("silu_done")
            CV = SM[:, 24:24 + 2 * KT].rearrange("p (k c) -> p k c", c=2)
            CS = SM[:, 44:44 + 2 * KT].rearrange("p (k c) -> p k c", c=2)
            xr = x_ready.plan(1)

            def sync():
                for one, n in [(one, 1) for one in w_used] + primed_sems:
                    sp.sem_inc(one, n)
                for signal in (sums_taken, u_used, v_used, y_taken, q_saved, s_saved):
                    sp.sem_inc(signal.sem, signal.credit)
                sp.dma_start(CV, t["cond"]).then_inc(in_sem, 16)
                sp.dma_start(XA[:, 0:2, :], t["x"].rearrange("(t p) d -> p t d", p=P)).then_inc(in_sem, 16)
                sp.dma_start(XA[:, 2:4, :], t["ctx"].rearrange("(t p) d -> p t d", p=P)).then_inc(in_sem, 16)
                sp.dma_start(H[:, 0:2, :], t["pos"].rearrange("(t p) d -> p t d", p=P)).then_inc(in_sem, 16)
                sp.dma_start(CON[:, :], t["consts"][:, 0:C_ALL]).then_inc(in_sem, 16)

            def act_():
                a.wait_ge(in_sem, 80)
                a.activation(CS, CV, ACT.Silu).then_inc(cs_done, 1)

            def dve_():
                v.wait_ge(in_sem, 80)
                v.tensor_tensor(XA[:, 0:2, :], XA[:, 0:2, :], H[:, 0:2, :], ALU.add).then_inc(x_ready.sem, 1)

            return Stage(sync=sync, act=act_, dve=dve_), cs_done, CS

        mod_stored = sem("mod_stored")

        def load_mod(layer, rows_c):
            li = load_in.plan(32)
            xr = x_ready.total

            def sync():
                sp.wait_ge(x_ready.sem, xr)
                sp.wait_ge(mod_stored, 32)
                sp.dma_start(AR[:, 0:N_MOD * D], row(mod_scr[layer, 0])).then_inc(load_in.sem, 16)
                sp.dma_start(AR[:, N_MOD * D:(N_MOD + rows_c) * D], row(mod_scr[layer, 1, 0:rows_c * D])).then_inc(load_in.sem, 16)

            def dve_():
                v.wait_ge(load_in.sem, li + 32)

            return Stage(sync=sync, dve=dve_)

        NEPS = SM[:, 0:1]
        SUMSQ, VAR, STD, RSTD = (SM[:, 4 + 4 * i:8 + 4 * i] for i in range(4))

        def norm(src, tbs, gain=None, mod=None, dst=None, width=D, junk=None, out_ht=True, ht_off=0):
            src = src or (lambda tb: XA[:, tb, :])
            dst = dst or (lambda tb: H[:, tb, :])
            n = len(tbs)
            xr = x_ready.total
            ss, va, sd, hh = n_sumsq.plan(n), n_var.plan(n), n_std.plan(n), n_h.plan(n)
            kt = width // P
            halves = (kt + 3) // 4
            tu, ht = n_turned.plan(n * halves), n_ht.plan(n * halves)
            gi = gain_in.plan(16)
            grow = GAIN[:, 0:width]

            def sync():
                sp.wait_ge(x_ready.sem, xr)
                if hh:
                    sp.wait_ge(n_h.sem, hh)
                sp.dma_start(grow, row(gain)).then_inc(gain_in.sem, 16)

            def act_():
                a.wait_ge(x_ready.sem, xr)
                if hh:
                    a.wait_ge(n_h.sem, hh)
                if tu:
                    a.wait_ge(n_turned.sem, tu)
                for i, tb in enumerate(tbs):
                    a.activation((junk or dst)(tb), src(tb), ACT.Square, accum_out=SUMSQ[:, i:i + 1]).then_inc(n_sumsq.sem, 1)
                for i, tb in enumerate(tbs):
                    a.wait_ge(n_var.sem, va + i + 1)
                    a.activation(STD[:, i:i + 1], VAR[:, i:i + 1], ACT.Sqrt).then_inc(n_std.sem, 1)
                if not out_ht:
                    return
                for i, tb in enumerate(tbs):
                    for q in range(halves):
                        m = min(4, kt - 4 * q)
                        a.wait_ge(n_turned.sem, tu + i * halves + q + 1)
                        a.copy(HT[:, 4 * q:4 * q + m, ht_off + i * P:ht_off + (i + 1) * P],
                               PS[:, 4 + (i * halves + q) % 4, 0:m * P].rearrange("p (k t) -> p k t", k=m)).then_inc(n_ht.sem, 1)

            def dve_():
                for i, tb in enumerate(tbs):
                    v.wait_ge(n_sumsq.sem, ss + i + 1)
                    v.tensor_scalar(VAR[:, i:i + 1], SUMSQ[:, i:i + 1], 1.0 / width, EPS, ALU.mult, ALU.add).then_inc(n_var.sem, 1)
                v.wait_ge(gain_in.sem, gi + 16)
                if mod:
                    for shift, scale in dict.fromkeys(mod):
                        sc = AR[:, scale:scale + D]
                        dve.link(v, v.scalar_tensor_tensor(sc, sc, 1.0, grow, ALU.add, ALU.mult))
                for i, tb in enumerate(tbs):
                    v.wait_ge(n_std.sem, sd + i + 1)
                    dve.link(v, v.reciprocal(RSTD[:, i:i + 1], STD[:, i:i + 1]))
                    mul = AR[:, mod[i][1]:mod[i][1] + D] if mod else grow
                    one = v.scalar_tensor_tensor(dst(tb), src(tb), RSTD[:, i:i + 1], mul, ALU.mult, ALU.mult)
                    if mod:
                        dve.link(v, one)
                        one = v.tensor_tensor(dst(tb), dst(tb), AR[:, mod[i][0]:mod[i][0] + D], ALU.add)
                    one.then_inc(n_h.sem, 1)

            def pe_():
                if not out_ht:
                    return
                for i, tb in enumerate(tbs):
                    pe.wait_ge(n_h.sem, hh + i + 1)
                    for q in range(halves):
                        b = i * halves + q
                        if b >= 4:
                            pe.wait_ge(n_ht.sem, ht + b - 3)
                        elif ht:
                            pe.wait_ge(n_ht.sem, ht)
                        m = min(4, kt - 4 * q)
                        for k in range(m):
                            mm = pe.transpose(PS[:, 4 + b % 4, k * P:(k + 1) * P],
                                              dst(tb)[:, (4 * q + k) * P:(4 * q + k + 1) * P], IDENT)
                        mm.then_inc(n_turned.sem, 1)

            if not out_ht:
                n_turned.total -= n * halves
                n_ht.total -= n * halves
            return Stage(sync=sync, pe=pe_ , act=act_, dve=dve_)

        def turn(src, tbs, kt, ready, ready_at, dst):
            halves = kt // 4
            n = len(tbs)
            tu, ht = n_turned.plan(n * halves), n_ht.plan(n * halves)

            def pe_():
                for i, tb in enumerate(tbs):
                    pe.wait_ge(ready, ready_at(i))
                    for q in range(halves):
                        b = i * halves + q
                        pe.wait_ge(n_ht.sem, ht + max(0, b - 3))
                        for k in range(4):
                            mm = pe.transpose(PS[:, 4 + b % 4, k * P:(k + 1) * P],
                                              src(tb)[:, (4 * q + k) * P:(4 * q + k + 1) * P], IDENT)
                        mm.then_inc(n_turned.sem, 1)

            def act_():
                for i, tb in enumerate(tbs):
                    for q in range(halves):
                        b = i * halves + q
                        a.wait_ge(n_turned.sem, tu + b + 1)
                        a.copy(dst(q, i), PS[:, 4 + b % 4, :].rearrange("p (k t) -> p k t", k=4)).then_inc(n_ht.sem, 1)

            return pe_, act_, ht + n * halves

        def linear(w, nblk, ntb, lhs, evac, unroll=4, ht_at=None, kt=KT):
            uw = take([nblk // unroll if s < unroll else 0 for s in range(SLOTS)])
            st = sums_taken.plan(nblk * ntb)
            rounds = nblk // unroll
            cols = BLK // kt

            def sync():
                with sp.Fori(0, rounds) as r:
                    for s in range(unroll):
                        load(s, r + uw[s], wblock(w, r * unroll + s))

            def bank(s, tb):
                return PS[:, (s % 2) * 2 + tb // 2, (tb % 2) * cols:(tb % 2 + 1) * cols]

            def pe_():
                if ht_at is not None:
                    pe.wait_ge(n_ht.sem, ht_at)
                pe.wait_ge(sums_taken.sem, st)
                with pe.Fori(0, rounds) as r:
                    for s in range(unroll):
                        pe.wait_ge(w_full[s], (r + uw[s] + 1) * 16)
                        pe.wait_ge(sums_taken.sem, r * (unroll * ntb) + (st + (s - 1) * ntb))
                        for tb in range(ntb):
                            for k in range(kt):
                                mm = pe.matmul(bank(s, tb), lhs(k, tb), W[:, s, k * cols:(k + 1) * cols],
                                               start=(k == 0), stop=(k == kt - 1))
                        mm.then_inc(w_used[s], 1)

            def take_sums(eng, chain=None, per=0):
                with eng.Fori(0, rounds) as r:
                    if chain:
                        chain.enter(r, per)
                    for s in range(unroll):
                        eng.wait_ge(w_used[s], r + uw[s] + 2)
                        for tb in range(ntb):
                            evac(r * unroll + s, tb, bank(s, tb)).then_inc(sums_taken.sem, 1)
                if chain:
                    chain.leave(rounds)

            return sync, pe_, take_sums, st + nblk * ntb

        def add_gated(gate_of, ntb, tmp, cols=COLS):
            def evac(blk, tb, sums):
                dst = XA[:, tb, ds(blk * cols, cols)]
                if gate_of is None:
                    return v.tensor_tensor(dst, dst, sums, ALU.add)
                half = tmp[:, tb % 2, :]
                dve.link(v, v.tensor_tensor(half, sums, AR[:, ds(blk * cols + gate_of(tb), cols)], ALU.mult))
                return v.tensor_tensor(dst, dst, half, ALU.add)
            return evac

        def mark_x(n_h_unused=None):
            x_ready.plan(1)

            def dve_():
                v.wait_ge(sums_taken.sem, sums_now[0])
                v.memset(SM[:, 500:501], 0.0).then_inc(x_ready.sem, 1)
            sums_now = [sums_taken.total]
            return dve_

        def chunk_mixer(ht_at):
            Z = view(12288, 4, 2 * D)
            WS = view(20480, KT, P)
            BS = view(21504, KT)
            LNG, LNB = view(22528, D), view(23552, D)
            JUNK = view(24576, D)
            TMP = view(25600, 2, COLS)
            MEAN, NMEAN, VARV, STDV, RV = (SM[:, 24 + 4 * i:28 + 4 * i] for i in range(5))
            z_done = sem("z_done")
            mean_done, nmean_done, var_sum, var_done, std_done, v_done = (sem("cm_" + n) for n in
                ("sum", "negmean", "sqsum", "var", "std", "v"))
            mix_done, mixed = sem("cm_spatial"), sem("cm_mixed")
            li = load_in.plan(64)
            par_in = load_in.sem

            def gelu_out(blk, tb, sums):
                return a.activation(Z[:, tb, ds(blk * COLS, COLS)], sums, ACT.Gelu_apprx_tanh)

            in_sync, in_pe, in_take, in_end = linear(t["cm_w_in"], 8, 4, lambda k, tb: HT[:, k, tb * P:(tb + 1) * P],
                                                     gelu_out, ht_at=ht_at)
            turn_pe, turn_act, turn_end = turn(lambda tb: Z[:, tb, 0:D], range(4), KT, mixed, lambda i: 8 * (i + 1),
                                               lambda q, i: HT[:, 4 * q:4 * q + 4, i * P:(i + 1) * P])
            out_sync, out_pe, out_take, out_end = linear(t["cm_w_out"], 4, 4, lambda k, tb: HT[:, k, tb * P:(tb + 1) * P],
                                                         add_gated(lambda tb: (2 if tb < 2 else 8) * D, 4, TMP), ht_at=turn_end)
            mark = mark_x()
            cb_free = n_h.total

            def sync():
                sp.wait_ge(n_h.sem, cb_free)
                sp.dma_start(WS, t["cm_ws"]).then_inc(par_in, 16)
                sp.dma_start(BS, t["cm_bs"]).then_inc(par_in, 16)
                sp.dma_start(LNG, row(t["cm_ln_g"])).then_inc(par_in, 16)
                sp.dma_start(LNB, row(t["cm_ln_b"])).then_inc(par_in, 16)
                in_sync()
                out_sync()

            def act_():
                in_take(a)
                a.wait_ge(sums_taken.sem, in_end)
                for tb in range(4):
                    a.activation(JUNK, Z[:, tb, D:2 * D], ACT.Copy, accum_out=MEAN[:, tb:tb + 1]).then_inc(mean_done, 1)
                    a.wait_ge(mean_done, tb + 1)
                for tb in range(4):
                    a.wait_ge(nmean_done, tb + 1)
                    a.activation(JUNK, Z[:, tb, D:2 * D], ACT.Square, bias=NMEAN[:, tb:tb + 1],
                                 accum_out=VARV[:, tb:tb + 1]).then_inc(var_sum, 1)
                    a.wait_ge(var_sum, tb + 1)
                for tb in range(4):
                    a.wait_ge(var_done, tb + 1)
                    a.activation(STDV[:, tb:tb + 1], VARV[:, tb:tb + 1], ACT.Sqrt).then_inc(std_done, 1)
                turn_act()

            def dve_():
                for tb in range(4):
                    v.wait_ge(mean_done, tb + 1)
                    v.tensor_scalar(NMEAN[:, tb:tb + 1], MEAN[:, tb:tb + 1], -1.0 / D, None, ALU.mult).then_inc(nmean_done, 1)
                for tb in range(4):
                    v.wait_ge(var_sum, tb + 1)
                    v.tensor_scalar(VARV[:, tb:tb + 1], VARV[:, tb:tb + 1], 1.0 / D, EPS, ALU.mult, ALU.add).then_inc(var_done, 1)
                v.wait_ge(par_in, li + 64)
                v.wait_ge(nmean_done, 4)
                for tb in range(4):
                    zv = Z[:, tb, D:2 * D]
                    v.wait_ge(std_done, tb + 1)
                    dve.link(v, v.reciprocal(RV[:, tb:tb + 1], STDV[:, tb:tb + 1]))
                    dve.link(v, v.tensor_scalar(zv, zv, NMEAN[:, tb:tb + 1], RV[:, tb:tb + 1], ALU.add, ALU.mult))
                    dve.link(v, v.tensor_tensor(zv, zv, LNG, ALU.mult))
                    v.tensor_tensor(zv, zv, LNB, ALU.add).then_inc(v_done, 1)
                for tb in range(4):
                    v.wait_ge(mix_done, tb + 1)
                    for h in range(KT):
                        u = Z[:, tb, h * P:(h + 1) * P]
                        v.scalar_tensor_tensor(u, PS[:, 4 + (tb % 2) * 2 + h // 4, (h % 4) * P:(h % 4 + 1) * P], BS[:, h:h + 1], u,
                                               ALU.add, ALU.mult).then_inc(mixed, 1)
                out_take(v, dve, 16)
                mark()

            def pe_():
                in_pe()
                pe.wait_ge(par_in, li + 64)
                for tb in range(4):
                    pe.wait_ge(v_done, tb + 1)
                    if tb >= 2:
                        pe.wait_ge(mixed, 8 * (tb - 1))
                    for h in range(KT):
                        mm = pe.matmul(PS[:, 4 + (tb % 2) * 2 + h // 4, (h % 4) * P:(h % 4 + 1) * P], WS[:, h, :],
                                       Z[:, tb, D + h * P:D + (h + 1) * P], start=True, stop=True)
                    mm.then_inc(mix_done, 1)
                pe.wait_ge(mixed, 32)
                turn_pe()
                out_pe()

            return Stage(sync=sync, act=act_, dve=dve_, pe=pe_)

        u_full = [sem(f"u_full{s}") for s in range(RING)]
        v_full = [sem(f"v_full{s}") for s in range(RING)]
        u_used, v_used = Signal(sem("u_used"), RING), Signal(sem("v_used"), RING)
        keys_in, q_saved = Signal(sem("keys_in")), Signal(sem("q_saved"), 2)
        q_sums = Signal(sem("q_sums"))
        s_sums, s_saved = Signal(sem("s_sums")), Signal(sem("s_saved"), 2)
        ids_ready, top_shift, exp_done = Signal(sem("ids_ready")), Signal(sem("top_shift")), Signal(sem("exp_done"))
        gelu_done, w_ready, diag_ready = Signal(sem("gelu_done")), Signal(sem("w_ready")), Signal(sem("diag_ready"))
        y_taken = Signal(sem("y_taken"), 2)
        ring_use = [0]

        def peer(layer, ntb, ht_at):
            T = ntb * P
            UB = view(12288, RING, D)
            VB = [view(i * D, D) for i in range(4)] + [view((6 + i) * D, D) for i in range(4)]
            KEY = view(20480, HEADS, 4, KEYS)
            QT = view(24576, 4, TOK)
            S = view(26624, 4, 2, KEYS)
            CAND, CAND2 = view(27648, 2 * KEYS), view(27904, 2 * KEYS)
            S2 = view(28160, 2, KEYS)
            OH = view(28416, 2, TOPK, TOPK)
            DIAG = view(4 * D, 4, P)
            YG = view(10 * D, D)
            at = 64
            TV, IXF, TAB, K12 = (SM[:, at + 32 * i:at + 32 * (i + 1)].rearrange("p (h k) -> p h k", h=2) for i in range(4))
            TI = SM[:, 192:224].bitcast(U32).rearrange("p (h k) -> p h k", h=2)
            TABU = SM[:, 224:256].bitcast(U32).rearrange("p (h k) -> p h k", h=2)
            TS, EX = view(28928, 4, TOPK), view(28992, 4, TOPK)
            TC = SM[:, 272:288].bitcast(U32)
            NTOP, SUM = view(29056, 4), view(29060, 4)
            RSUM = SM[:, 306:307]
            EX2 = view(4 * D + 640, TOPK)
            ACTV = SM[:, 308:372].rearrange("p (t k) -> p t k", t=4)
            GELU = SM[:, 372:436].rearrange("p (t k) -> p t k", t=4)
            GATE = SM[:, 436:500].rearrange("p (t k) -> p t k", t=4)
            WGT = GELU
            IDS = view(4 * D + 512, 4, TOPK).bitcast(U32)
            IDP = view(4 * D + 576, 4, TOPK).bitcast(U32)

            n = HEADS * ntb
            rows_n = n * TOPK
            per_slot = ntb * TOPK // RING
            rb = ring_use[0]
            ring_use[0] += HEADS * per_slot
            uw = take([HEADS, HEADS, 0, 0])
            uu, vu = u_used.plan(rows_n), v_used.plan(rows_n)
            ki = keys_in.plan(16)
            qm, qs = q_sums.plan(HEADS * 2), q_saved.plan(HEADS * 4)
            sm_, sv = s_sums.plan(n), s_saved.plan(n)
            ir, tsh, ed = ids_ready.plan(n), top_shift.plan(n), exp_done.plan(n)
            gd, wr, dr = gelu_done.plan(n), w_ready.plan(n), diag_ready.plan(rows_n)
            yt = y_taken.plan(n)
            hh = n_h.total
            st = sums_taken.total
            xr = x_ready.plan(1)
            H_ROWS = ntb * TOPK

            def sync():
                sp.wait_ge(n_h.sem, hh)
                sp.dma_start(KEY, t["peer_keys"][layer].rearrange("p h a b k -> p h (a b) k")).then_inc(keys_in.sem, 16)
                with sp.Fori(0, HEADS) as h:
                    for s in range(2):
                        load(s, h + uw[s], wblock(t[f"peer_w_q{layer}"], h * 2 + s))

            def queries(h):
                for j in range(4):
                    if j % 2 == 0:
                        pe.wait_ge(w_full[j // 2], (h + uw[j // 2] + 1) * 16)
                    pe.wait_ge(q_saved.sem, h * 4 + (qs + j - 1))
                    for k in range(KT):
                        mm = pe.matmul(PS[:, j % 2, 0:T], W[:, j // 2, k * COLS + (j % 2) * P:k * COLS + (j % 2 + 1) * P],
                                       HT[:, k, 0:T], start=(k == 0), stop=(k == KT - 1))
                    mm.then_inc(w_used[j // 2] if j % 2 else q_sums.sem, 1)
                pe.wait_ge(q_saved.sem, h * 4 + (qs + 4))
                for tb in range(ntb):
                    pe.wait_ge(s_saved.sem, h * ntb + (sv + tb - 1))
                    for half in range(2):
                        for c in range(2):
                            mm = pe.matmul(PS[:, 2 + tb % 2, half * KEYS:(half + 1) * KEYS],
                                           QT[:, half * 2 + c, tb * P:(tb + 1) * P],
                                           KEY[:, ds(h, 1), half * 2 + c, :].rearrange("p a k -> p (a k)"),
                                           start=(c == 0), stop=(c == 1))
                    mm.then_inc(s_sums.sem, 1)

            def pe_head(h, more):
                if more:
                    queries(h + 1)
                for tb in range(ntb):
                    pe.wait_ge(y_taken.sem, h * ntb + (yt + tb - 1))
                    for k in range(TOPK):
                        i = tb * TOPK + k
                        pe.wait_ge(diag_ready.sem, h * H_ROWS + (dr + i + 1))
                        pe.wait_ge(v_full[i % RING], (h * per_slot + (rb + i // RING + 1)) * 16)
                        for c in range(2):
                            mm = pe.matmul(PS[:, 4 + (tb % 2) * 2 + c, :], DIAG[:, k % 4, :], VB[i % RING][:, c * 512:(c + 1) * 512],
                                           start=(k == 0), stop=(k == TOPK - 1))
                        mm.then_inc(v_used.sem, 1)

            def pe_():
                pe.wait_ge(n_ht.sem, ht_at)
                pe.wait_ge(sums_taken.sem, st)
                pe.wait_ge(keys_in.sem, ki + 16)
                queries(0)
                with pe.Fori(0, HEADS - 1) as h:
                    pe_head(h, True)
                pe_head(HEADS - 1, False)

            def save_queries(h):
                for j in range(4):
                    if j % 2:
                        a.wait_ge(w_used[j // 2], h + (uw[j // 2] + 2))
                    else:
                        a.wait_ge(q_sums.sem, h * 2 + (qm + j // 2 + 1))
                    a.copy(QT[:, j, 0:T], PS[:, j % 2, 0:T]).then_inc(q_saved.sem, 1)
                for tb in range(ntb):
                    a.wait_ge(s_sums.sem, h * ntb + (sm_ + tb + 1))
                    a.wait_ge(ids_ready.sem, h * ntb + (ir + tb + 1 - ntb) if not isinstance(h, int) else ir)
                    a.copy(S[:, tb], PS[:, 2 + tb % 2, 0:2 * KEYS].rearrange("p (h k) -> p h k", h=2)).then_inc(s_saved.sem, 1)

            def exps(h, tb):
                a.wait_ge(top_shift.sem, h * ntb + (tsh + tb + 1))
                a.activation(EX[:, tb, :], TS[:, tb, :], ACT.Exp, bias=NTOP[:, tb:tb + 1], accum_out=SUM[:, tb:tb + 1]).then_inc(exp_done.sem, 1)

            def act_head(h, more):
                if more:
                    save_queries(h + 1)
                for tb in range(ntb):
                    a.wait_ge(u_used.sem, h * H_ROWS + (uu + (tb + 1) * TOPK))
                    a.activation(GELU[:, tb, :], ACTV[:, tb, :], ACT.Gelu_apprx_tanh).then_inc(gelu_done.sem, 1)
                    a.wait_ge(w_ready.sem, h * ntb + (wr + tb + 1))
                    for k in range(TOPK):
                        a.wait_ge(v_used.sem, h * H_ROWS + (vu + tb * TOPK + k - 3))
                        a.mul(DIAG[:, k % 4, :], IDENT, WGT[:, tb, k:k + 1]).then_inc(diag_ready.sem, 1)
                    if more:
                        exps(h + 1, tb)

            def act_():
                a.wait_ge(n_h.sem, hh)
                save_queries(0)
                for tb in range(ntb):
                    exps(0, tb)
                with a.Fori(0, HEADS - 1) as h:
                    act_head(h, True)
                act_head(HEADS - 1, False)

            def best16(vals, ix, src, scratch):
                m = len(src)
                apart(v)
                for j in range(m):
                    last = v.max(vals[j][:, 0:8], src[j])
                dve.link(v, last)
                apart(v)
                for j in range(m):
                    v.max_index(ix[j][:, 0:8], vals[j][:, 0:8], src[j])
                    last = v.match_replace(scratch[j], vals[j][:, 0:8], src[j], NEG)
                dve.link(v, last)
                apart(v)
                for j in range(m):
                    last = v.max(vals[j][:, 8:16], scratch[j])
                dve.link(v, last)
                apart(v)
                for j in range(m):
                    last = v.max_index(ix[j][:, 8:16], vals[j][:, 8:16], scratch[j])
                dve.link(v, last)

            def choose(h, tb):
                v.wait_ge(s_saved.sem, h * ntb + (sv + tb + 1))
                best16([TV[:, 0, :], TV[:, 1, :]], [TI[:, 0, :], TI[:, 1, :]], [S[:, tb, 0, :], S[:, tb, 1, :]],
                       [S2[:, 0, :], S2[:, 1, :]])
                v.tensor_copy(IXF, TI)
                dve.link(v, v.tensor_tensor(CAND.rearrange("p (a b) -> p a b", a=TOPK),
                                            TV[:, 0, :].unsqueeze(2).to_broadcast([P, TOPK, TOPK]),
                                            TV[:, 1, :].unsqueeze(1).to_broadcast([P, TOPK, TOPK]), ALU.add))
                best16([TS[:, tb, :]], [TC], [CAND], [CAND2])
                v.tensor_scalar(NTOP[:, tb:tb + 1], TS[:, tb, 0:1], -1.0, None, ALU.mult).then_inc(top_shift.sem, 1)
                v.tensor_scalar(TABU[:, 0, :], TC, 4, None, ALU.logical_shift_right)
                dve.link(v, v.tensor_scalar(TABU[:, 1, :], TC, 15, None, ALU.bitwise_and))
                dve.link(v, v.tensor_copy(TAB, TABU))
                flat = OH.rearrange("p h k j -> p (h k) j")
                dve.link(v, v.tensor_tensor(flat, TAB.rearrange("p h k -> p (h k)").unsqueeze(2).to_broadcast([P, 2 * TOPK, TOPK]),
                                            IOTA.unsqueeze(1).to_broadcast([P, 2 * TOPK, TOPK]), ALU.is_equal))
                dve.link(v, v.tensor_tensor(OH, OH, IXF.unsqueeze(2).to_broadcast([P, 2, TOPK, TOPK]), ALU.mult))
                dve.link(v, v.tensor_reduce(K12.rearrange("p h k -> p (h k)"), flat, AX_X, ALU.add))
                dve.link(v, v.scalar_tensor_tensor(EX2, K12[:, 0, :], float(KEYS), K12[:, 1, :], ALU.mult, ALU.add))
                v.tensor_scalar(IDS[:, tb, :], EX2, float(layer * EXPERTS), None, ALU.add).then_inc(ids_ready.sem, 1)

            def gates(h, tb):
                v.wait_ge(exp_done.sem, h * ntb + (ed + tb + 1))
                dve.link(v, v.reciprocal(RSUM, SUM[:, tb:tb + 1]))
                dve.link(v, v.tensor_scalar(GATE[:, tb, :], EX[:, tb, :], RSUM, None, ALU.mult))

            def add_rows(m):
                h, tb = m
                v.wait_ge(v_used.sem, h * H_ROWS + (vu + (tb + 1) * TOPK))
                gate = MODX[5] if tb < 2 else MODC[5]
                sums = PS[:, 4 + (tb % 2) * 2:6 + (tb % 2) * 2, :].rearrange("p a b -> p (a b)")
                dve.link(v, v.tensor_tensor(YG, sums, gate, ALU.mult))
                v.tensor_tensor(XA[:, tb, :], XA[:, tb, :], YG, ALU.add).then_inc(y_taken.sem, 1)

            def dve_head(h, more, before=True):
                for tb in range(ntb):
                    for k in range(TOPK):
                        i = tb * TOPK + k
                        v.wait_ge(u_full[i % RING], (h * per_slot + (rb + i // RING + 1)) * 16)
                        v.tensor_tensor_reduce(UB[:, i % RING, :], UB[:, i % RING, :], H[:, tb, :], 1.0, 0.0,
                                               ALU.mult, ALU.add, ACTV[:, tb, k:k + 1]).then_inc(u_used.sem, 1)
                    if tb:
                        add_rows((h, tb - 1))
                    elif before:
                        add_rows((h - 1, ntb - 1))
                        gates(h, ntb - 1)
                    v.wait_ge(gelu_done.sem, h * ntb + (gd + tb + 1))
                    v.tensor_tensor(WGT[:, tb, :], GELU[:, tb, :], GATE[:, tb, :], ALU.mult).then_inc(w_ready.sem, 1)
                    if more:
                        if tb:
                            gates(h + 1, tb - 1)
                        choose(h + 1, tb)

            LINKS = 15

            def dve_():
                v.wait_ge(n_h.sem, hh)
                for tb in range(ntb):
                    choose(0, tb)
                    gates(0, tb)
                dve_head(0, True, before=False)
                with v.Fori(1, HEADS - 1) as h:
                    dve.enter(h - 1, ntb * (LINKS + 2 + 1))
                    dve_head(h, True)
                    dve.leave(HEADS - 2)
                dve_head(HEADS - 1, False)
                add_rows((HEADS - 1, ntb - 1))
                v.wait_ge(y_taken.sem, yt + n)
                v.memset(SM[:, 500:501], 0.0).then_inc(x_ready.sem, 1)

            def pool_head(h):
                def fetch(tb, k, table, ring, full, used):
                    i = tb * TOPK + k
                    g.wait_ge(used[0].sem, h * H_ROWS + (used[1] + i + 1 - RING))
                    apart(g)
                    g.indirect_dma_start(out=ring[i % RING], out_offset=None, in_=table,
                                         in_offset=bass.IndirectOffsetOnAxis(ap=IDP[:, tb, k:k + 1], axis=0)).then_inc(full[i % RING], 16)

                ub = [UB[:, i, :] for i in range(RING)]
                for tb in range(ntb + 1):
                    if tb < ntb:
                        g.wait_ge(ids_ready.sem, h * ntb + (ir + tb + 1))
                        apart(g)
                        pool.link(g, g.tensor_copy(IDP[:, tb, :], IDS[:, tb, :]))
                    for k in range(TOPK):
                        if tb < ntb:
                            fetch(tb, k, t["peer_u"], ub, u_full, (u_used, uu))
                        if tb:
                            fetch(tb - 1, k, t["peer_v"], VB, v_full, (v_used, vu))

            def pool_():
                with g.Fori(0, HEADS) as h:
                    pool.enter(h, ntb)
                    pool_head(h)
                    pool.leave(HEADS)

            return Stage(sync=sync, pe=pe_, act=act_, dve=dve_, pool=pool_)

        NCH = GROUPS // CG
        A8R = SM[:, 64:192].rearrange("p (r g) -> p r g", r=2)
        A8S = SM[:, 192:320].rearrange("p (r g) -> p r g", r=2)
        mats_stored = Signal(sem("mats_stored"))

        def front(cs_done, CS):
            at = [N_MOD * DEPTH * D]

            def new(*dims):
                ap = view(at[0], *dims)
                at[0] += int(np.prod(dims))
                return ap

            small = [0]
            HF = HT[:, :, :].rearrange("p k t -> p (k t)")

            def tiny(*dims):
                n = int(np.prod(dims))
                ap = HF[:, small[0]:small[0] + n]
                small[0] += n
                return ap.rearrange("p (a b) -> p a b", a=dims[0]) if len(dims) == 2 else ap.rearrange("p (a b c) -> p a b c", a=dims[0], b=dims[1])

            G_ = GROUPS
            LR, LI, LOGS, STEP, E, MAG, TH, K, RED, SN, CS_, A_R, A_I, DEN, X1, X2, CO_R, CO_I = (tiny(1, G_) for _ in range(18))
            BR, BI, CR, CI, BBR, BBI = (new(G_, GDIM) for _ in range(6))
            T1, T2 = new(G_, GDIM), new(G_, GDIM)
            PR, PI = new(T8 + 1, G_), new(T8 + 1, G_)
            INR, INI, OUTR, OUTI = (new(T8, G_) for _ in range(4))
            MIN = new(2, CG, T8 * GDIM)
            MOUT = new(2, CG, T8 * GDIM)
            CST = new(2, CG, GDIM)
            MT = new(CG * 2, P)
            KS = tiny(CG, 2, GDIM)
            PER = 6
            WIDE = PER * COLS
            EV = tiny(1, WIDE)[0:2, 0, :]
            z_n = GDIM * (2 * T8 - 1) * GDIM
            ZERO = AR[0:GROUPS, 23680:23680 + z_n]
            THIRDS = 3
            uw = take([2 * NCH] * THIRDS + [0])
            ev_saved, ev_added, bias_in = sem("ada_saved"), primed("ada_added"), sem("ada_bias_in")
            a8_done, a8_out = sem("ssm_step_done"), sem("ssm_step_out")
            par_in, zero_done = sem("ssm_par_in"), sem("ssm_zero")
            lr_done, e_done, mag_done, th_done, sin_done = (sem("ssm_" + n) for n in ("lr", "step", "mag", "theta", "sin"))
            min_done, mout_done = sem("ssm_min"), sem("ssm_mout")
            mt_sums, k_sums = primed("ssm_turned"), primed("ssm_lags")
            mt_saved, k_saved = primed("ssm_min_saved"), primed("ssm_lags_saved")
            mt_out, mout_out, k_out = primed("ssm_min_out"), primed("ssm_mout_out"), primed("ssm_lags_out")
            zero_out = sem("ssm_zero_out")
            N_K = T8 * 16

            def slot_use(c, j):
                s = j % THIRDS
                return s, c * 2 + (uw[s] + j // THIRDS)

            def sync():
                sp.sem_inc(ev_saved, 2)
                for dst, name in ((LR[:, 0], "ssm_lr"), (LI[:, 0], "ssm_li"), (LOGS[:, 0], "ssm_ls"), (BR, "ssm_br"), (BI, "ssm_bi"),
                                  (CR, "ssm_cr"), (CI, "ssm_ci")):
                    sp.dma_start(dst, t[name]).then_inc(par_in, 16)
                for c in range(2):
                    sp.dma_start(AR[c:c + 1, 0:DEPTH * N_MOD * D], t["ada_b"].rearrange("(a l) n -> a (l n)", a=1)).then_inc(bias_in, 16)
                def load_blocks(c):
                    for j in range(PER):
                        s, n = slot_use(c, j)
                        load(s, n, wblock(t["ada_w"], c * PER + j))

                def store_matrices(c):
                    sp.wait_ge(mout_done, c + 1)
                    sp.dma_start(wblock(mout_scr, c), MOUT.rearrange("p r g x -> p (r g x)")).then_inc(mout_out, 16)
                    sp.wait_ge(mt_saved, 1 + c + 1)
                    sp.dma_start(wblock(min_scr, c), MT.rearrange("p g x -> p (g x)")).then_inc(mt_out, 16)
                    sp.wait_ge(k_saved, 1 + c * 2 + 2)
                    lags = lag_scr[:, ds(c * CG, CG), :].rearrange("c g (d l) -> c (g d) l", d=2)
                    for s in range(T8):
                        sp.dma_start(lags[:, :, s * GDIM:(s + 1) * GDIM],
                                     KS[s * GDIM:(s + 1) * GDIM].rearrange("p g d x -> p (g d) x")).then_inc(k_out, 16)

                sp.wait_ge(zero_done, 1)
                for d in range(2):
                    sp.dma_start(lag_scr[:, :, d * LAGS:(d + 1) * LAGS].rearrange("c g l -> g c l"),
                                 ZERO.rearrange("g (c l) -> g c l", c=GDIM)).then_inc(zero_out, 16)
                load_blocks(0)
                with sp.Fori(0, NCH - 1) as c:
                    load_blocks(c + 1)
                    store_matrices(c)
                store_matrices(NCH - 1)
                sp.wait_ge(a8_done, 1)
                sp.dma_start(step_scr, SM[:, 64:64 + 4 * GROUPS]).then_inc(a8_out, 16)
                sp.wait_ge(ev_added, 1 + NCH)
                for l in range(DEPTH):
                    sp.dma_start(mod_scr[l], AR[0:2, l * N_MOD * D:(l + 1) * N_MOD * D]).then_inc(mod_stored, 16)
                sp.wait_ge(mod_stored, 32)
                sp.wait_ge(mt_out, 1 + 16 * NCH)
                sp.wait_ge(mout_out, 1 + 16 * NCH)
                sp.wait_ge(k_out, 1 + N_K * NCH)
                sp.wait_ge(a8_out, 16)

            def pool_():
                g.memset(ZERO, 0.0).then_inc(zero_done, 1)

            def act_():
                a.wait_ge(par_in, 112)
                a.activation(STEP[:, 0], LOGS[:, 0], ACT.Exp).then_inc(lr_done, 1)
                a.wait_ge(e_done, 1)
                a.activation(MAG[:, 0], E[:, 0], ACT.Exp).then_inc(mag_done, 1)
                a.wait_ge(th_done, 1)
                a.activation(SN[:, 0], RED[:, 0], ACT.Sin).then_inc(sin_done, 1)
                a.wait_ge(th_done, 2)
                a.activation(CS_[:, 0], X1[:, 0], ACT.Sin).then_inc(sin_done, 1)
                with a.Fori(0, NCH) as c:
                    a.wait_ge(ev_added, 1 + c)
                    for j in range(PER):
                        s, n = slot_use(c, j)
                        a.wait_ge(w_used[s], n + 2)
                        a.copy(EV[:, j * COLS:(j + 1) * COLS], PS[0:2, 6 + j % 2, 0:COLS]).then_inc(ev_saved, 1)
                    a.wait_ge(mt_sums, 1 + c + 1)
                    a.wait_ge(mt_out, 1 + c * 16)
                    a.copy(MT.rearrange("p (b g) x -> p b (g x)", b=4), PS[:, 0:4, :]).then_inc(mt_saved, 1)
                    a.wait_ge(k_sums, 1 + c + 1)
                    a.wait_ge(k_out, 1 + c * N_K)
                    for d in range(2):
                        a.copy(KS[:, :, d, :], PS[:, 4 + d, 0:P].rearrange("p (g x) -> p g x", g=CG)).then_inc(k_saved, 1)

            def dve_():
                L = lambda ins: dve.link(v, ins)
                tt = lambda o, x, y, op: L(v.tensor_tensor(o, x, y, op))
                ts = lambda o, x, s1, s2, op0, op1=ALU.bypass: L(v.tensor_scalar(o, x, s1, s2, op0, op1) if s2 is not None else v.tensor_scalar(o, x, s1, None, op0))
                stt = lambda o, x, s, y, op0, op1: L(v.scalar_tensor_tensor(o, x, s, y, op0, op1))
                v.wait_ge(par_in, 112)
                v.wait_ge(lr_done, 1)
                v.tensor_tensor(E, LR, STEP, ALU.mult).then_inc(e_done, 1)
                tt(TH, LI, STEP, ALU.mult)
                ts(K, TH, 1.0 / TWO_PI, ROUND, ALU.mult, ALU.add)
                ts(K, K, -ROUND, None, ALU.add)
                stt(RED, K, -PI_A, TH, ALU.mult, ALU.add)
                stt(RED, K, -PI_B, RED, ALU.mult, ALU.add)
                stt(RED, K, -PI_C, RED, ALU.mult, ALU.add)
                ts(RED, RED, PI_F, -PI_F, ALU.min, ALU.max)
                ts(X1, RED, math.pi / 2, None, ALU.add)
                v.memset(SM[:, 502:503], 0.0).then_inc(th_done, 1)
                ts(X2, X1, PI_F, None, ALU.is_gt)
                stt(X1, X2, -TWO_PI, X1, ALU.mult, ALU.add)
                ts(X1, X1, PI_F, -PI_F, ALU.min, ALU.max)
                v.memset(SM[:, 502:503], 0.0).then_inc(th_done, 1)
                v.wait_ge(mag_done, 1)
                v.wait_ge(sin_done, 2)
                tt(A_R, MAG, CS_, ALU.mult)
                tt(A_I, MAG, SN, ALU.mult)
                tt(DEN, LR, LR, ALU.mult)
                tt(X1, LI, LI, ALU.mult)
                tt(DEN, DEN, X1, ALU.add)
                L(v.reciprocal(DEN, DEN))
                ts(K, A_R, -1.0, None, ALU.add)
                tt(X1, K, LR, ALU.mult)
                tt(X2, A_I, LI, ALU.mult)
                tt(X1, X1, X2, ALU.add)
                tt(CO_R, X1, DEN, ALU.mult)
                tt(X1, A_I, LR, ALU.mult)
                tt(X2, K, LI, ALU.mult)
                tt(X1, X1, X2, ALU.subtract)
                tt(CO_I, X1, DEN, ALU.mult)

                def over_c(x):
                    return x[:, 0, :].unsqueeze(2).to_broadcast([P, G_, GDIM])

                def cmul(o_r, o_i, xr_, xi_, yr, yi, t1, t2):
                    v.tensor_tensor(t1, xr_, yr, ALU.mult)
                    tt(t2, xi_, yi, ALU.mult)
                    tt(o_r, t1, t2, ALU.subtract)
                    v.tensor_tensor(t1, xr_, yi, ALU.mult)
                    tt(t2, xi_, yr, ALU.mult)
                    tt(o_i, t1, t2, ALU.add)

                cmul(BBR, BBI, over_c(CO_R), over_c(CO_I), BR, BI, T1, T2)
                L(v.memset(PR[:, 0], 1.0))
                L(v.memset(PI[:, 0], 0.0))
                L(v.tensor_copy(PR[:, 1], A_R[:, 0]))
                L(v.tensor_copy(PI[:, 1], A_I[:, 0]))
                for n in range(2, T8 + 1):
                    cmul(PR[:, n], PI[:, n], PR[:, n - 1], PI[:, n - 1], A_R[:, 0], A_I[:, 0], X1[:, 0], X2[:, 0])
                for src, i_, o_ in ((PR, INR, OUTR), (PI, INI, OUTI)):
                    v.tensor_copy(i_[0:64], src[0:64, T8 - 1::-1, :])
                    v.tensor_copy(o_[0:64], src[0:64, T8:0:-1, :])
                    v.tensor_copy(i_[64:P], src[64:P, 0:T8, :])
                    L(v.tensor_copy(o_[64:P], src[64:P, 1:T8 + 1, :]))
                for r in range(2):
                    L(v.tensor_copy(A8R[:, r, :], PR[:, T8]))
                L(v.tensor_copy(A8S[:, 1, :], PI[:, T8]))
                v.tensor_scalar(A8S[:, 0, :], PI[:, T8], -1.0, None, ALU.mult).then_inc(a8_done, 1)
                shape = [P, CG, T8, GDIM]

                def by_step(x, c):
                    return x[:, :, ds(c * CG, CG)].rearrange("p s g -> p g s").unsqueeze(3).to_broadcast(shape)

                def by_group(x, c):
                    return x[:, ds(c * CG, CG), :].unsqueeze(2).to_broadcast(shape)

                def tile(x):
                    return x.rearrange("p g (s c) -> p g s c", s=T8)

                t1, t2 = (x.rearrange("p (g s) c -> p g s c", g=CG) for x in (T1, T2))
                v.wait_ge(zero_out, 32)
                v.wait_ge(bias_in, 32)
                with v.Fori(0, NCH) as c:
                    dve.enter(c, 10)
                    v.wait_ge(k_sums, 1 + c)
                    v.wait_ge(mt_sums, 1 + c)
                    i_r, i_i, b_r, b_i = by_step(INR, c), by_step(INI, c), by_group(BBR, c), by_group(BBI, c)
                    cmul(tile(MIN[:, 0]), tile(MIN[:, 1]), i_r, i_i, b_r, b_i, t1, t2)
                    L(v.tensor_copy(CST[:, 0], CR[:, ds(c * CG, CG), :]))
                    v.tensor_scalar(CST[:, 1], CI[:, ds(c * CG, CG), :], -1.0, None, ALU.mult).then_inc(min_done, 1)
                    v.wait_ge(mout_out, 1 + c * 16)
                    o_r, o_i, c_r, c_i = by_step(OUTR, c), by_step(OUTI, c), by_group(CR, c), by_group(CI, c)
                    v.tensor_tensor(t1, o_r, c_r, ALU.mult)
                    tt(t2, o_i, c_i, ALU.mult)
                    tt(tile(MOUT[:, 0]), t1, t2, ALU.subtract)
                    v.tensor_scalar(t1, c_i, -1.0, None, ALU.mult)
                    tt(t2, o_i, c_r, ALU.mult)
                    tt(t1, t1, o_r, ALU.mult)
                    tt(tile(MOUT[:, 1]), t1, t2, ALU.subtract)
                    v.memset(SM[:, 502:503], 0.0).then_inc(mout_done, 1)
                    v.wait_ge(ev_saved, c * PER + (PER + 2))
                    rows_ = AR[0:2, ds(c * WIDE, WIDE)]
                    v.tensor_tensor(rows_, rows_, EV, ALU.add).then_inc(ev_added, 1)
                    dve.leave(NCH)

            def pe_():
                pe.wait_ge(cs_done, 1)
                with pe.Fori(0, NCH) as c:
                    for j in range(PER):
                        s, n = slot_use(c, j)
                        pe.wait_ge(w_full[s], (n + 1) * 16)
                        pe.wait_ge(ev_saved, c * PER + (j + 1))
                        for k in range(KT):
                            mm = pe.matmul(PS[0:2, 6 + j % 2, 0:COLS], CS[:, k, :], W[:, s, k * COLS:(k + 1) * COLS],
                                           start=(k == 0), stop=(k == KT - 1))
                        mm.then_inc(w_used[s], 1)
                    pe.wait_ge(min_done, c + 1)
                    pe.wait_ge(mt_saved, 1 + c)
                    for i in range(CG):
                        for r in range(2):
                            b = i * 2 + r
                            mm = pe.transpose(PS[:, b // 4, (b % 4) * P:(b % 4 + 1) * P], MIN[:, r, i, :], IDENT)
                    mm.then_inc(mt_sums, 1)
                    pe.wait_ge(k_saved, 1 + c * 2)
                    for i in range(CG):
                        for d in range(2):
                            half = slice(d * STATE, (d + 1) * STATE)
                            for r in range(2):
                                mm = pe.matmul(PS[:, 4 + d, i * GDIM:(i + 1) * GDIM], MIN[half, r, i, :], CST[half, r, i, :],
                                               start=(r == 0), stop=(r == 1))
                    mm.then_inc(k_sums, 1)

            return Stage(sync=sync, pe=pe_, act=act_, dve=dve_, pool=pool_)

        def ssm(ht_at):
            V = view(6144, NBLK, 2, GROUPS)
            UTL = view(14336, GROUPS, LATB)
            SLM = [view(at, CG, 2, P) for at in (16384, 18432)]
            UC = [view(at, T8, P)[0:NBLK] for at in (22528, 23552)]
            UCG = [view(at, CG, P)[0:NBLK] for at in (27136, 20480)]
            UTST = [view(at, CG, NBLK) for at in (25088, 24576)]
            SLO = [view(at, 2, CG, P) for at in (18432, 16384)]
            DF, DB = [view(at, CG, P) for at in (20480, 22528)], [view(at, CG, P) for at in (21504, 27136)]
            YC = [view(at, T8, P)[0:LATB] for at in (23552, 28416)]
            HST = [view(at, 2, CG, LATB) for at in (24576, 25088)]
            UTLS = [view(at, CG, LATB) for at in (25600, 28160)]
            TA, TB_ = view(25856, 2, GROUPS), view(25984, 2, GROUPS)
            Y = view(6144, 2, D)
            DROW = view(8192, D)
            VAL = view(12288, 2, D)
            TMP = view(26112, 2, COLS)
            SG = view(26624, 2, COLS)

            def two(name):
                return [sem(f"ssm_{name}{u}") for u in range(2)]

            u_out, uc_cut, scanned, step_in = (sem("ssm_" + n) for n in ("u_out", "uc_cut", "scanned", "step_in"))
            scan = primed("ssm_scan", 6)
            slm_in, uc_in, slo_in, df_in, db_in = (two(n) for n in ("slm_in", "uc_in", "slo_in", "df_in", "db_in"))
            y_out = [primed(f"ssm_y_out{u}") for u in range(2)]
            ut_sums, ut_saved, utl_saved, v_sums, vf_saved, vb_saved, y_sums, y_saved = (primed("ssm_" + n, 2) for n in
                ("ut_sums", "ut_saved", "utl_saved", "v_sums", "vf_saved", "vb_saved", "y_sums", "y_saved"))
            d_sum, hst_done, y_in = (sem("ssm_" + n) for n in ("d_sum", "hst", "y_in"))
            y_done, z_done, sg_done = sem("ssm_y"), sem("ssm_z"), sem("ssm_gate")
            xr = x_ready.total

            def parts(u):
                return PS[:, 5 - 5 * u:7 - 5 * u, :].rearrange("p b (g r k) -> p (b g) r k", g=4, r=2)

            def to_h(blk, tb, sums):
                return a.copy(H[:, tb, ds(blk * COLS, COLS)], sums)

            in_sync, in_pe, in_take, in_end = linear(t["ssm_w_in"], 4, 4, lambda k, tb: HT[:, k, tb * P:(tb + 1) * P], to_h, ht_at=ht_at)
            turn_pe, turn_act, turn_end = turn(lambda tb: VAL[:, tb, :], range(2), KT, z_done, lambda i: i + 1,
                                               lambda q, i: HT[:, 4 * q:4 * q + 4, i * P:(i + 1) * P])
            NW = 8
            uw = take([NW // 4] * SLOTS)
            st = sums_taken.plan(NW * 2)
            N_D = T8 * 16
            ROUNDS = NCH // 2

            def lag_rows(eng, c, u, d, dst, full):
                for s in range(T8):
                    at = d * LAGS + s * GDIM
                    eng.dma_start(dst[u][s * GDIM:(s + 1) * GDIM], lag_scr[:, ds(c * CG, CG), at:at + P]).then_inc(full[u], 16)

            def pool_():
                g.wait_ge(v_sums, 2 + NCH)
                with g.Fori(0, ROUNDS) as r:
                    for u in range(2):
                        g.wait_ge(y_sums, r * 2 + (1 + u))
                        apart(g)
                        lag_rows(g, r * 2 + u, u, 1, DB, db_in)

            def sync():
                in_sync()
                sp.wait_ge(sums_taken.sem, in_end)
                sp.dma_start(SM[:, 64:64 + 4 * GROUPS], step_scr).then_inc(step_in, 16)
                for tb, at in ((2, 0), (3, P), (0, 2 * P), (1, 3 * P)):
                    sp.dma_start(u_scr[at:at + P, :], H[:, tb, :]).then_inc(u_out, 16)
                sp.wait_ge(u_out, 64)
                u_steps = u_scr.rearrange("(k s) d -> k s d", s=T8)
                with sp.Fori(0, ROUNDS) as r:
                    for u in range(2):
                        c = r * 2 + u
                        sp.wait_ge(v_sums, 1 + c)
                        sp.dma_start(UC[u], u_steps[:, :, ds(c * P, P)]).then_inc(uc_in[u], 16)
                        sp.dma_start(SLM[u].rearrange("p g r x -> p (g r x)"), wblock(min_scr, c)).then_inc(slm_in[u], 16)
                sp.wait_ge(v_sums, 2 + NCH)

                def load_out(c, u):
                    sp.wait_ge(y_sums, 1 + c)
                    sp.dma_start(SLO[u].rearrange("p r g x -> p (r g x)"), wblock(mout_scr, c)).then_inc(slo_in[u], 16)
                    lag_rows(sp, c, u, 0, DF, df_in)

                def store_y(c, r, u):
                    sp.wait_ge(y_saved, 2 + c + 1)
                    sp.dma_start(y_scr.rearrange("(k s) d -> k s d", s=T8)[:, :, ds(c * P, P)], YC[u]).then_inc(y_out[u], 16)

                load_out(0, 0)
                with sp.Fori(0, ROUNDS - 1) as r:
                    for u in range(2):
                        load_out(r * 2 + (u + 1), 1 - u)
                        store_y(r * 2 + u, r, u)
                load_out(NCH - 1, 1)
                store_y(NCH - 2, ROUNDS - 1, 0)
                store_y(NCH - 1, ROUNDS - 1, 1)
                for u in range(2):
                    sp.wait_ge(y_out[u], 1 + 16 * ROUNDS)
                sp.dma_start(Y, y_scr.rearrange("(t p) d -> p t d", p=P)).then_inc(y_in, 16)
                sp.dma_start(DROW, row(t["ssm_d"])).then_inc(y_in, 16)
                with sp.Fori(0, NW // 4) as r:
                    for s in range(SLOTS):
                        load(s, r + uw[s], wblock(t["ssm_w_out"], r * 4 + s))

            def pe_():
                in_pe()
                def turn_inputs(c, u):
                    pe.wait_ge(uc_cut, c + 1)
                    pe.wait_ge(ut_saved, 1 + c)
                    apart(pe)
                    for i in range(CG):
                        mm = pe.transpose(PS[:, 4 + 3 * u, i * NBLK:(i + 1) * NBLK], UCG[u][:, i, :], IDENT[0:NBLK, 0:NBLK])
                    mm.then_inc(ut_sums, 1)

                def states(c, r, u):
                    pe.wait_ge(slm_in[u], r * 16 + 16)
                    pe.wait_ge(ut_saved, 2 + c + 1)
                    pe.wait_ge(vf_saved, 1 + c)
                    pe.wait_ge(vb_saved, 1 + c)
                    for i in range(CG):
                        for x in range(2):
                            mm = pe.matmul(PS[:, 5 - 5 * u + i // 4, ((i % 4) * 2 + x) * NBLK:((i % 4) * 2 + x + 1) * NBLK],
                                           SLM[u][:, i, x, :], UTST[u][:, i, :], start=True, stop=True)
                    mm.then_inc(v_sums, 1)

                def state_round(r, more):
                    for u in range(2):
                        states(r * 2 + u, r, u)
                        if more or u == 0:
                            turn_inputs(r * 2 + (u + 1), 1 - u)

                turn_inputs(0, 0)
                with pe.Fori(0, ROUNDS - 1) as r:
                    state_round(r, True)
                state_round(ROUNDS - 1, False)
                with pe.Fori(0, ROUNDS) as r:
                    for u in range(2):
                        c = r * 2 + u
                        pe.wait_ge(slo_in[u], r * 16 + 16)
                        pe.wait_ge(d_sum, c + 1)
                        pe.wait_ge(hst_done, c * 3 + 3)
                        pe.wait_ge(y_saved, 1 + c)
                        for i in range(CG):
                            out = PS[0:LATB, 2 * u + i // 4, (i % 4) * P:(i % 4 + 1) * P]
                            pe.matmul(out, UTLS[u][:, i, :], DF[u][:, i, :], start=True, stop=False)
                            pe.matmul(out, HST[u][:, 0, i, :], SLO[u][:, 0, i, :], start=False, stop=False)
                            mm = pe.matmul(out, HST[u][:, 1, i, :], SLO[u][:, 1, i, :], start=False, stop=True)
                        mm.then_inc(y_sums, 1)
                turn_pe()
                pe.wait_ge(n_ht.sem, turn_end)
                pe.wait_ge(y_saved, 2 + NCH)
                with pe.Fori(0, NW // 4) as r:
                    for s in range(4):
                        pe.wait_ge(w_full[s], (r + uw[s] + 1) * 16)
                        pe.wait_ge(sums_taken.sem, r * 8 + (st + (s // 2 - 1) * 4))
                        for tb in range(2):
                            for k in range(KT):
                                mm = pe.matmul(PS[:, s, tb * COLS:(tb + 1) * COLS], HT[:, k, tb * P:(tb + 1) * P],
                                               W[:, s, k * COLS:(k + 1) * COLS], start=(k == 0), stop=(k == KT - 1))
                        mm.then_inc(w_used[s], 1)

            def act_():
                in_take(a)
                def cut_inputs(c, r, u):
                    a.wait_ge(uc_in[u], r * 16 + 16)
                    a.wait_ge(ut_sums, 1 + c)
                    a.copy(UCG[u].rearrange("k g (s c) -> k g s c", s=T8), UC[u].rearrange("k s (g c) -> k g s c", g=CG)).then_inc(uc_cut, 1)

                def save_round(r, more):
                    for u in range(2):
                        c = r * 2 + u
                        a.wait_ge(ut_sums, 2 + c + 1)
                        a.wait_ge(v_sums, 1 + c)
                        a.wait_ge(utl_saved, 1 + c)
                        a.copy(UTST[u], PS[:, 4 + 3 * u, :].rearrange("p (g k) -> p g k", g=CG)).then_inc(ut_saved, 1)
                        if u == 0:
                            cut_inputs(c + 1, r, 1)
                        elif more:
                            cut_inputs(c + 1, r + 1, 0)
                        a.wait_ge(v_sums, 2 + c + 1)
                        for x in range(2):
                            ins = a.copy(V[0:64, :, x, ds(c * CG, CG)].rearrange("p k g -> p g k"), parts(u)[0:64, :, x, :])
                        ins.then_inc(vf_saved, 1)

                cut_inputs(0, 0, 0)
                with a.Fori(0, ROUNDS - 1) as r:
                    save_round(r, True)
                save_round(ROUNDS - 1, False)
                a.wait_ge(utl_saved, 2 + NCH)
                a.wait_ge(scanned, 1)

                def cut_states(c, u):
                    a.wait_ge(y_sums, 1 + c)
                    a.copy(UTLS[u], UTL[:, ds(c * CG, CG), :]).then_inc(hst_done, 1)
                    first = NBLK - LATB - 1
                    fwd = V[0:64, first:NBLK - 1, :, ds(c * CG, CG)].rearrange("p k r g -> p r g k")
                    bwd = V[64:P, first:NBLK - 1, :, ds(c * CG, CG)].rearrange("p k r g -> p r g k")
                    a.copy(HST[u][0:64], fwd).then_inc(hst_done, 1)
                    a.copy(HST[u][64:P][:, :, :, ::-1], bwd).then_inc(hst_done, 1)

                def save_y(c, r, u):
                    a.wait_ge(y_sums, 2 + c + 1)
                    a.wait_ge(y_out[u], 1 + r * 16)
                    a.copy(YC[u].rearrange("k t (g x) -> k g t x", g=CG)[:, :, ::-1, :],
                           PS[0:LATB, 2 * u:2 * u + 2, :].rearrange("k b (g t x) -> k (b g) t x", g=4, t=T8)).then_inc(y_saved, 1)

                cut_states(0, 0)
                with a.Fori(0, ROUNDS - 1) as r:
                    for u in range(2):
                        cut_states(r * 2 + (u + 1), 1 - u)
                        save_y(r * 2 + u, r, u)
                cut_states(NCH - 1, 1)
                save_y(NCH - 2, ROUNDS - 1, 0)
                save_y(NCH - 1, ROUNDS - 1, 1)
                for tb in range(2):
                    a.wait_ge(y_done, tb + 1)
                    a.activation(VAL[:, tb, :], Y[:, tb, :], ACT.Gelu_apprx_tanh).then_inc(z_done, 1)
                turn_act()
                with a.Fori(0, NW // 4) as r:
                    for s in (1, 3):
                        a.wait_ge(w_used[s], r + uw[s] + 2)
                        a.wait_ge(sums_taken.sem, r * 8 + (st + (s // 2) * 4))
                        a.activation(SG, PS[:, s, :].rearrange("p (t c) -> p t c", t=2), ACT.Sigmoid).then_inc(sg_done, 1)

            def dve_():
                with v.Fori(0, ROUNDS) as r:
                    for u in range(2):
                        c = r * 2 + u
                        v.wait_ge(ut_saved, 2 + c + 1)
                        v.tensor_copy(UTL[:, ds(c * CG, CG), :], UTST[u][:, :, NBLK - LATB:NBLK]).then_inc(utl_saved, 1)
                        v.wait_ge(v_sums, 2 + c + 1)
                        for lo, hi in ((0, NBLK - LATB), (NBLK - LATB, NBLK)):
                            for x in range(2):
                                last = v.tensor_copy(V[64:P, lo:hi, x, ds(c * CG, CG)].rearrange("p k g -> p g k"),
                                                     parts(u)[64:P, :, x, lo:hi][:, :, ::-1])
                        last.then_inc(vb_saved, 1)
                v.wait_ge(vf_saved, 2 + NCH)
                v.wait_ge(vb_saved, 2 + NCH)
                v.wait_ge(step_in, 16)
                halves = [slice(h * (GROUPS // 2), (h + 1) * (GROUPS // 2)) for h in range(2)]
                with v.Fori(1, NBLK - 1) as j:
                    last, cur = (V[:, ds(j - o, 1)].rearrange("p a r g -> p (a r) g") for o in (1, 0))
                    at = (j - 1) * 6
                    for h, gr in enumerate(halves):
                        v.wait_ge(scan, at + (h + 5))
                        v.tensor_tensor(TA[:, :, gr], A8R[:, :, gr], last[:, :, gr], ALU.mult)
                        v.tensor_tensor(TB_[:, ::-1, gr], A8S[:, ::-1, gr], last[:, :, gr], ALU.mult).then_inc(scan, 1)
                    for h, gr in enumerate(halves):
                        v.wait_ge(scan, at + (h + 7))
                        v.tensor_tensor(TA[:, :, gr], TA[:, :, gr], TB_[:, :, gr], ALU.add).then_inc(scan, 1)
                    for h, gr in enumerate(halves):
                        v.wait_ge(scan, at + (h + 9))
                        v.tensor_tensor(cur[:, :, gr], cur[:, :, gr], TA[:, :, gr], ALU.add).then_inc(scan, 1)
                v.wait_ge(scan, 6 * (NBLK - 1))
                v.memset(SM[:, 501:502], 0.0).then_inc(scanned, 1)
                with v.Fori(0, ROUNDS) as r:
                    for u in range(2):
                        v.wait_ge(df_in[u], r * N_D + N_D)
                        v.wait_ge(db_in[u], r * N_D + N_D)
                        v.tensor_tensor(DF[u], DF[u], DB[u], ALU.add).then_inc(d_sum, 1)
                v.wait_ge(y_in, 32)
                for tb in range(2):
                    dve.link(v, v.tensor_tensor(H[:, tb, :], H[:, tb, :], DROW, ALU.mult))
                    v.tensor_tensor(Y[:, tb, :], Y[:, tb, :], H[:, tb, :], ALU.add).then_inc(y_done, 1)
                with v.Fori(0, NW // 4) as r:
                    dve.enter(r, 8)
                    for s in (1, 3):
                        v.wait_ge(sg_done, r * 2 + (s // 2 + 1))
                        v.wait_ge(w_used[s - 1], r + uw[s - 1] + 2)
                        for tb in range(2):
                            col = r * (2 * COLS) + (s // 2) * COLS
                            dst = XA[:, tb, ds(col, COLS)]
                            x = TMP[:, tb, :]
                            dve.link(v, v.tensor_tensor(x, PS[:, s - 1, tb * COLS:(tb + 1) * COLS], SG[:, tb, :], ALU.mult))
                            dve.link(v, v.tensor_tensor(x, x, AR[:, ds(col + 2 * D, COLS)], ALU.mult))
                            v.tensor_tensor(dst, dst, x, ALU.add).then_inc(sums_taken.sem, 2)
                    dve.leave(NW // 4)
                mark()

            mark = mark_x()
            return Stage(sync=sync, pe=pe_, act=act_, dve=dve_, pool=pool_)

        PIECES = ((0, P), (P, 3 * P))
        SCORES = 3 * P

        def fox(ht_at):
            O = view(0, 2, D)
            VT = view(2048, 2, D)
            QP, KP = view(4096, 2, SEQ), view(4608, 2, SEQ)
            LT = view(5120, 2, SCORES)
            SB = view(5888, 2, SCORES)
            PB = view(6656, 2, SCORES)
            PTB = view(7424, 2, SCORES)
            FW = view(8192, KT, FOX_H)
            BF = view(8320, FOX_H)
            ZF, AF, LF = view(8336, 2, FOX_H), view(8368, 2, FOX_H), view(8400, 2, FOX_H)
            NM, SUMS, RS = view(8432, 4), view(8436, 4), view(8440, 4)
            TMPM = view(8444, 4)
            SUF = view(8448, 2, SEQ)
            PAIRS = FOX_H // 2
            ROUNDS = PAIRS // 2
            par_in, f_sums, f_z, f_exp, f_one, f_log = (sem("fox_" + n) for n in ("par_in", "f_sums", "f_abs", "f_exp", "f_one", "f_log"))
            lt_ready, s_sums, neg_ready, pv_sums = (sem("fox_" + n) for n in ("gates", "s_sums", "negmax", "pv_sums"))
            s_taken, exp_done, pt_sums, pt_saved, o_taken = (primed("fox_" + n) for n in ("s_taken", "exp", "turned", "pt_saved", "o_taken"))
            qk_saved, v_saved = sem("fox_qk_saved"), sem("fox_v_saved")
            uw = take([ROUNDS, ROUNDS, ROUNDS, 0])
            turn_pe, turn_act, turn_end = turn(lambda tb: O[:, tb, :], range(2), KT, o_taken, lambda i: 1 + 4 * PAIRS,
                                               lambda q, i: HT[:, 4 * q:4 * q + 4, i * P:(i + 1) * P])
            out_sync, out_pe, out_take, out_end = linear(t["fox_out"], 4, 2, lambda k, tb: HT[:, k, tb * P:(tb + 1) * P],
                                                         add_gated(None, 2, None), ht_at=turn_end)
            mark = mark_x()
            st = sums_taken.total - 8

            def sync():
                sp.wait_ge(n_ht.sem, ht_at)
                sp.sem_inc(qk_saved, 4)
                sp.dma_start(FW, t["fox_f"]).then_inc(par_in, 16)
                sp.dma_start(BF, row(t["fox_b"])).then_inc(par_in, 16)
                sp.dma_start(SUF.rearrange("p b k -> p (b k)"), t["consts"][:, C_SUF:C_SUF + 2 * SEQ]).then_inc(par_in, 16)
                with sp.Fori(0, ROUNDS) as r:
                    load(0, r + uw[0], wblock(t["fox_qk"], r * 2))
                    load(2, r + uw[2], wblock(t["fox_v"], r))
                    load(1, r + uw[1], wblock(t["fox_qk"], r * 2 + 1))
                out_sync()

            def pe_():
                def project(r, s):
                    j = r * 2 + s
                    pe.wait_ge(w_full[s], (r + uw[s] + 1) * 16)
                    pe.wait_ge(qk_saved, j * 2 + 2)
                    for part in range(2):
                        for k in range(KT):
                            mm = pe.matmul(PS[:, s, part * SEQ:(part + 1) * SEQ], W[:, s, k * COLS + part * P:k * COLS + (part + 1) * P],
                                           HT[:, k, 0:SEQ], start=(k == 0), stop=(k == KT - 1))
                    mm.then_inc(w_used[s], 1)
                    if s == 0:
                        pe.wait_ge(w_full[2], (r + uw[2] + 1) * 16)
                        pe.wait_ge(v_saved, r)
                        for tb in range(2):
                            for k in range(KT):
                                mm = pe.matmul(PS[:, 2, tb * COLS:(tb + 1) * COLS], HT[:, k, tb * P:(tb + 1) * P],
                                               W[:, 2, k * COLS:(k + 1) * COLS], start=(k == 0), stop=(k == KT - 1))
                        mm.then_inc(w_used[2], 1)

                def scores(r, s):
                    j = r * 2 + s
                    pe.wait_ge(qk_saved, j * 2 + 6)
                    pe.wait_ge(lt_ready, j * 2 + 2)
                    pe.wait_ge(s_taken, 1 + j * 2)
                    for i in range(2):
                        h = slice(i * FOX_D, (i + 1) * FOX_D)
                        first, second = PS[:, 3 + i, 0:P], PS[:, 3 + i, P:SCORES]
                        pe.matmul(first, QP[h, s, 0:P], KP[h, s, 0:P], start=True, stop=False)
                        pe.matmul(first, LT[:, i, 0:P], SUF[:, 0, 0:P], start=False, stop=True)
                        pe.matmul(second, QP[h, s, P:SEQ], KP[h, s, :], start=True, stop=False)
                        pe.matmul(second, LT[:, i, P:SEQ], SUF[:, 0, :], start=False, stop=False)
                        mm = pe.matmul(second, LT[:, i, SEQ:SCORES], SUF[:, 1, :], start=False, stop=True)
                    mm.then_inc(s_sums, 1)

                def values(r, s):
                    j = r * 2 + s
                    for i in range(2):
                        pe.wait_ge(exp_done, 1 + j * 4 + (2 * i + 2))
                        pe.wait_ge(pt_saved, 1 + j * 2)
                        for k in range(3):
                            mm = pe.transpose(PS[:, 5 + i, k * P:(k + 1) * P], PB[:, i, k * P:(k + 1) * P], IDENT)
                        mm.then_inc(pt_sums, 1)
                    pe.wait_ge(v_saved, r + 1)
                    pe.wait_ge(o_taken, 1 + j * 4)
                    for i in range(2):
                        pe.wait_ge(pt_saved, 1 + j * 2 + (i + 1))
                        vh = [VT[:, kb, ds(r * COLS + (s * 2 + i) * FOX_D, FOX_D)] for kb in range(2)]
                        outs = [PS[:, 7, (2 * i + q) * FOX_D:(2 * i + q + 1) * FOX_D] for q in range(2)]
                        pe.matmul(outs[0], PTB[:, i, 0:P], vh[0], start=True, stop=True)
                        pe.matmul(outs[1], PTB[:, i, P:SEQ], vh[0], start=True, stop=False)
                        pe.matmul(outs[1], PTB[:, i, SEQ:SCORES], vh[1], start=False, stop=True).then_inc(pv_sums, 1)

                def pe_round(r, more):
                    for s in range(2):
                        scores(r, s)
                        if s == 0:
                            project(r, 1)
                        elif more:
                            project(r + 1, 0)
                        values(r, s)

                pe.wait_ge(n_ht.sem, ht_at)
                pe.wait_ge(par_in, 48)
                pe.wait_ge(sums_taken.sem, st)
                for tb in range(2):
                    for k in range(KT):
                        mm = pe.matmul(PS[:, 7, tb * FOX_H:(tb + 1) * FOX_H], HT[:, k, tb * P:(tb + 1) * P], FW[:, k, :],
                                       start=(k == 0), stop=(k == KT - 1))
                mm.then_inc(f_sums, 1)
                project(0, 0)
                with pe.Fori(0, ROUNDS - 1) as r:
                    pe_round(r, True)
                pe_round(ROUNDS - 1, False)
                turn_pe()
                out_pe()

            def act_():
                def save(r, s):
                    a.wait_ge(w_used[s], r + uw[s] + 2)
                    a.activation(QP[:, s, :], PS[:, s, 0:SEQ], ACT.Copy, scale=FOX_D ** -0.5).then_inc(qk_saved, 1)
                    a.copy(KP[:, s, :], PS[:, s, SEQ:2 * SEQ]).then_inc(qk_saved, 1)
                    if s == 0:
                        a.wait_ge(w_used[2], r + uw[2] + 2)
                        a.copy(VT[:, :, ds(r * COLS, COLS)], PS[:, 2, :].rearrange("p (t c) -> p t c", t=2)).then_inc(v_saved, 1)

                def soft(r, s):
                    j = r * 2 + s
                    a.wait_ge(neg_ready, j + 1)
                    a.wait_ge(pt_sums, 1 + j * 2)
                    for i in range(2):
                        for q, (lo, hi) in enumerate(PIECES):
                            c = 2 * i + q
                            a.activation(PB[:, i, lo:hi], SB[:, i, lo:hi], ACT.Exp, bias=NM[:, c:c + 1],
                                         accum_out=SUMS[:, c:c + 1]).then_inc(exp_done, 1)

                def save_turned(r, s):
                    j = r * 2 + s
                    for i in range(2):
                        a.wait_ge(pt_sums, 1 + j * 2 + (i + 1))
                        a.copy(PTB[:, i, :], PS[:, 5 + i, 0:SCORES]).then_inc(pt_saved, 1)

                def act_round(r, more):
                    for s in range(2):
                        soft(r, s)
                        if s == 0:
                            save(r, 1)
                        elif more:
                            save(r + 1, 0)
                        save_turned(r, s)

                a.wait_ge(f_z, 1)
                a.activation(AF, AF, ACT.Exp, scale=-1.0).then_inc(f_exp, 1)
                a.wait_ge(f_one, 1)
                a.activation(AF, AF, ACT.Ln).then_inc(f_log, 1)
                save(0, 0)
                with a.Fori(0, ROUNDS - 1) as r:
                    act_round(r, True)
                act_round(ROUNDS - 1, False)
                turn_act()

            def dve_():
                def gates(j):
                    v.wait_ge(s_sums, j)
                    for i in range(2):
                        for lo, hi, tb in ((0, SEQ, 0), (SEQ, SCORES, 1)):
                            one = v.tensor_tensor(LT[:, i, lo:hi], TRI[:, lo:hi], LF[:, tb, ds(j * 2 + i, 1)].to_broadcast([P, hi - lo]), ALU.mult)
                        one.then_inc(lt_ready, 1)

                def pair(j, more):
                    v.wait_ge(s_sums, j + 1)
                    v.wait_ge(exp_done, 1 + j * 4)
                    for i in range(2):
                        last = v.tensor_tensor(SB[:, i, :], PS[:, 3 + i, 0:SCORES], FOX_MASK, ALU.add)
                        last.then_inc(s_taken, 1)
                    v.wait_ge(s_taken, 1 + j * 2 + 2)
                    for i in range(2):
                        for q, (lo, hi) in enumerate(PIECES):
                            last = v.tensor_reduce(TMPM[:, 2 * i + q:2 * i + q + 1], SB[:, i, lo:hi], AX_X, ALU.max)
                    dve.link(v, last)
                    v.tensor_scalar(NM, TMPM, -1.0, None, ALU.mult).then_inc(neg_ready, 1)
                    if more:
                        gates(j + 1)
                    v.wait_ge(exp_done, 1 + j * 4 + 4)
                    dve.link(v, v.reciprocal(RS, SUMS))
                    v.wait_ge(pv_sums, j * 2 + 2)
                    for i in range(2):
                        for q in range(2):
                            c = 2 * i + q
                            v.tensor_scalar(O[:, q, ds(j * P + i * FOX_D, FOX_D)], PS[:, 7, c * FOX_D:(c + 1) * FOX_D],
                                            RS[:, c:c + 1], None, ALU.mult).then_inc(o_taken, 1)

                v.wait_ge(par_in, 48)
                v.wait_ge(f_sums, 1)
                sums = PS[:, 7, 0:2 * FOX_H].rearrange("p (t h) -> p t h", t=2)
                dve.link(v, v.tensor_tensor(ZF, sums, BF.unsqueeze(1).to_broadcast([P, 2, FOX_H]), ALU.add))
                v.scalar_tensor_tensor(AF, ZF, -1.0, ZF, ALU.mult, ALU.max).then_inc(f_z, 1)
                v.wait_ge(f_exp, 1)
                v.tensor_scalar(AF, AF, 1.0, None, ALU.add).then_inc(f_one, 1)
                v.wait_ge(f_log, 1)
                dve.link(v, v.scalar_tensor_tensor(LF, ZF, 0.0, AF, ALU.min, ALU.subtract))
                gates(0)
                with v.Fori(0, PAIRS - 1) as j:
                    dve.enter(j, 2)
                    pair(j, True)
                    dve.leave(PAIRS - 1)
                pair(PAIRS - 1, False)
                out_take(v)
                mark()

            return Stage(sync=sync, pe=pe_, act=act_, dve=dve_)

        cw_in, pad_done, cw_ready, silu_done = (sem("ffn_" + n) for n in ("taps_in", "pad", "taps_cut", "silu"))
        u_saved, conv_done, gv_ready = (primed("ffn_" + n) for n in ("u_saved", "conv", "gated"))

        def ffn(layer, ht_at):
            U = view(0, 4, SEQ + 2)
            CT = view(1040, 4, SEQ)
            SIL = view(2064, 2, SEQ)
            GV = view(2576, 2, SEQ)
            CW = view(3088, FFC, 16)
            CWC = view(3088 + 16 * FFC, 4, 4)
            uw = take([FFC, FFC, FFC, 0])
            c0 = layer * FFC
            st = sums_taken.plan(4)
            xr = x_ready.total

            def sync():
                sp.wait_ge(x_ready.sem, xr)
                sp.dma_start(CW, t["ffn_conv"][layer]).then_inc(cw_in, 16)
                def load_in_blocks(c):
                    load(0, c + uw[0], wblock(t[f"ffn_gate{layer}"], c))
                    load(1, c + uw[1], wblock(t[f"ffn_val{layer}"], c))

                def load_out_block(c):
                    load(2, c + uw[2], wblock(t[f"ffn_out{layer}"], c))

                load_in_blocks(0)
                with sp.Fori(0, FFC - 1) as c:
                    load_in_blocks(c + 1)
                    load_out_block(c)
                load_out_block(FFC - 1)

            def pe_():
                def project(c):
                    for s in range(2):
                        pe.wait_ge(w_full[s], (c + uw[s] + 1) * 16)
                        pe.wait_ge(u_saved, 1 + (c + c0) * 8)
                        for m in range(2):
                            for k in range(KT):
                                mm = pe.matmul(PS[:, 4 + s, m * SEQ:(m + 1) * SEQ], W[:, s, k * COLS + m * P:k * COLS + (m + 1) * P],
                                               HT[:, k, 0:SEQ], start=(k == 0), stop=(k == KT - 1))
                        mm.then_inc(w_used[s], 1)

                def output(c, start, stop):
                    pe.wait_ge(w_full[2], (c + uw[2] + 1) * 16)
                    pe.wait_ge(gv_ready, 1 + c0 + c + 1)
                    for tb in range(2):
                        for half in range(2):
                            for k in range(2):
                                mm = pe.matmul(PS[:, tb * 2 + half, :], GV[:, k, tb * P:(tb + 1) * P],
                                               W[:, 2, k * D + half * 512:k * D + (half + 1) * 512],
                                               start=(start and k == 0), stop=(stop and k == 1))
                    mm.then_inc(w_used[2], 1)

                pe.wait_ge(n_ht.sem, ht_at)
                pe.wait_ge(sums_taken.sem, st)
                project(0)
                project(1)
                output(0, True, False)
                with pe.Fori(1, FFC - 1) as c:
                    project(c + 1)
                    output(c, False, False)
                output(FFC - 1, False, True)

            def act_():
                a.wait_ge(pad_done, layer + 1)
                with a.Fori(0, FFC) as c:
                    a.wait_ge(cw_ready, c0 + c + 1)
                    a.wait_ge(conv_done, 1 + c0 + c)
                    for s in range(2):
                        a.wait_ge(w_used[s], c + uw[s] + 2)
                        for m in range(2):
                            i = s * 2 + m
                            src = PS[:, 4 + s, m * SEQ:(m + 1) * SEQ]
                            a.copy(U[:, i, 2:SEQ + 2], src).then_inc(u_saved, 1)
                            a.activation(CT[:, i, :], src, ACT.Identity, scale=CWC[:, i, 2:3], bias=CWC[:, i, 3:4]).then_inc(u_saved, 1)
                    a.wait_ge(conv_done, 1 + c0 + c + 1)
                    a.wait_ge(gv_ready, 1 + c0 + c)
                    a.activation(SIL, CT[:, 0:2, :], ACT.Silu).then_inc(silu_done, 1)

            def dve_():
                v.wait_ge(x_ready.sem, xr)
                v.memset(U[:, :, 0:2], 0.0).then_inc(pad_done, 1)
                v.wait_ge(pad_done, layer + 1)
                v.wait_ge(cw_in, 16 * (layer + 1))
                with v.Fori(0, FFC) as c:
                    dve.enter(c, 1)
                    v.wait_ge(u_saved, 1 + (c + c0) * 8)
                    v.wait_ge(conv_done, 1 + c0 + c)
                    v.tensor_copy(CWC.rearrange("p i j -> p (i j)"), CW[:, ds(c, 1), :].rearrange("p a j -> p (a j)")).then_inc(cw_ready, 1)
                    v.wait_ge(u_saved, 1 + (c + c0) * 8 + 8)
                    for i in range(4):
                        last = v.scalar_tensor_tensor(CT[:, i, :], U[:, i, 1:SEQ + 1], CWC[:, i, 1:2], CT[:, i, :], ALU.mult, ALU.add)
                    dve.link(v, last)
                    for i in range(4):
                        last = v.scalar_tensor_tensor(CT[:, i, :], U[:, i, 0:SEQ], CWC[:, i, 0:1], CT[:, i, :], ALU.mult, ALU.add)
                    last.then_inc(conv_done, 1)
                    v.wait_ge(silu_done, c0 + c + 1)
                    v.wait_ge(w_used[2], c + (uw[2] + 1))
                    v.tensor_tensor(GV, SIL, CT[:, 2:4, :], ALU.mult).then_inc(gv_ready, 1)
                    dve.leave(FFC)
                v.wait_ge(w_used[2], uw[2] + FFC + 1)
                for tb in range(2):
                    for half in range(2):
                        dst = XA[:, tb, half * 512:(half + 1) * 512]
                        v.tensor_tensor(dst, dst, PS[:, tb * 2 + half, :], ALU.add).then_inc(sums_taken.sem, 1)
                mark()

            mark = mark_x()
            return Stage(sync=sync, pe=pe_, act=act_, dve=dve_)

        KR = view(28160, 2, SEQ)
        QD = lambda tb: H[:, tb, 0:QL]
        CKV = lambda tb: H[:, 2 + tb, 0:KVL]

        def rope(dst, src, t1, t2, done):
            x1, x2 = src[:, 0, :], src[:, 1, :]
            v.tensor_tensor(t1[:, 0, :], x1, COS, ALU.mult)
            v.tensor_tensor(t2[:, 0, :], x2, SIN, ALU.mult)
            v.tensor_tensor(t1[:, 1, :], x1, SIN, ALU.mult)
            dve.link(v, v.tensor_tensor(t2[:, 1, :], x2, COS, ALU.mult))
            v.tensor_tensor(dst[:, 0, :], t1[:, 0, :], t2[:, 0, :], ALU.subtract)
            return v.tensor_tensor(dst[:, 1, :], t1[:, 1, :], t2[:, 1, :], ALU.add).then_inc(done, 1)

        def mla_down(ht_at):
            RAW, T1, T2 = view(0, 2, SEQ), view(512, 2, SEQ), view(1024, 2, SEQ)
            n_blk = QL // COLS + 2
            uw = take([2, 1, 1, 1])
            saved, roped = sem("mla_down_saved"), sem("mla_key_roped")
            st = sums_taken.total
            x_ready.plan(1)

            def sync():
                for b in range(n_blk):
                    load(b % SLOTS, uw[b % SLOTS] + b // SLOTS, t["mla_down"][b])

            def pe_():
                pe.wait_ge(n_ht.sem, ht_at)
                pe.wait_ge(sums_taken.sem, st)
                for b in range(n_blk):
                    s = b % SLOTS
                    pe.wait_ge(w_full[s], (uw[s] + b // SLOTS + 1) * 16)
                    for half in range(2):
                        for k in range(KT):
                            if b < n_blk - 1:
                                at = half * P + (SEQ if b == n_blk - 2 else 0)
                                ops = HT[:, k, at:at + P], W[:, s, k * COLS:(k + 1) * COLS]
                            else:
                                ops = W[:, s, k * COLS + half * P:k * COLS + (half + 1) * P], HT[:, k, SEQ:2 * SEQ]
                            mm = pe.matmul(PS[:, b, half * COLS:(half + 1) * COLS], *ops, start=(k == 0), stop=(k == KT - 1))
                    mm.then_inc(w_used[s], 1)

            def act_():
                for b in range(n_blk):
                    s = b % SLOTS
                    a.wait_ge(w_used[s], uw[s] + b // SLOTS + 2)
                    sums = PS[:, b, :].rearrange("p (t c) -> p t c", t=2)
                    dst = H[:, 0:2, b * COLS:(b + 1) * COLS] if b < n_blk - 2 else H[:, 2:4, 0:KVL] if b == n_blk - 2 else RAW
                    a.copy(dst, sums).then_inc(saved, 1)

            def dve_():
                v.wait_ge(saved, n_blk)
                rope(KR, RAW, T1, T2, roped)
                v.memset(SM[:, 500:501], 0.0).then_inc(x_ready.sem, 1)

            return Stage(sync=sync, pe=pe_, act=act_, dve=dve_)

        def mla(ht_at):
            G4 = 4
            ROUNDS = MLA_H // G4
            HV = MLA_H * VD
            O = view(0, 2, HV)
            VT = view(4096, 2, HV)
            QN, KN = view(8192, G4, SEQ), view(9216, G4, SEQ)
            RAW, T1, T2, QR = view(10240, 2, SEQ), view(10752, 2, SEQ), view(11264, 2, SEQ), view(11776, 2, SEQ)
            SB, PB, PTB = view(12288, G4, SCORES), view(13824, G4, SCORES), view(15360, G4, SCORES)
            NM, SUMS, RS, TMPM = (view(16896 + 8 * i, 8) for i in range(4))
            QK, LK = QL // P, KVL // P
            OT = HT[:, :, :].rearrange("p k (a t) -> p (k a) t", a=2)
            UNITS = 7
            scale = (NOPE + ROPE) ** -0.5
            p_sums, p_taken, roped = sem("mla_p_sums"), sem("mla_p_taken"), sem("mla_q_roped")
            s_sums, s_taken, neg_ready, pt_saved, pv_sums = (sem("mla_" + n) for n in ("s_sums", "s_taken", "negmax", "pt_saved", "pv_sums"))
            exp_done, pt_sums, o_taken = (primed("mla_" + n) for n in ("exp", "turned", "o_taken"))
            uw = take([ROUNDS] * SLOTS)
            turn_pe, turn_act, turn_end = turn(lambda tb: O[:, tb, :], range(2), HV // P, o_taken, lambda i: 1 + 2 * MLA_H,
                                               lambda q, i: OT[:, 4 * q:4 * q + 4, i * P:(i + 1) * P])
            out_sync, out_pe, out_take, out_end = linear(t["mla_out"], 8, 2, lambda k, tb: OT[:, k, tb * P:(tb + 1) * P],
                                                         add_gated(None, 2, None, cols=P), ht_at=turn_end, kt=HV // P)
            mark = mark_x()
            n_h_at = n_h.total

            def sync():
                with sp.Fori(0, ROUNDS) as r:
                    for s in range(3):
                        load(s, r + uw[s], wblock(t["mla_uq"], r * 3 + s), cols=QK * COLS)
                    load(3, r + uw[3], wblock(t["mla_ukv"], r))
                out_sync()

            def pe_():
                def project(r):
                    for u in range(UNITS):
                        s = min(u, 3)
                        if u <= 3:
                            pe.wait_ge(w_full[s], (r + uw[s] + 1) * 16)
                        pe.wait_ge(p_taken, r * UNITS + max(0, u - 3))
                        bank = PS[:, 4 + u % 4, :]
                        if u < 3:
                            for m in range(2):
                                for k in range(QK):
                                    mm = pe.matmul(bank[:, m * SEQ:(m + 1) * SEQ], W[:, s, k * COLS + m * P:k * COLS + (m + 1) * P],
                                                   HT[:, k, 0:SEQ], start=(k == 0), stop=(k == QK - 1))
                            mm.then_inc(w_used[s], 1)
                        elif u < 5:
                            for m in range(2):
                                col = ((u - 3) * 2 + m) * P
                                for k in range(LK):
                                    mm = pe.matmul(bank[:, m * SEQ:(m + 1) * SEQ], W[:, s, k * 512 + col:k * 512 + col + P],
                                                   HT[:, k, SEQ:2 * SEQ], start=(k == 0), stop=(k == LK - 1))
                            mm.then_inc(p_sums, 1)
                        else:
                            tb = u - 5
                            for k in range(LK):
                                mm = pe.matmul(bank, HT[:, k, SEQ + tb * P:SEQ + (tb + 1) * P], W[:, s, 1024 + k * 512:1024 + (k + 1) * 512],
                                               start=(k == 0), stop=(k == LK - 1))
                            mm.then_inc(p_sums if tb == 0 else w_used[s], 1)

                def scores(r):
                    pe.wait_ge(p_taken, r * UNITS + 5)
                    pe.wait_ge(roped, r + 1)
                    for i in range(G4):
                        pe.wait_ge(o_taken, 1 + r * (2 * G4))
                        b = slice(i * 32, (i + 1) * 32)
                        for (lo, hi), q in zip(PIECES, (slice(0, P), slice(P, SEQ))):
                            keys = slice(0, hi - lo)
                            out = PS[:, i, lo:hi]
                            pe.matmul(out, QN[:, i, q], KN[:, i, keys], start=True, stop=False)
                            for x in range(2):
                                mm = pe.matmul(out, QR[b, x, q], KR[b, x, keys], start=False, stop=(x == 1))
                        mm.then_inc(s_sums, 1)

                def values(r):
                    for i in range(G4):
                        pe.wait_ge(exp_done, 1 + r * (2 * G4) + (2 * i + 2))
                        for k in range(3):
                            mm = pe.transpose(PS[:, i, k * P:(k + 1) * P], PB[:, i, k * P:(k + 1) * P], IDENT)
                        mm.then_inc(pt_sums, 1)
                    pe.wait_ge(p_taken, r * UNITS + UNITS)
                    for i in range(G4):
                        pe.wait_ge(pt_saved, r * G4 + (i + 1))
                        vh = [VT[:, kb, ds(r * (G4 * VD) + i * VD, VD)] for kb in range(2)]
                        pe.matmul(PS[:, i, 0:VD], PTB[:, i, 0:P], vh[0], start=True, stop=True)
                        pe.matmul(PS[:, i, VD:2 * VD], PTB[:, i, P:SEQ], vh[0], start=True, stop=False)
                        pe.matmul(PS[:, i, VD:2 * VD], PTB[:, i, SEQ:SCORES], vh[1], start=False, stop=True).then_inc(pv_sums, 1)

                pe.wait_ge(n_ht.sem, ht_at)
                project(0)
                with pe.Fori(0, ROUNDS - 1) as r:
                    scores(r)
                    project(r + 1)
                    values(r)
                scores(ROUNDS - 1)
                values(ROUNDS - 1)
                turn_pe()
                out_pe()

            def act_():
                def save(r):
                    for u in range(UNITS):
                        if u < 3:
                            a.wait_ge(w_used[u], r + (uw[u] + 2))
                        elif u < 6:
                            a.wait_ge(p_sums, r * 3 + (u - 2))
                        else:
                            a.wait_ge(w_used[3], r + (uw[3] + 2))
                        sums = PS[:, 4 + u % 4, :]
                        two = sums.rearrange("p (m t) -> p m t", m=2)
                        if u < 2:
                            one = a.activation(QN[:, 2 * u:2 * u + 2, :], two, ACT.Copy, scale=scale)
                        elif u == 2:
                            a.wait_ge(roped, r)
                            one = a.activation(RAW, two, ACT.Copy, scale=scale)
                        elif u < 5:
                            one = a.copy(KN[:, 2 * (u - 3):2 * (u - 3) + 2, :], two)
                        else:
                            one = a.copy(VT[:, u - 5, ds(r * (G4 * VD), G4 * VD)], sums)
                        one.then_inc(p_taken, 1)

                def soft(r):
                    for i in range(G4):
                        a.wait_ge(neg_ready, r * G4 + (i + 1))
                        a.wait_ge(pt_sums, 1 + r * G4)
                        for q, (lo, hi) in enumerate(PIECES):
                            c = 2 * i + q
                            a.activation(PB[:, i, lo:hi], SB[:, i, lo:hi], ACT.Exp, bias=NM[:, c:c + 1],
                                         accum_out=SUMS[:, c:c + 1]).then_inc(exp_done, 1)

                def save_turned(r):
                    for i in range(G4):
                        a.wait_ge(pt_sums, 1 + r * G4 + (i + 1))
                        a.copy(PTB[:, i, :], PS[:, i, 0:SCORES]).then_inc(pt_saved, 1)

                a.wait_ge(n_ht.sem, ht_at)
                save(0)
                with a.Fori(0, ROUNDS - 1) as r:
                    soft(r)
                    save(r + 1)
                    save_turned(r)
                soft(ROUNDS - 1)
                save_turned(ROUNDS - 1)
                turn_act()

            def dve_():
                def turn_queries(r):
                    v.wait_ge(p_taken, r * UNITS + 3)
                    v.wait_ge(s_sums, r * G4)
                    rope(QR, RAW, T1, T2, roped)

                def four(r, more):
                    v.wait_ge(exp_done, 1 + r * (2 * G4))
                    for i in range(G4):
                        v.wait_ge(s_sums, r * G4 + (i + 1))
                        v.tensor_tensor(SB[:, i, :], PS[:, i, 0:SCORES], MLA_MASK, ALU.add).then_inc(s_taken, 1)
                    for i in range(G4):
                        v.wait_ge(s_taken, r * G4 + (i + 1))
                        for q, (lo, hi) in enumerate(PIECES):
                            c = 2 * i + q
                            last = v.tensor_reduce(TMPM[:, c:c + 1], SB[:, i, lo:hi], AX_X, ALU.max)
                        dve.link(v, last)
                        v.tensor_scalar(NM[:, 2 * i:2 * i + 2], TMPM[:, 2 * i:2 * i + 2], -1.0, None, ALU.mult).then_inc(neg_ready, 1)
                    if more:
                        turn_queries(r + 1)
                    v.wait_ge(exp_done, 1 + r * (2 * G4) + 2 * G4)
                    dve.link(v, v.reciprocal(RS, SUMS))
                    for i in range(G4):
                        v.wait_ge(pv_sums, r * G4 + (i + 1))
                        for q in range(2):
                            c = 2 * i + q
                            v.tensor_scalar(O[:, q, ds(r * (G4 * VD) + i * VD, VD)], PS[:, i, q * VD:(q + 1) * VD],
                                            RS[:, c:c + 1], None, ALU.mult).then_inc(o_taken, 1)

                v.wait_ge(n_h.sem, n_h_at)
                turn_queries(0)
                with v.Fori(0, ROUNDS - 1) as r:
                    dve.enter(r, G4 + 2)
                    four(r, True)
                    dve.leave(ROUNDS - 1)
                four(ROUNDS - 1, False)
                out_take(v)
                mark()

            return Stage(sync=sync, pe=pe_, act=act_, dve=dve_)

        def mark_norm():
            x_ready.plan(1)
            at = n_h.total

            def dve_():
                v.wait_ge(n_h.sem, at)
                v.memset(SM[:, 500:501], 0.0).then_inc(x_ready.sem, 1)
            return Stage(dve=dve_)

        def write_out():
            at, out_done = n_h.total, sem("out_done")

            def sync():
                sp.wait_ge(n_h.sem, at)
                sp.dma_start(t["out"].rearrange("(t p) d -> p t d", p=P), H[:, 0:2, :]).then_inc(out_done, 16)
                sp.wait_ge(out_done, 16)
            return Stage(sync=sync)

        stages = []
        first, cs_done, CS = setup()
        stages.append(first)
        stages.append(front(cs_done, CS))
        stages.append(load_mod(0, N_MOD))
        mod1 = [(0, D)] * 2 + [(6 * D, 7 * D)] * 2
        stages.append(norm(None, range(4), gain=t["norm1_g"][0], mod=mod1))
        stages.append(chunk_mixer(n_ht.total))
        mod2 = [(3 * D, 4 * D)] * 2 + [(9 * D, 10 * D)] * 2
        stages.append(norm(None, range(4), gain=t["norm2_g"][0], mod=mod2))
        stages.append(peer(0, 4, n_ht.total))
        stages.append(load_mod(1, 2))
        stages.append(norm(None, range(4), gain=t["norm1_g"][1], mod=mod1))
        stages.append(ssm(n_ht.total))
        stages.append(norm(None, range(2), gain=t["norm2_g"][1], mod=mod2[:2]))
        stages.append(peer(1, 2, n_ht.total))
        stages.append(norm(None, range(2), gain=t["final_g"], dst=lambda tb: XA[:, tb, :], junk=lambda tb: H[:, tb, :], out_ht=False))
        stages.append(mark_norm())
        stages.append(norm(None, range(2), gain=t["fox_norm"]))
        stages.append(fox(n_ht.total))
        stages.append(norm(None, range(2), gain=t["ffn_norm"][0]))
        stages.append(ffn(0, n_ht.total))
        stages.append(norm(None, range(2), gain=t["kv_in_norm"], ht_off=SEQ))
        stages.append(norm(None, range(2), gain=t["mla_norm"]))
        stages.append(mla_down(n_ht.total))
        stages.append(norm(CKV, range(2), gain=t["kv_norm"], width=KVL, dst=CKV, junk=lambda tb: view(2048 + tb * D, KVL), ht_off=SEQ))
        stages.append(norm(QD, range(2), gain=t["q_norm"], width=QL, dst=QD, junk=lambda tb: view(2048 + tb * D, QL)))
        stages.append(mla(n_ht.total))
        stages.append(norm(None, range(2), gain=t["ffn_norm"][1]))
        stages.append(ffn(1, n_ht.total))
        stages.append(norm(None, range(2), gain=t["final_norm"], out_ht=False))
        stages.append(write_out())
        block = ctx.enter_context(nc.Block())

        @block.sync
        def _(eng):
            for s in stages:
                if s.sync:
                    s.sync()

        @block.tensor
        def _(eng):
            for s in stages:
                if s.pe:
                    s.pe()

        @block.scalar
        def _(eng):
            for s in stages:
                if s.act:
                    s.act()

        @block.vector
        def _(eng):
            for s in stages:
                if s.dve:
                    s.dve()

        @block.gpsimd
        def _(eng):
            for s in stages:
                if s.pool:
                    s.pool()


def blocks(w):
    k, n = w.shape
    return np.ascontiguousarray(w.reshape(k // P, P, n // COLS, COLS).transpose(2, 1, 0, 3).reshape(n // COLS, P, -1))


def sincos(pos, dim):
    omega = 1.0 / (10000.0 ** (np.arange(dim // 2, dtype=np.float32) / np.float32(dim // 2)))
    ang = (pos[:, None] * omega[None, :].astype(np.float32)).astype(np.float32)
    return np.concatenate([np.sin(ang), np.cos(ang)], axis=-1)


def constants():
    rows = np.repeat(np.arange(SEQ // GRID_W, dtype=np.float32), GRID_W)
    cols = np.tile(np.arange(GRID_W, dtype=np.float32), SEQ // GRID_W)
    pos = np.concatenate([sincos(rows, D // 2), sincos(cols, D // 2)], axis=-1).astype(np.float32)
    c = np.zeros((P, C_SUF + 2 * SEQ), np.float32)
    c[:, C_ID:C_ID + P] = np.eye(P)
    s, tt = np.arange(SEQ)[:, None], np.arange(SEQ)[None, :]
    tri = (s <= tt).astype(np.float32)
    c[:, C_TRI:C_TRI + SEQ], c[:, C_TRI + SEQ:C_TRI + 3 * P] = tri[:P], tri[P:, P:]
    c[:, C_SUF:C_SUF + SEQ], c[:, C_SUF + SEQ:C_SUF + 2 * SEQ] = 1 - tri[:P], 1 - tri[P:]
    q, k = np.arange(P)[:, None], np.arange(P)[None, :]
    for at, seen in ((C_FOX, k <= q), (C_MLA, k // 64 <= q // 64)):
        m = np.where(seen, 0.0, MASKED)
        c[:, at:at + P] = m
        c[:, at + 2 * P:at + 3 * P] = m
    inv = (np.float32(10000.0) ** (-np.arange(0, ROPE, 2, dtype=np.float32) / np.float32(ROPE))).astype(np.float32)
    ang = (np.arange(SEQ, dtype=np.float32)[:, None] * inv[None, :]).astype(np.float32)
    c[:, C_COS:C_COS + SEQ] = np.tile(np.cos(ang).T, (4, 1))
    c[:, C_SIN:C_SIN + SEQ] = np.tile(np.sin(ang).T, (4, 1))
    c[:, C_IOTA:C_IOTA + TOPK] = np.arange(TOPK)
    return pos, c


def layout(i):
    i = {k: np.asarray(x) for k, x in i.items()}
    pos, consts = constants()
    o = {
        "x": i["x"][0], "ctx": i["ctx"][0], "pos": pos, "consts": consts,
        "cond": np.stack([i["c"][0], i["c_ctx"]], -1).reshape(KT, P, 2).transpose(1, 0, 2),
        "ada_w": np.concatenate([blocks(w) for w in i["ada_w"]]), "ada_b": i["ada_b"], "norm1_g": i["norm1_g"], "norm2_g": i["norm2_g"], "final_g": i["final_g"],
        "cm_w_in": blocks(i["cm_w_in"][0]), "cm_w_out": blocks(i["cm_w_out"][0]),
        "cm_ws": i["cm_w_s"][0].transpose(2, 0, 1), "cm_bs": i["cm_b_s"][0].T,
        "cm_ln_g": i["cm_ln_g"][0], "cm_ln_b": i["cm_ln_b"][0],
        "peer_u": i["peer_u"].reshape(-1, D), "peer_v": i["peer_v"].reshape(-1, D),
        "peer_keys": i["peer_keys"].transpose(0, 4, 1, 2, 3).reshape(DEPTH, 2, P, HEADS, 2, KEYS).transpose(0, 2, 3, 4, 1, 5),
    }
    for l in range(DEPTH):
        o[f"peer_w_q{l}"] = blocks(i["peer_w_q"][l])
    pairs = np.stack(np.split(i["ssm_w_out"][0].reshape(D, 2 * D // COLS, COLS), 2, axis=1), 2).reshape(D, 2 * D)
    both = lambda x: x[0].transpose(0, 2, 1).reshape(P, GROUPS)
    o |= {
        "ssm_w_in": blocks(i["ssm_w_in"][0]), "ssm_w_out": blocks(pairs), "ssm_d": i["ssm_d"][0],
        "ssm_lr": both(i["ssm_lam_re"]), "ssm_li": both(i["ssm_lam_im"]),
        "ssm_ls": np.repeat(i["ssm_log_step"][0], STATE, axis=0),
    }
    for n in ("re", "im"):
        o["ssm_b" + n[0]] = i["ssm_b_" + n][0].transpose(0, 2, 1, 3).reshape(P, GROUPS, GDIM)
        o["ssm_c" + n[0]] = i["ssm_c_" + n][0].transpose(0, 3, 1, 2).reshape(P, GROUPS, GDIM)
    w, h3 = i["w_fox_in_2"][0], FOX_H * FOX_D
    q, k, v = (w[:, n * h3:(n + 1) * h3].reshape(D, FOX_H // 2, P) for n in range(3))
    down, uq = i["w_dkv_2"], i["w_uq_2"][0].reshape(QL, MLA_H // 4, 4, NOPE + ROPE)
    half = ROPE // 2
    uq = np.concatenate([uq[..., :NOPE].reshape(QL, 4, -1), uq[..., NOPE:NOPE + half].reshape(QL, 4, -1),
                         uq[..., NOPE + half:].reshape(QL, 4, -1)], -1).reshape(QL, -1)
    fours = lambda m: m.reshape(KVL // P, P, MLA_H // 4, 4 * P).transpose(2, 1, 0, 3).reshape(MLA_H // 4, P, -1)
    o |= {
        "fox_norm": i["fox_norm_2"][0], "fox_b": i["b_fox_f_2"][0], "fox_out": blocks(i["w_fox_out_2"][0]),
        "fox_qk": blocks(np.concatenate([q, k], -1).reshape(D, -1)), "fox_v": blocks(v.reshape(D, -1)),
        "fox_f": w[:, 3 * h3:].reshape(KT, P, FOX_H).transpose(1, 0, 2),
        "ffn_norm": i["ffn_norm_2"], "kv_in_norm": i["kv_in_norm_2"], "kv_norm": i["kv_norm_2"],
        "mla_norm": i["mla_norm_2"][0], "q_norm": i["q_norm_2"][0], "final_norm": i["final_norm_2"],
        "mla_down": blocks(np.concatenate([i["w_dq_2"][0], down[:, :KVL]] + [down[:, KVL:KVL + half]] * 4
                                          + [down[:, KVL + half:]] * 4, -1)),
        "mla_uq": blocks(uq), "mla_ukv": np.concatenate([fours(i["w_uk_2"]), fours(i["w_uv_2"])], -1),
        "mla_out": i["w_mla_out_2"][0].reshape(-1, P, KT, P).transpose(2, 1, 0, 3).reshape(KT, P, -1),
    }
    taps = np.concatenate([i["ffn_conv_w_2"], i["ffn_conv_b_2"][:, None]], 1)
    o["ffn_conv"] = taps.reshape(DEPTH, 4, 2, FFC, 2, P).transpose(0, 5, 3, 2, 4, 1).reshape(DEPTH, P, FFC, 16)
    for l in range(DEPTH):
        o[f"ffn_gate{l}"], o[f"ffn_val{l}"] = (blocks(m) for m in np.split(i["w_ffn_in_2"][l], 2, axis=1))
        o[f"ffn_out{l}"] = i["w_ffn_out_2"][l].reshape(FFC, 2, P, D).transpose(0, 2, 1, 3).reshape(FFC, P, -1)
    return {k: np.ascontiguousarray(x) for k, x in o.items()}


def kernel(**inputs):
    import concourse.bacc as bacc
    from concourse.bass_utils import run_bass_kernel_spmd as run

    nc = bacc.Bacc("TRN2", target_bir_lowering=False, num_devices=1)
    arrays = {f"in_{n}": x for n, x in layout(inputs).items()}
    t = {n[3:]: nc.dram_tensor(n, x.shape, mybir.dt.from_np(x.dtype), kind="ExternalInput").ap() for n, x in arrays.items()}
    t["out"] = nc.dram_tensor("out", [SEQ, D], F32, kind="ExternalOutput").ap()
    program(nc, t)
    return run(nc, [arrays], core_ids=[0]).results[0]["out"].reshape(1, SEQ, D)
```

```python
import math
from contextlib import ExitStack

import numpy as np

import concourse.bass as bass
from concourse import mybir

ALU = mybir.AluOpType
ACT = mybir.ActivationFunctionType
F32 = mybir.dt.float32
U32 = mybir.dt.uint32
F22 = mybir.dt.float32r
HIGH = 0xFFFFF000
AX_X = mybir.AxisListType.X
ds = bass.ds

P = 128
D = 1024
KT = D // P
SEQ = 256
TOK = 2 * SEQ
DEPTH = 2
N_MOD = 6
EPS = 1e-6
GRID_W = 64
BLK = 2048
COLS = BLK // KT
SLOTS = 4
HEADS, KEYS, TOPK, DHALF = 8, 128, 16, 256
EXPERTS = KEYS * KEYS
RING = 8
GROUPS, GDIM, STATE = 64, 16, 64
T8 = 8
NBLK = TOK // T8
LATB = SEQ // T8
CG = 8
FOX_H, FOX_D = 16, 64
MLA_H, NOPE, ROPE, VD = 16, 128, 64, 128
KVL, QL = 256, 768
D_FF = 2816
FFC = D_FF // 256
NEG = -3.0e38
MASKED = -1.0e30
TWO_PI = 2.0 * math.pi
PI_A = 6.28125
PI_B = float(np.float32(round((TWO_PI - PI_A) * 2.0 ** 21) / 2.0 ** 21))
PI_C = TWO_PI - PI_A - PI_B
ROUND = 1.5 * 2.0 ** 23
PI_F = 3.1415925

C_ID, C_TRI, C_FOX, C_MLA, C_COS, C_SIN, C_IOTA = 0, 128, 512, 896, 1280, 1536, 1792
C_ALL = 1808
C_SUF = C_ALL


class Signal:

    def __init__(self, sem, credit=0):
        self.sem, self.total, self.credit = sem, credit, credit

    def plan(self, n):
        base = self.total
        self.total += n
        return base


class Chain:

    def __init__(self, sem):
        self.sem, self.n, self.it, self.per = sem, 0, None, 0

    def link(self, eng, ins):
        self.n += 1
        ins.then_inc(self.sem, 1)
        eng.wait_ge(self.sem, self.n if self.it is None else self.it * self.per + self.n)

    def enter(self, it, per):
        self.it, self.per, self.start = it, per, self.n

    def leave(self, rounds):
        assert self.n - self.start == self.per, (self.n - self.start, self.per)
        self.n = self.start + self.per * rounds
        self.it = None


class Stage:
    def __init__(self, sync=None, pe=None, act=None, dve=None, pool=None):
        self.sync, self.pe, self.act, self.dve, self.pool = sync, pe, act, dve, pool


def program(nc, t):
    with ExitStack() as ctx:
        def sb(name, shape, dt=F32):
            return ctx.enter_context(nc.sbuf_tensor(name, shape, dt))

        def sem(name):
            return ctx.enter_context(nc.semaphore(name))

        primed_sems = []

        def primed(name, n=1):
            primed_sems.append((sem(name), n))
            return primed_sems[-1][0]

        def dram(name, shape):
            return nc.dram_tensor(name, shape, F32, kind="Internal").ap()

        XA = sb("XA", [P, 4, D])
        H = sb("H", [P, 4, D])
        HT = sb("HT", [P, KT, TOK])
        W = sb("W", [P, SLOTS, BLK])
        CON = sb("CON", [P, C_ALL])
        SM = sb("SM", [P, 512])
        with nc.sbuf_tensor("AR", [P, 30208], F32) as whole_arena:
            AR = whole_arena
        sb("below_parts", [P, 6144])
        WP = sb("WP", [P, 3, 2, BLK], F22)
        XP = sb("XP", [P, 2, KT, SEQ], F22)
        GVP = sb("GVP", [P, 2, 2, SEQ], F22)
        PARTS_END = 6144 + 6 * BLK + 2 * KT * SEQ + 4 * SEQ
        PS = ctx.enter_context(nc.psum_tensor("PS", [P, 8, 512], F32))

        u_scr = dram("u_scr", [TOK, D])
        y_scr = dram("y_scr", [SEQ, D])
        min_scr = dram("min_scr", [GROUPS // CG, P, CG * 2 * P])
        mout_scr = dram("mout_scr", [GROUPS // CG, P, 2 * CG * P])
        mod_scr = dram("mod_scr", [DEPTH, 2, N_MOD * D])
        step_scr = dram("step_scr", [P, 4 * GROUPS])
        LAGS = (2 * T8 - 1) * GDIM
        LAG_STEP = LAGS + (T8 - 1) * GDIM
        lag_scr = dram("lag_scr", [GDIM, GROUPS, 2 * LAG_STEP])

        def view(off, *dims):
            n = int(np.prod(dims))
            assert off + n <= 30208
            ap = AR[:, off:off + n]
            if len(dims) == 2:
                return ap.rearrange("p (a b) -> p a b", a=dims[0])
            if len(dims) == 3:
                return ap.rearrange("p (a b c) -> p a b c", a=dims[0], b=dims[1])
            if len(dims) == 4:
                return ap.rearrange("p (a b c d) -> p a b c d", a=dims[0], b=dims[1], c=dims[2])
            return ap

        IDENT = CON[:, C_ID:C_ID + P]
        TRI = CON[:, C_TRI:C_TRI + 3 * P]
        FOX_MASK, MLA_MASK = CON[:, C_FOX:C_FOX + 3 * P], CON[:, C_MLA:C_MLA + 3 * P]
        COS, SIN = CON[:, C_COS:C_COS + SEQ], CON[:, C_SIN:C_SIN + SEQ]
        IOTA = CON[:, C_IOTA:C_IOTA + TOPK]
        MODX_ALL = AR[:, 0:N_MOD * D]
        MODX = [view(r * D, D) for r in range(N_MOD)]
        MODC = [view((N_MOD + r) * D, D) for r in range(N_MOD)]
        GAIN = view(29184, D)

        w_full = [sem(f"w_full{s}") for s in range(SLOTS)]
        w_used = [sem(f"w_used{s}") for s in range(SLOTS)]
        uses = [0] * SLOTS
        sums_taken = Signal(sem("sums_taken"), 64)
        x_ready = Signal(sem("x_ready"))
        n_sumsq = Signal(sem("n_sumsq"))
        n_var = Signal(sem("n_var"))
        n_std = Signal(sem("n_std"))
        n_h = Signal(sem("n_h"))
        n_turned = Signal(sem("n_turned"))
        n_ht = Signal(sem("n_ht"))
        gain_in = Signal(sem("gain_in"))
        parted = sem("parted")
        load_in = Signal(sem("load_in"))
        dve = Chain(sem("dve_chain"))
        act = Chain(sem("act_chain"))
        pool = Chain(sem("pool_chain"))
        v, a, g, pe, sp = nc.vector, nc.scalar, nc.gpsimd, nc.tensor, nc.sync

        def take(counts):
            base = list(uses)
            for s, n in enumerate(counts):
                uses[s] += n
            return base

        def load(slot, n, src, cols=BLK):
            sp.wait_ge(w_used[slot], n + 1)
            sp.dma_start(W[:, slot, 0:cols], src).then_inc(w_full[slot], 16)

        def wblock(w, i):
            return w[ds(i, 1)].rearrange("a p c -> (a p) c")

        def apart(eng):
            eng.sem_inc(parted, 1)

        def row(ap):
            return ap.partition_broadcast(P)

        def setup():
            in_sem, cs_done = sem("inputs_in"), sem("silu_done")
            CV = SM[:, 24:24 + 2 * KT].rearrange("p (k c) -> p k c", c=2)
            CS = SM[:, 44:44 + 2 * KT].rearrange("p (k c) -> p k c", c=2)
            xr = x_ready.plan(1)

            def sync():
                for one, n in [(one, 1) for one in w_used] + primed_sems:
                    sp.sem_inc(one, n)
                for signal in (sums_taken, u_used, v_used, y_taken, q_saved, s_saved):
                    sp.sem_inc(signal.sem, signal.credit)
                sp.dma_start(CV, t["cond"]).then_inc(gain_in.sem, 16)
                sp.dma_start(CON[:, :], t["consts"][:, 0:C_ALL]).then_inc(gain_in.sem, 16)

            def load_x():
                sp.dma_start(XA[:, 0:2, :], t["x"].rearrange("(t p) d -> p t d", p=P)).then_inc(in_sem, 16)
                sp.dma_start(XA[:, 2:4, :], t["ctx"].rearrange("(t p) d -> p t d", p=P)).then_inc(in_sem, 16)
                sp.dma_start(H[:, 0:2, :], t["pos"].rearrange("(t p) d -> p t d", p=P)).then_inc(in_sem, 16)

            def act_():
                a.wait_ge(gain_in.sem, 32)
                a.activation(CS, CV, ACT.Silu).then_inc(cs_done, 1)

            def dve_():
                v.wait_ge(in_sem, 48)
                v.tensor_tensor(XA[:, 0:2, :], XA[:, 0:2, :], H[:, 0:2, :], ALU.add).then_inc(x_ready.sem, 1)

            gain_in.plan(32)
            return Stage(sync=sync, act=act_), Stage(dve=dve_), load_x, cs_done, CS

        mod_stored = sem("mod_stored")

        def load_mod(layer, rows_c):
            li = load_in.plan(32)
            xr = x_ready.total

            def sync():
                sp.wait_ge(x_ready.sem, xr)
                sp.dma_start(AR[:, 0:2 * D], row(mod_scr[layer, 0, 0:2 * D])).then_inc(load_in.sem, 16)
                sp.dma_start(AR[:, N_MOD * D:(N_MOD + rows_c) * D], row(mod_scr[layer, 1, 0:rows_c * D])).then_inc(load_in.sem, 16)

            def dve_():
                v.wait_ge(load_in.sem, li + 32)

            return Stage(sync=sync if layer else None, dve=dve_)

        NEPS = SM[:, 0:1]
        SUMSQ, VAR, STD, RSTD = (SM[:, 4 + 4 * i:8 + 4 * i] for i in range(4))

        def norm(src, tbs, gain=None, mod=None, dst=None, width=D, junk=None, out_ht=True, ht_off=0, grow=None, keep=False):
            src = src or (lambda tb: XA[:, tb, :])
            dst = dst or (lambda tb: H[:, tb, :])
            n = len(tbs)
            xr = x_ready.total
            m = 0 if keep else n
            ss, va, sd, hh = n_sumsq.plan(m), n_var.plan(m), n_std.plan(m), n_h.plan(n)
            kt = width // P
            halves = (kt + 3) // 4
            tu, ht = n_turned.plan(n * halves), n_ht.plan(n * halves)
            own_row = grow is not None
            gain_sig = load_in if own_row else gain_in
            gi = gain_sig.plan(16)
            grow = grow if own_row else GAIN[:, 0:width]

            def sync():
                sp.wait_ge(x_ready.sem, xr)
                if hh and not own_row:
                    sp.wait_ge(n_h.sem, hh)
                sp.dma_start(grow, row(gain)).then_inc(gain_sig.sem, 16)

            def act_():
                a.wait_ge(x_ready.sem, xr)
                if hh:
                    a.wait_ge(n_h.sem, hh)
                if tu:
                    a.wait_ge(n_turned.sem, tu)
                stat_tbs = [] if keep else list(enumerate(tbs))
                for i, tb in stat_tbs:
                    a.activation((junk or dst)(tb), src(tb), ACT.Square, accum_out=SUMSQ[:, i:i + 1]).then_inc(n_sumsq.sem, 1)
                for i, tb in stat_tbs:
                    a.wait_ge(n_var.sem, va + i + 1)
                    a.activation(STD[:, i:i + 1], VAR[:, i:i + 1], ACT.Sqrt).then_inc(n_std.sem, 1)
                if not out_ht:
                    return
                for i, tb in enumerate(tbs):
                    for q in range(halves):
                        m = min(4, kt - 4 * q)
                        a.wait_ge(n_turned.sem, tu + i * halves + q + 1)
                        a.copy(HT[:, 4 * q:4 * q + m, ht_off + i * P:ht_off + (i + 1) * P],
                               PS[:, 4 + (i * halves + q) % 4, 0:m * P].rearrange("p (k t) -> p k t", k=m)).then_inc(n_ht.sem, 1)

            def dve_():
                for i, tb in [] if keep else enumerate(tbs):
                    v.wait_ge(n_sumsq.sem, ss + i + 1)
                    v.tensor_scalar(VAR[:, i:i + 1], SUMSQ[:, i:i + 1], 1.0 / width, EPS, ALU.mult, ALU.add).then_inc(n_var.sem, 1)
                v.wait_ge(gain_sig.sem, gi + 16)
                if mod:
                    for shift, scale in dict.fromkeys(mod):
                        sc = AR[:, scale:scale + D]
                        dve.link(v, v.scalar_tensor_tensor(sc, sc, 1.0, grow, ALU.add, ALU.mult))
                for i, tb in enumerate(tbs):
                    if not keep:
                        v.wait_ge(n_std.sem, sd + i + 1)
                        dve.link(v, v.reciprocal(RSTD[:, i:i + 1], STD[:, i:i + 1]))
                    mul = AR[:, mod[i][1]:mod[i][1] + D] if mod else grow
                    one = v.scalar_tensor_tensor(dst(tb), src(tb), RSTD[:, i:i + 1], mul, ALU.mult, ALU.mult)
                    if mod:
                        dve.link(v, one)
                        one = v.tensor_tensor(dst(tb), dst(tb), AR[:, mod[i][0]:mod[i][0] + D], ALU.add)
                    one.then_inc(n_h.sem, 1)

            def pe_():
                if not out_ht:
                    return
                for i, tb in enumerate(tbs):
                    pe.wait_ge(n_h.sem, hh + i + 1)
                    for q in range(halves):
                        b = i * halves + q
                        if b >= 4:
                            pe.wait_ge(n_ht.sem, ht + b - 3)
                        elif ht:
                            pe.wait_ge(n_ht.sem, ht)
                        m = min(4, kt - 4 * q)
                        for k in range(m):
                            mm = pe.transpose(PS[:, 4 + b % 4, k * P:(k + 1) * P],
                                              dst(tb)[:, (4 * q + k) * P:(4 * q + k + 1) * P], IDENT)
                        mm.then_inc(n_turned.sem, 1)

            if not out_ht:
                n_turned.total -= n * halves
                n_ht.total -= n * halves
            return Stage(sync=sync, pe=pe_ , act=act_, dve=dve_)

        def turn(src, tbs, kt, ready, ready_at, dst):
            halves = kt // 4
            n = len(tbs)
            tu, ht = n_turned.plan(n * halves), n_ht.plan(n * halves)

            def pe_():
                for i, tb in enumerate(tbs):
                    pe.wait_ge(ready, ready_at(i))
                    for q in range(halves):
                        b = i * halves + q
                        pe.wait_ge(n_ht.sem, ht + max(0, b - 3))
                        for k in range(4):
                            mm = pe.transpose(PS[:, 4 + b % 4, k * P:(k + 1) * P],
                                              src(tb)[:, (4 * q + k) * P:(4 * q + k + 1) * P], IDENT)
                        mm.then_inc(n_turned.sem, 1)

            def act_():
                for i, tb in enumerate(tbs):
                    for q in range(halves):
                        b = i * halves + q
                        a.wait_ge(n_turned.sem, tu + b + 1)
                        a.copy(dst(q, i), PS[:, 4 + b % 4, :].rearrange("p (k t) -> p k t", k=4)).then_inc(n_ht.sem, 1)

            return pe_, act_, ht + n * halves

        def linear(w, nblk, ntb, lhs, evac, unroll=4, ht_at=None, kt=KT):
            uw = take([nblk // unroll if s < unroll else 0 for s in range(SLOTS)])
            st = sums_taken.plan(nblk * ntb)
            rounds = nblk // unroll
            cols = BLK // kt

            def sync():
                with sp.Fori(0, rounds) as r:
                    for s in range(unroll):
                        load(s, r + uw[s], wblock(w, r * unroll + s))

            def bank(s, tb):
                return PS[:, (s % 2) * 2 + tb // 2, (tb % 2) * cols:(tb % 2 + 1) * cols]

            def pe_():
                if ht_at is not None:
                    pe.wait_ge(n_ht.sem, ht_at)
                pe.wait_ge(sums_taken.sem, st)
                with pe.Fori(0, rounds) as r:
                    for s in range(unroll):
                        pe.wait_ge(w_full[s], (r + uw[s] + 1) * 16)
                        pe.wait_ge(sums_taken.sem, r * (unroll * ntb) + (st + (s - 1) * ntb))
                        for tb in range(ntb):
                            for k in range(kt):
                                mm = pe.matmul(bank(s, tb), lhs(k, tb), W[:, s, k * cols:(k + 1) * cols],
                                               start=(k == 0), stop=(k == kt - 1))
                        mm.then_inc(w_used[s], 1)

            def take_round(eng, r):
                for s in range(unroll):
                    eng.wait_ge(w_used[s], r + uw[s] + 2)
                    for tb in range(ntb):
                        evac(r * unroll + s, tb, bank(s, tb)).then_inc(sums_taken.sem, 1)

            def take_sums(eng, chain=None, per=0, only=None):
                if only is not None:
                    take_round(eng, only)
                    return
                with eng.Fori(0, rounds) as r:
                    if chain:
                        chain.enter(r, per)
                    take_round(eng, r)
                if chain:
                    chain.leave(rounds)

            return sync, pe_, take_sums, st + nblk * ntb

        def add_gated(gate_of, ntb, tmp, cols=COLS):
            def evac(blk, tb, sums):
                dst = XA[:, tb, ds(blk * cols, cols)]
                if gate_of is None:
                    return v.tensor_tensor(dst, dst, sums, ALU.add)
                half = tmp[:, tb % 2, :]
                dve.link(v, v.tensor_tensor(half, sums, AR[:, ds(blk * cols + gate_of(tb), cols)], ALU.mult))
                return v.tensor_tensor(dst, dst, half, ALU.add)
            return evac

        def mark_x():
            x_ready.plan(1)

            def dve_():
                v.wait_ge(sums_taken.sem, sums_now[0])
                v.memset(SM[:, 500:501], 0.0).then_inc(x_ready.sem, 1)
            sums_now = [sums_taken.total]
            return dve_

        def chunk_mixer(ht_at):
            Z = view(12288, 4, 2 * D)
            WS = view(20480, KT, P)
            BS = view(21504, KT)
            LNG, LNB = view(22528, D), view(23552, D)
            JUNK = view(24576, D)
            TMP = view(25600, 2, COLS)
            MEAN, NMEAN, VARV, STDV, RV = (SM[:, 24 + 4 * i:28 + 4 * i] for i in range(5))
            z_done = sem("z_done")
            mean_done, nmean_done, var_sum, var_done, std_done, v_done = (sem("cm_" + n) for n in
                ("sum", "negmean", "sqsum", "var", "std", "v"))
            mix_done, mixed = sem("cm_spatial"), sem("cm_mixed")
            li = load_in.plan(64)
            par_in = load_in.sem

            def gelu_out(blk, tb, sums):
                return a.activation(Z[:, tb, ds(blk * COLS, COLS)], sums, ACT.Gelu_apprx_tanh)

            in_sync, in_pe, in_take, in_end = linear(t["cm_w_in"], 8, 4, lambda k, tb: HT[:, k, tb * P:(tb + 1) * P],
                                                     gelu_out, ht_at=ht_at)
            turn_pe, turn_act, turn_end = turn(lambda tb: Z[:, tb, D:2 * D], range(4), KT, mixed, lambda i: 8 * (i + 1),
                                               lambda q, i: HT[:, 4 * q:4 * q + 4, i * P:(i + 1) * P])
            out_sync, out_pe, out_take, out_end = linear(t["cm_w_out"], 4, 4, lambda k, tb: HT[:, k, tb * P:(tb + 1) * P],
                                                         add_gated(lambda tb: (2 if tb < 2 else 8) * D, 4, TMP), ht_at=turn_end)
            mark = mark_x()
            cb_free = n_h.total

            def sync():
                sp.wait_ge(n_h.sem, cb_free)
                sp.dma_start(WS, t["cm_ws"]).then_inc(par_in, 16)
                sp.dma_start(BS, t["cm_bs"]).then_inc(par_in, 16)
                sp.dma_start(LNG, row(t["cm_ln_g"])).then_inc(par_in, 16)
                sp.dma_start(LNB, row(t["cm_ln_b"])).then_inc(par_in, 16)
                in_sync()
                out_sync()

            def act_():
                in_take(a, only=0)
                a.wait_ge(sums_taken.sem, in_end - 16)
                for tb in range(4):
                    a.activation(JUNK, Z[:, tb, 0:D], ACT.Copy, accum_out=MEAN[:, tb:tb + 1]).then_inc(mean_done, 1)
                    a.wait_ge(mean_done, tb + 1)
                for tb in range(4):
                    a.wait_ge(nmean_done, tb + 1)
                    a.activation(JUNK, Z[:, tb, 0:D], ACT.Square, bias=NMEAN[:, tb:tb + 1],
                                 accum_out=VARV[:, tb:tb + 1]).then_inc(var_sum, 1)
                    a.wait_ge(var_sum, tb + 1)
                for tb in range(4):
                    a.wait_ge(var_done, tb + 1)
                    a.activation(STDV[:, tb:tb + 1], VARV[:, tb:tb + 1], ACT.Sqrt).then_inc(std_done, 1)
                in_take(a, only=1)
                turn_act()

            def dve_():
                for tb in range(4):
                    v.wait_ge(mean_done, tb + 1)
                    v.tensor_scalar(NMEAN[:, tb:tb + 1], MEAN[:, tb:tb + 1], -1.0 / D, None, ALU.mult).then_inc(nmean_done, 1)
                for tb in range(4):
                    v.wait_ge(var_sum, tb + 1)
                    v.tensor_scalar(VARV[:, tb:tb + 1], VARV[:, tb:tb + 1], 1.0 / D, EPS, ALU.mult, ALU.add).then_inc(var_done, 1)
                v.wait_ge(par_in, li + 64)
                v.wait_ge(nmean_done, 4)
                for tb in range(4):
                    zv = Z[:, tb, 0:D]
                    v.wait_ge(std_done, tb + 1)
                    dve.link(v, v.reciprocal(RV[:, tb:tb + 1], STDV[:, tb:tb + 1]))
                    dve.link(v, v.tensor_scalar(zv, zv, NMEAN[:, tb:tb + 1], RV[:, tb:tb + 1], ALU.add, ALU.mult))
                    dve.link(v, v.tensor_tensor(zv, zv, LNG, ALU.mult))
                    v.tensor_tensor(zv, zv, LNB, ALU.add).then_inc(v_done, 1)
                v.wait_ge(sums_taken.sem, in_end)
                for tb in range(4):
                    v.wait_ge(mix_done, tb + 1)
                    for h in range(KT):
                        u = Z[:, tb, D + h * P:D + (h + 1) * P]
                        v.scalar_tensor_tensor(u, PS[:, 4 + (tb % 2) * 2 + h // 4, (h % 4) * P:(h % 4 + 1) * P], BS[:, h:h + 1], u,
                                               ALU.add, ALU.mult).then_inc(mixed, 1)
                out_take(v, dve, 16)
                mark()

            def pe_():
                in_pe()
                pe.wait_ge(par_in, li + 64)
                for tb in range(4):
                    pe.wait_ge(v_done, tb + 1)
                    if tb >= 2:
                        pe.wait_ge(mixed, 8 * (tb - 1))
                    for h in range(KT):
                        mm = pe.matmul(PS[:, 4 + (tb % 2) * 2 + h // 4, (h % 4) * P:(h % 4 + 1) * P], WS[:, h, :],
                                       Z[:, tb, h * P:(h + 1) * P], start=True, stop=True)
                    mm.then_inc(mix_done, 1)
                pe.wait_ge(mixed, 32)
                turn_pe()
                out_pe()

            return Stage(sync=sync, act=act_, dve=dve_, pe=pe_)

        u_full = [sem(f"u_full{s}") for s in range(RING)]
        v_full = [sem(f"v_full{s}") for s in range(RING)]
        u_used, v_used = Signal(sem("u_used"), RING), Signal(sem("v_used"), RING)
        keys_in, q_saved = Signal(sem("keys_in")), Signal(sem("q_saved"), 2)
        q_sums = Signal(sem("q_sums"))
        s_sums, s_saved = Signal(sem("s_sums")), Signal(sem("s_saved"), 2)
        ids_ready, top_shift, exp_done = Signal(sem("ids_ready")), Signal(sem("top_shift")), Signal(sem("exp_done"))
        gelu_done, w_ready, diag_ready = Signal(sem("gelu_done")), Signal(sem("w_ready")), Signal(sem("diag_ready"))
        y_taken = Signal(sem("y_taken"), 2)
        ring_use = [0]

        def peer(layer, ntb, ht_at):
            T = ntb * P
            UB = view(12288, RING, D)
            VB = [view(i * D, D) for i in range(4)] + [view((6 + i) * D, D) for i in range(4)]
            KEY = view(20480, HEADS, 4, KEYS)
            QT = view(24576, 4, TOK)
            S = view(26624, 4, 2, KEYS)
            CAND, CAND2 = view(27648, 2 * KEYS), view(27904, 2 * KEYS)
            S2 = view(28160, 2, KEYS)
            OH = view(28416, 2, TOPK, TOPK)
            DIAG = view(4 * D, 4, P)
            YG = view(10 * D, D)
            at = 64
            TV, IXF, TAB, K12 = (SM[:, at + 32 * i:at + 32 * (i + 1)].rearrange("p (h k) -> p h k", h=2) for i in range(4))
            TI = SM[:, 192:224].bitcast(U32).rearrange("p (h k) -> p h k", h=2)
            TABU = SM[:, 224:256].bitcast(U32).rearrange("p (h k) -> p h k", h=2)
            TS, EX = view(28928, 4, TOPK), view(28992, 4, TOPK)
            TC = SM[:, 272:288].bitcast(U32)
            NTOP, SUM = view(29056, 4), view(29060, 4)
            RSUM = SM[:, 306:307]
            EX2 = view(4 * D + 640, TOPK)
            ACTV = SM[:, 308:372].rearrange("p (t k) -> p t k", t=4)
            GELU = SM[:, 372:436].rearrange("p (t k) -> p t k", t=4)
            GATE = SM[:, 436:500].rearrange("p (t k) -> p t k", t=4)
            WGT = GELU
            IDS = view(4 * D + 512, 4, TOPK).bitcast(U32)
            IDP = view(4 * D + 576, 4, TOPK).bitcast(U32)

            n = HEADS * ntb
            rows_n = n * TOPK
            per_slot = ntb * TOPK // RING
            rb = ring_use[0]
            ring_use[0] += HEADS * per_slot
            uw = take([HEADS, HEADS, 0, 0])
            uu, vu = u_used.plan(rows_n), v_used.plan(rows_n)
            ki = keys_in.plan(16)
            q_first, qs_first = q_sums.plan(HEADS * 2 + 4), q_saved.plan(HEADS * 4 + 4)
            qm, qs = q_first + 4, qs_first + 4
            HALF = T // 2
            sm_, sv = s_sums.plan(n), s_saved.plan(n)
            ir, tsh, ed = ids_ready.plan(n), top_shift.plan(n), exp_done.plan(n)
            gd, wr, dr = gelu_done.plan(n), w_ready.plan(n), diag_ready.plan(rows_n)
            yt = y_taken.plan(n)
            hh = n_h.total
            st = sums_taken.total
            xr = x_ready.plan(1)
            H_ROWS = ntb * TOPK

            def sync():
                sp.wait_ge(n_h.sem, hh)
                sp.dma_start(KEY, t["peer_keys"][layer].rearrange("p h a b k -> p h (a b) k")).then_inc(keys_in.sem, 16)
                with sp.Fori(0, HEADS) as h:
                    for s in range(2):
                        load(s, h + uw[s], wblock(t[f"peer_w_q{layer}"], h * 2 + s))

            def queries(h):
                for j in range(4):
                    if j % 2 == 0:
                        pe.wait_ge(w_full[j // 2], (h + uw[j // 2] + 1) * 16)
                    pe.wait_ge(q_saved.sem, h * 4 + (qs + j - 1))
                    for k in range(KT):
                        mm = pe.matmul(PS[:, j % 2, 0:T], W[:, j // 2, k * COLS + (j % 2) * P:k * COLS + (j % 2 + 1) * P],
                                       HT[:, k, 0:T], start=(k == 0), stop=(k == KT - 1))
                    mm.then_inc(w_used[j // 2] if j % 2 else q_sums.sem, 1)
                pe.wait_ge(q_saved.sem, h * 4 + (qs + 4))
                key_scores(h, range(ntb))

            def first_queries():
                for part in range(2):
                    for j in range(4):
                        if part == 0 and j % 2 == 0:
                            pe.wait_ge(w_full[j // 2], (uw[j // 2] + 1) * 16)
                        pe.wait_ge(q_saved.sem, qs_first + part * 4 + j - 1)
                        for k in range(KT):
                            mm = pe.matmul(PS[:, j % 2, 0:HALF], W[:, j // 2, k * COLS + (j % 2) * P:k * COLS + (j % 2 + 1) * P],
                                           HT[:, k, part * HALF:(part + 1) * HALF], start=(k == 0), stop=(k == KT - 1))
                        mm.then_inc(w_used[j // 2] if part and j % 2 else q_sums.sem, 1)
                    pe.wait_ge(q_saved.sem, qs_first + part * 4 + 4)
                    key_scores(0, range(part * ntb // 2, (part + 1) * ntb // 2))

            def key_scores(h, tbs):
                for tb in tbs:
                    pe.wait_ge(s_saved.sem, h * ntb + (sv + tb - 1))
                    for half in range(2):
                        for c in range(2):
                            mm = pe.matmul(PS[:, 2 + tb % 2, half * KEYS:(half + 1) * KEYS],
                                           QT[:, half * 2 + c, tb * P:(tb + 1) * P],
                                           KEY[:, ds(h, 1), half * 2 + c, :].rearrange("p a k -> p (a k)"),
                                           start=(c == 0), stop=(c == 1))
                    mm.then_inc(s_sums.sem, 1)

            def pe_head(h, more):
                if more:
                    queries(h + 1)
                for tb in range(ntb):
                    pe.wait_ge(y_taken.sem, h * ntb + (yt + tb - 1))
                    for k in range(TOPK):
                        i = tb * TOPK + k
                        pe.wait_ge(diag_ready.sem, h * H_ROWS + (dr + i + 1))
                        pe.wait_ge(v_full[i % RING], (h * per_slot + (rb + i // RING + 1)) * 16)
                        for c in range(2):
                            mm = pe.matmul(PS[:, 4 + (tb % 2) * 2 + c, :], DIAG[:, k % 4, :], VB[i % RING][:, c * 512:(c + 1) * 512],
                                           start=(k == 0), stop=(k == TOPK - 1))
                        mm.then_inc(v_used.sem, 1)

            def pe_():
                pe.wait_ge(n_ht.sem, ht_at)
                pe.wait_ge(sums_taken.sem, st)
                pe.wait_ge(keys_in.sem, ki + 16)
                first_queries()
                with pe.Fori(0, HEADS - 1) as h:
                    pe_head(h, True)
                pe_head(HEADS - 1, False)

            def save_queries(h):
                for j in range(4):
                    if j % 2:
                        a.wait_ge(w_used[j // 2], h + (uw[j // 2] + 2))
                    else:
                        a.wait_ge(q_sums.sem, h * 2 + (qm + j // 2 + 1))
                    a.copy(QT[:, j, 0:T], PS[:, j % 2, 0:T]).then_inc(q_saved.sem, 1)
                save_scores(h, range(ntb))

            def save_first_queries():
                for part in range(2):
                    for j in range(4):
                        if part and j % 2:
                            a.wait_ge(w_used[j // 2], uw[j // 2] + 2)
                        else:
                            a.wait_ge(q_sums.sem, q_first + (4 + j // 2 if part else j) + 1)
                        a.copy(QT[:, j, part * HALF:(part + 1) * HALF], PS[:, j % 2, 0:HALF]).then_inc(q_saved.sem, 1)
                    save_scores(0, range(part * ntb // 2, (part + 1) * ntb // 2))

            def save_scores(h, tbs):
                for tb in tbs:
                    a.wait_ge(s_sums.sem, h * ntb + (sm_ + tb + 1))
                    a.wait_ge(ids_ready.sem, h * ntb + (ir + tb + 1 - ntb) if not isinstance(h, int) else ir)
                    a.copy(S[:, tb], PS[:, 2 + tb % 2, 0:2 * KEYS].rearrange("p (h k) -> p h k", h=2)).then_inc(s_saved.sem, 1)

            def exps(h, tb):
                a.wait_ge(top_shift.sem, h * ntb + (tsh + tb + 1))
                a.activation(EX[:, tb, :], TS[:, tb, :], ACT.Exp, bias=NTOP[:, tb:tb + 1], accum_out=SUM[:, tb:tb + 1]).then_inc(exp_done.sem, 1)

            def act_head(h, more):
                if more:
                    save_queries(h + 1)
                for tb in range(ntb):
                    a.wait_ge(u_used.sem, h * H_ROWS + (uu + (tb + 1) * TOPK))
                    a.activation(GELU[:, tb, :], ACTV[:, tb, :], ACT.Gelu_apprx_tanh).then_inc(gelu_done.sem, 1)
                    a.wait_ge(w_ready.sem, h * ntb + (wr + tb + 1))
                    for k in range(TOPK):
                        a.wait_ge(v_used.sem, h * H_ROWS + (vu + tb * TOPK + k - 3))
                        a.mul(DIAG[:, k % 4, :], IDENT, WGT[:, tb, k:k + 1]).then_inc(diag_ready.sem, 1)
                    if more:
                        exps(h + 1, tb)

            def act_():
                a.wait_ge(n_h.sem, hh)
                save_first_queries()
                for tb in range(ntb):
                    exps(0, tb)
                with a.Fori(0, HEADS - 1) as h:
                    act_head(h, True)
                act_head(HEADS - 1, False)

            def best16(vals, ix, src, scratch):
                m = len(src)
                apart(v)
                for j in range(m):
                    last = v.max(vals[j][:, 0:8], src[j])
                dve.link(v, last)
                apart(v)
                for j in range(m):
                    v.max_index(ix[j][:, 0:8], vals[j][:, 0:8], src[j])
                    last = v.match_replace(scratch[j], vals[j][:, 0:8], src[j], NEG)
                dve.link(v, last)
                apart(v)
                for j in range(m):
                    last = v.max(vals[j][:, 8:16], scratch[j])
                dve.link(v, last)
                apart(v)
                for j in range(m):
                    last = v.max_index(ix[j][:, 8:16], vals[j][:, 8:16], scratch[j])
                dve.link(v, last)

            def choose(h, tb):
                v.wait_ge(s_saved.sem, h * ntb + (sv + tb + 1))
                best16([TV[:, 0, :], TV[:, 1, :]], [TI[:, 0, :], TI[:, 1, :]], [S[:, tb, 0, :], S[:, tb, 1, :]],
                       [S2[:, 0, :], S2[:, 1, :]])
                v.tensor_copy(IXF, TI)
                dve.link(v, v.tensor_tensor(CAND.rearrange("p (a b) -> p a b", a=TOPK),
                                            TV[:, 0, :].unsqueeze(2).to_broadcast([P, TOPK, TOPK]),
                                            TV[:, 1, :].unsqueeze(1).to_broadcast([P, TOPK, TOPK]), ALU.add))
                best16([TS[:, tb, :]], [TC], [CAND], [CAND2])
                v.tensor_scalar(NTOP[:, tb:tb + 1], TS[:, tb, 0:1], -1.0, None, ALU.mult).then_inc(top_shift.sem, 1)
                v.tensor_scalar(TABU[:, 0, :], TC, 4, None, ALU.logical_shift_right)
                dve.link(v, v.tensor_scalar(TABU[:, 1, :], TC, 15, None, ALU.bitwise_and))
                dve.link(v, v.tensor_copy(TAB, TABU))
                flat = OH.rearrange("p h k j -> p (h k) j")
                dve.link(v, v.tensor_tensor(flat, TAB.rearrange("p h k -> p (h k)").unsqueeze(2).to_broadcast([P, 2 * TOPK, TOPK]),
                                            IOTA.unsqueeze(1).to_broadcast([P, 2 * TOPK, TOPK]), ALU.is_equal))
                dve.link(v, v.tensor_tensor(OH, OH, IXF.unsqueeze(2).to_broadcast([P, 2, TOPK, TOPK]), ALU.mult))
                dve.link(v, v.tensor_reduce(K12.rearrange("p h k -> p (h k)"), flat, AX_X, ALU.add))
                dve.link(v, v.scalar_tensor_tensor(EX2, K12[:, 0, :], float(KEYS), K12[:, 1, :], ALU.mult, ALU.add))
                v.tensor_scalar(IDS[:, tb, :], EX2, float(layer * EXPERTS), None, ALU.add).then_inc(ids_ready.sem, 1)

            def gates(h, tb):
                v.wait_ge(exp_done.sem, h * ntb + (ed + tb + 1))
                dve.link(v, v.reciprocal(RSUM, SUM[:, tb:tb + 1]))
                dve.link(v, v.tensor_scalar(GATE[:, tb, :], EX[:, tb, :], RSUM, None, ALU.mult))

            def add_rows(m):
                h, tb = m
                v.wait_ge(v_used.sem, h * H_ROWS + (vu + (tb + 1) * TOPK))
                gate = MODX[5] if tb < 2 else MODC[5]
                sums = PS[:, 4 + (tb % 2) * 2:6 + (tb % 2) * 2, :].rearrange("p a b -> p (a b)")
                dve.link(v, v.tensor_tensor(YG, sums, gate, ALU.mult))
                v.tensor_tensor(XA[:, tb, :], XA[:, tb, :], YG, ALU.add).then_inc(y_taken.sem, 1)

            def dve_head(h, more, before=True):
                for tb in range(ntb):
                    for k in range(TOPK):
                        i = tb * TOPK + k
                        v.wait_ge(u_full[i % RING], (h * per_slot + (rb + i // RING + 1)) * 16)
                        v.tensor_tensor_reduce(UB[:, i % RING, :], UB[:, i % RING, :], H[:, tb, :], 1.0, 0.0,
                                               ALU.mult, ALU.add, ACTV[:, tb, k:k + 1]).then_inc(u_used.sem, 1)
                    if tb:
                        add_rows((h, tb - 1))
                    elif before:
                        add_rows((h - 1, ntb - 1))
                        gates(h, ntb - 1)
                    v.wait_ge(gelu_done.sem, h * ntb + (gd + tb + 1))
                    v.tensor_tensor(WGT[:, tb, :], GELU[:, tb, :], GATE[:, tb, :], ALU.mult).then_inc(w_ready.sem, 1)
                    if more:
                        if tb:
                            gates(h + 1, tb - 1)
                        choose(h + 1, tb)

            LINKS = 15

            def dve_():
                v.wait_ge(n_h.sem, hh)
                for tb in range(ntb):
                    choose(0, tb)
                    gates(0, tb)
                dve_head(0, True, before=False)
                with v.Fori(1, HEADS - 1) as h:
                    dve.enter(h - 1, ntb * (LINKS + 2 + 1))
                    dve_head(h, True)
                    dve.leave(HEADS - 2)
                dve_head(HEADS - 1, False)
                add_rows((HEADS - 1, ntb - 1))
                v.wait_ge(y_taken.sem, yt + n)
                v.memset(SM[:, 500:501], 0.0).then_inc(x_ready.sem, 1)

            def pool_head(h):
                def fetch(tb, k, table, ring, full, used):
                    i = tb * TOPK + k
                    g.wait_ge(used[0].sem, h * H_ROWS + (used[1] + i + 1 - RING))
                    apart(g)
                    g.indirect_dma_start(out=ring[i % RING], out_offset=None, in_=table,
                                         in_offset=bass.IndirectOffsetOnAxis(ap=IDP[:, tb, k:k + 1], axis=0)).then_inc(full[i % RING], 16)

                ub = [UB[:, i, :] for i in range(RING)]
                for tb in range(ntb + 1):
                    if tb < ntb:
                        g.wait_ge(ids_ready.sem, h * ntb + (ir + tb + 1))
                        apart(g)
                        pool.link(g, g.tensor_copy(IDP[:, tb, :], IDS[:, tb, :]))
                    for k in range(TOPK):
                        if tb < ntb:
                            fetch(tb, k, t["peer_u"], ub, u_full, (u_used, uu))
                        if tb:
                            fetch(tb - 1, k, t["peer_v"], VB, v_full, (v_used, vu))

            def pool_():
                with g.Fori(0, HEADS) as h:
                    pool.enter(h, ntb)
                    pool_head(h)
                    pool.leave(HEADS)

            return Stage(sync=sync, pe=pe_, act=act_, dve=dve_, pool=pool_)

        NCH = GROUPS // CG
        A8R = SM[:, 64:192].rearrange("p (r g) -> p r g", r=2)
        A8S = SM[:, 192:320].rearrange("p (r g) -> p r g", r=2)
        mats_stored = Signal(sem("mats_stored"))

        def front(cs_done, CS, load_x):
            at = [N_MOD * DEPTH * D]

            def new(*dims):
                ap = view(at[0], *dims)
                at[0] += int(np.prod(dims))
                return ap

            small = [0]
            HF = HT[:, :, :].rearrange("p k t -> p (k t)")

            def tiny(*dims):
                n = int(np.prod(dims))
                ap = HF[:, small[0]:small[0] + n]
                small[0] += n
                return ap.rearrange("p (a b) -> p a b", a=dims[0]) if len(dims) == 2 else ap.rearrange("p (a b c) -> p a b c", a=dims[0], b=dims[1])

            G_ = GROUPS
            LR, LI, LOGS, STEP, E, MAG, TH, K, RED, SN, CS_, A_R, A_I, DEN, X1, X2, CO_R, CO_I = (tiny(1, G_) for _ in range(18))
            BR, BI, CR, CI, BBR, BBI = (new(G_, GDIM) for _ in range(6))
            T1, T2 = new(G_, GDIM), new(G_, GDIM)
            PR, PI = new(T8 + 1, G_), new(T8 + 1, G_)
            INR, INI, OUTR, OUTI = (new(T8, G_) for _ in range(4))
            MIN = new(2, CG, T8 * GDIM)
            MOUT = new(2, CG, T8 * GDIM)
            CST = tiny(2, CG, 2 * GDIM)
            MT = new(CG * 2, P)
            KS = tiny(CG, 2, GDIM)
            PER = 6
            WIDE = PER * COLS
            EV = tiny(1, WIDE)[0:2, 0, :]
            z_n = GDIM * (2 * T8 - 1) * GDIM
            ZERO = AR[0:GROUPS, 23680:23680 + z_n]
            THIRDS = 3
            uw = take([2 * NCH] * THIRDS + [0])
            ev_saved, ev_added, bias_in = sem("ada_saved"), primed("ada_added"), sem("ada_bias_in")
            a8_done, a8_out = sem("ssm_step_done"), sem("ssm_step_out")
            par_in, zero_done = sem("ssm_par_in"), sem("ssm_zero")
            lr_done, e_done, mag_done, th_done, sin_done = (sem("ssm_" + n) for n in ("lr", "step", "mag", "theta", "sin"))
            min_done, mout_done = sem("ssm_min"), sem("ssm_mout")
            mt_sums, k_sums = primed("ssm_turned"), primed("ssm_lags")
            mt_saved, k_saved = primed("ssm_min_saved"), primed("ssm_lags_saved")
            mt_out, mout_out, k_out = primed("ssm_min_out"), primed("ssm_mout_out"), primed("ssm_lags_out")
            zero_out = sem("ssm_zero_out")
            N_K = T8 * 16

            def slot_use(c, j):
                s = j % THIRDS
                return s, c * 2 + (uw[s] + j // THIRDS)

            def sync():
                sp.sem_inc(ev_saved, 2)
                for dst, name in ((LR[:, 0], "ssm_lr"), (LI[:, 0], "ssm_li"), (LOGS[:, 0], "ssm_ls"), (BR, "ssm_br"), (BI, "ssm_bi"),
                                  (CR, "ssm_cr"), (CI, "ssm_ci")):
                    sp.dma_start(dst, t[name]).then_inc(par_in, 16)
                for c in range(2):
                    sp.dma_start(AR[c:c + 1, 0:DEPTH * N_MOD * D], t["ada_b"].rearrange("(a l) n -> a (l n)", a=1)).then_inc(bias_in, 16)
                def load_blocks(c):
                    for j in range(PER):
                        s, n = slot_use(c, j)
                        load(s, n, wblock(t["ada_w"], c * PER + j))

                sp.wait_ge(zero_done, 1)
                for d in range(2):
                    sp.dma_start(lag_scr[:, :, d * LAGS:(d + 1) * LAGS].rearrange("c g l -> g c l"),
                                 ZERO.rearrange("g (c l) -> g c l", c=GDIM)).then_inc(zero_out, 16)
                def store_rows(layer, rounds):
                    sp.wait_ge(ev_added, 1 + rounds)
                    sp.dma_start(mod_scr[layer], AR[0:2, layer * N_MOD * D:(layer + 1) * N_MOD * D]).then_inc(mod_stored, 16)

                with sp.Fori(0, 1) as c:
                    load_blocks(c)
                load_x()
                with sp.Fori(1, NCH // 2 + 1) as c:
                    load_blocks(c)
                store_rows(0, NCH // 2)
                with sp.Fori(NCH // 2 + 1, NCH // 2 + 2) as c:
                    load_blocks(c)
                sp.wait_ge(mod_stored, 16)
                sp.dma_start(MODX_ALL, row(mod_scr[0, 0])).then_inc(load_in.sem, 16)
                with sp.Fori(NCH // 2 + 2, NCH) as c:
                    load_blocks(c)
                store_rows(1, NCH)
                sp.wait_ge(a8_done, 1)
                sp.dma_start(step_scr, SM[:, 64:64 + 4 * GROUPS]).then_inc(a8_out, 16)
                sp.wait_ge(mod_stored, 32)
                sp.dma_start(AR[:, N_MOD * D:2 * N_MOD * D], row(mod_scr[0, 1])).then_inc(load_in.sem, 16)
                sp.wait_ge(mt_out, 1 + 16 * NCH)
                sp.wait_ge(mout_out, 1 + 16 * NCH)
                sp.wait_ge(k_out, 1 + N_K * NCH)
                sp.wait_ge(a8_out, 16)

            def pool_():
                g.memset(ZERO, 0.0).then_inc(zero_done, 1)

            def act_():
                a.wait_ge(par_in, 112)
                a.activation(STEP[:, 0], LOGS[:, 0], ACT.Exp).then_inc(lr_done, 1)
                a.wait_ge(e_done, 1)
                a.activation(MAG[:, 0], E[:, 0], ACT.Exp).then_inc(mag_done, 1)
                a.wait_ge(th_done, 1)
                a.activation(SN[:, 0], RED[:, 0], ACT.Sin).then_inc(sin_done, 1)
                a.wait_ge(th_done, 2)
                a.activation(CS_[:, 0], X1[:, 0], ACT.Sin).then_inc(sin_done, 1)
                with a.Fori(0, NCH) as c:
                    a.wait_ge(ev_added, 1 + c)
                    for j in range(PER):
                        s, n = slot_use(c, j)
                        a.wait_ge(w_used[s], n + 2)
                        a.copy(EV[:, j * COLS:(j + 1) * COLS], PS[0:2, 6 + j % 2, 0:COLS]).then_inc(ev_saved, 1)
                    a.wait_ge(mt_sums, 1 + c + 1)
                    a.wait_ge(mt_out, 1 + c * 16)
                    a.copy(MT.rearrange("p (b g) x -> p b (g x)", b=4), PS[:, 0:4, :]).then_inc(mt_saved, 1)
                    a.wait_ge(k_sums, 1 + c + 1)
                    a.wait_ge(k_out, 1 + c * N_K)
                    a.copy(KS, PS[:, 4, 0:2 * P].rearrange("p (g d x) -> p g d x", g=CG, d=2)).then_inc(k_saved, 1)
                    a.wait_ge(mout_done, c + 1)
                    a.dma_start(wblock(mout_scr, c), MOUT.rearrange("p r g x -> p (r g x)")).then_inc(mout_out, 16)
                    a.wait_ge(mt_saved, 1 + c + 1)
                    a.dma_start(wblock(min_scr, c), MT.rearrange("p g x -> p (g x)")).then_inc(mt_out, 16)
                    a.wait_ge(k_saved, 1 + c + 1)
                    lags = lag_scr[:, ds(c * CG, CG), :].rearrange("c g (d l) -> c (g d) l", d=2)
                    for s in range(T8):
                        a.dma_start(lags[:, :, s * GDIM:(s + 1) * GDIM],
                                     KS[s * GDIM:(s + 1) * GDIM].rearrange("p g d x -> p (g d) x")).then_inc(k_out, 16)

            def dve_():
                L = lambda ins: dve.link(v, ins)
                tt = lambda o, x, y, op: L(v.tensor_tensor(o, x, y, op))
                ts = lambda o, x, s1, s2, op0, op1=ALU.bypass: L(v.tensor_scalar(o, x, s1, s2, op0, op1) if s2 is not None else v.tensor_scalar(o, x, s1, None, op0))
                stt = lambda o, x, s, y, op0, op1: L(v.scalar_tensor_tensor(o, x, s, y, op0, op1))
                v.wait_ge(par_in, 112)
                v.wait_ge(lr_done, 1)
                v.tensor_tensor(E, LR, STEP, ALU.mult).then_inc(e_done, 1)
                tt(TH, LI, STEP, ALU.mult)
                ts(K, TH, 1.0 / TWO_PI, ROUND, ALU.mult, ALU.add)
                ts(K, K, -ROUND, None, ALU.add)
                stt(RED, K, -PI_A, TH, ALU.mult, ALU.add)
                stt(RED, K, -PI_B, RED, ALU.mult, ALU.add)
                stt(RED, K, -PI_C, RED, ALU.mult, ALU.add)
                ts(RED, RED, PI_F, -PI_F, ALU.min, ALU.max)
                ts(X1, RED, math.pi / 2, None, ALU.add)
                v.memset(SM[:, 502:503], 0.0).then_inc(th_done, 1)
                ts(X2, X1, PI_F, None, ALU.is_gt)
                stt(X1, X2, -TWO_PI, X1, ALU.mult, ALU.add)
                ts(X1, X1, PI_F, -PI_F, ALU.min, ALU.max)
                v.memset(SM[:, 502:503], 0.0).then_inc(th_done, 1)
                v.wait_ge(mag_done, 1)
                v.wait_ge(sin_done, 2)
                tt(A_R, MAG, CS_, ALU.mult)
                tt(A_I, MAG, SN, ALU.mult)
                tt(DEN, LR, LR, ALU.mult)
                tt(X1, LI, LI, ALU.mult)
                tt(DEN, DEN, X1, ALU.add)
                L(v.reciprocal(DEN, DEN))
                ts(K, A_R, -1.0, None, ALU.add)
                tt(X1, K, LR, ALU.mult)
                tt(X2, A_I, LI, ALU.mult)
                tt(X1, X1, X2, ALU.add)
                tt(CO_R, X1, DEN, ALU.mult)
                tt(X1, A_I, LR, ALU.mult)
                tt(X2, K, LI, ALU.mult)
                tt(X1, X1, X2, ALU.subtract)
                tt(CO_I, X1, DEN, ALU.mult)

                def over_c(x):
                    return x[:, 0, :].unsqueeze(2).to_broadcast([P, G_, GDIM])

                def cmul(o_r, o_i, xr_, xi_, yr, yi, t1, t2):
                    v.tensor_tensor(t1, xr_, yr, ALU.mult)
                    tt(t2, xi_, yi, ALU.mult)
                    tt(o_r, t1, t2, ALU.subtract)
                    v.tensor_tensor(t1, xr_, yi, ALU.mult)
                    tt(t2, xi_, yr, ALU.mult)
                    tt(o_i, t1, t2, ALU.add)

                cmul(BBR, BBI, over_c(CO_R), over_c(CO_I), BR, BI, T1, T2)
                L(v.memset(PR[:, 0], 1.0))
                L(v.memset(PI[:, 0], 0.0))
                L(v.tensor_copy(PR[:, 1], A_R[:, 0]))
                L(v.tensor_copy(PI[:, 1], A_I[:, 0]))
                for n in range(2, T8 + 1):
                    cmul(PR[:, n], PI[:, n], PR[:, n - 1], PI[:, n - 1], A_R[:, 0], A_I[:, 0], X1[:, 0], X2[:, 0])
                for src, i_, o_ in ((PR, INR, OUTR), (PI, INI, OUTI)):
                    v.tensor_copy(i_[0:64], src[0:64, T8 - 1::-1, :])
                    v.tensor_copy(o_[0:64], src[0:64, T8:0:-1, :])
                    v.tensor_copy(i_[64:P], src[64:P, 0:T8, :])
                    L(v.tensor_copy(o_[64:P], src[64:P, 1:T8 + 1, :]))
                for r in range(2):
                    L(v.tensor_copy(A8R[:, r, :], PR[:, T8]))
                L(v.tensor_copy(A8S[:, 1, :], PI[:, T8]))
                v.tensor_scalar(A8S[:, 0, :], PI[:, T8], -1.0, None, ALU.mult).then_inc(a8_done, 1)
                shape = [P, CG, T8, GDIM]

                def by_step(x, c):
                    return x[:, :, ds(c * CG, CG)].rearrange("p s g -> p g s").unsqueeze(3).to_broadcast(shape)

                def by_group(x, c):
                    return x[:, ds(c * CG, CG), :].unsqueeze(2).to_broadcast(shape)

                def tile(x):
                    return x.rearrange("p g (s c) -> p g s c", s=T8)

                t1, t2 = (x.rearrange("p (g s) c -> p g s c", g=CG) for x in (T1, T2))
                L(v.memset(CST, 0.0))
                v.wait_ge(zero_out, 32)
                v.wait_ge(bias_in, 32)
                with v.Fori(0, NCH) as c:
                    dve.enter(c, 9)
                    v.wait_ge(k_sums, 1 + c)
                    v.wait_ge(mt_sums, 1 + c)
                    i_r, i_i, b_r, b_i = by_step(INR, c), by_step(INI, c), by_group(BBR, c), by_group(BBI, c)
                    cmul(tile(MIN[:, 0]), tile(MIN[:, 1]), i_r, i_i, b_r, b_i, t1, t2)
                    for d in range(2):
                        half, cols = slice(d * STATE, (d + 1) * STATE), slice(d * GDIM, (d + 1) * GDIM)
                        v.tensor_copy(CST[half, 0, :, cols], CR[half, ds(c * CG, CG), :])
                        last = v.tensor_scalar(CST[half, 1, :, cols], CI[half, ds(c * CG, CG), :], -1.0, None, ALU.mult)
                    last.then_inc(min_done, 1)
                    v.wait_ge(mout_out, 1 + c * 16)
                    o_r, o_i, c_r, c_i = by_step(OUTR, c), by_step(OUTI, c), by_group(CR, c), by_group(CI, c)
                    v.tensor_tensor(t1, o_r, c_r, ALU.mult)
                    tt(t2, o_i, c_i, ALU.mult)
                    tt(tile(MOUT[:, 0]), t1, t2, ALU.subtract)
                    v.tensor_scalar(t1, c_i, -1.0, None, ALU.mult)
                    tt(t2, o_i, c_r, ALU.mult)
                    tt(t1, t1, o_r, ALU.mult)
                    tt(tile(MOUT[:, 1]), t1, t2, ALU.subtract)
                    v.memset(SM[:, 502:503], 0.0).then_inc(mout_done, 1)
                    v.wait_ge(ev_saved, c * PER + (PER + 2))
                    rows_ = AR[0:2, ds(c * WIDE, WIDE)]
                    v.tensor_tensor(rows_, rows_, EV, ALU.add).then_inc(ev_added, 1)
                    dve.leave(NCH)

            def pe_():
                pe.wait_ge(cs_done, 1)
                with pe.Fori(0, NCH) as c:
                    for j in range(PER):
                        s, n = slot_use(c, j)
                        pe.wait_ge(w_full[s], (n + 1) * 16)
                        pe.wait_ge(ev_saved, c * PER + (j + 1))
                        for k in range(KT):
                            mm = pe.matmul(PS[0:2, 6 + j % 2, 0:COLS], CS[:, k, :], W[:, s, k * COLS:(k + 1) * COLS],
                                           start=(k == 0), stop=(k == KT - 1))
                        mm.then_inc(w_used[s], 1)
                    pe.wait_ge(min_done, c + 1)
                    pe.wait_ge(mt_saved, 1 + c)
                    for i in range(CG):
                        for r in range(2):
                            b = i * 2 + r
                            mm = pe.transpose(PS[:, b // 4, (b % 4) * P:(b % 4 + 1) * P], MIN[:, r, i, :], IDENT)
                    mm.then_inc(mt_sums, 1)
                    pe.wait_ge(k_saved, 1 + c)
                    for i in range(CG):
                        for r in range(2):
                            mm = pe.matmul(PS[:, 4, i * 2 * GDIM:(i + 1) * 2 * GDIM], MIN[:, r, i, :], CST[:, r, i, :],
                                           start=(r == 0), stop=(r == 1))
                    mm.then_inc(k_sums, 1)

            return Stage(sync=sync, pe=pe_, act=act_, dve=dve_, pool=pool_)

        def ssm(ht_at):
            V = view(6144, NBLK, 2, GROUPS)
            UTL = view(14336, GROUPS, LATB)
            SLM = [view(at, CG, 2, P) for at in (16384, 18432)]
            UC = [view(at, T8, P)[0:NBLK] for at in (22528, 23552)]
            UCG = [view(at, CG, P)[0:NBLK] for at in (27136, 20480)]
            UTST = [view(at, CG, NBLK) for at in (25088, 24576)]
            SLO = [view(at, 2, CG, P) for at in (18432, 16384)]
            DF, DB = [view(at, CG, P) for at in (20480, 22528)], [view(at, CG, P) for at in (21504, 27136)]
            YC = [view(at, T8, P)[0:LATB] for at in (23552, 28416)]
            HST = [view(at, 2, CG, LATB) for at in (24576, 25088)]
            UTLS = [view(at, CG, LATB) for at in (25600, 28160)]
            TA, TB_ = view(25856, 2, GROUPS), view(25984, 2, GROUPS)
            Y = view(6144, 2, D)
            DROW = view(8192, D)
            VAL = view(12288, 2, D)
            TMP = view(26112, 2, COLS)
            SG = view(26624, 2, COLS)
            STATE_ = view(26112, 2, GROUPS)

            def two(name):
                return [sem(f"ssm_{name}{u}") for u in range(2)]

            u_out, uc_cut, step_in = (sem("ssm_" + n) for n in ("u_out", "uc_cut", "step_in"))
            whole = two("whole")
            placed = primed("ssm_placed")
            scaled, turned = two("scaled"), two("turned")
            slm_in, uc_in, slo_in, df_in, db_in = (two(n) for n in ("slm_in", "uc_in", "slo_in", "df_in", "db_in"))
            y_out = [primed(f"ssm_y_out{u}") for u in range(2)]
            ut_sums, ut_saved, utl_saved, v_sums, vf_saved, vb_saved, y_sums, y_saved = (primed("ssm_" + n, 2) for n in
                ("ut_sums", "ut_saved", "utl_saved", "v_sums", "vf_saved", "vb_saved", "y_sums", "y_saved"))
            d_sum, hst_done, y_in = (sem("ssm_" + n) for n in ("d_sum", "hst", "y_in"))
            y_done, z_done, sg_done = sem("ssm_y"), sem("ssm_z"), sem("ssm_gate")
            xr = x_ready.total

            def parts(u):
                return PS[:, 5 - 5 * u:7 - 5 * u, :].rearrange("p b (g r k) -> p (b g) r k", g=4, r=2)

            def to_h(blk, tb, sums):
                return a.copy(H[:, tb, ds(blk * COLS, COLS)], sums)

            in_sync, in_pe, in_take, in_end = linear(t["ssm_w_in"], 4, 4, lambda k, tb: HT[:, k, tb * P:(tb + 1) * P], to_h, ht_at=ht_at)
            turn_pe, turn_act, turn_end = turn(lambda tb: VAL[:, tb, :], range(2), KT, z_done, lambda i: i + 1,
                                               lambda q, i: HT[:, 4 * q:4 * q + 4, i * P:(i + 1) * P])
            NW = 8
            uw = take([NW // 4] * SLOTS)
            st = sums_taken.plan(NW * 2)
            N_D = T8 * 16
            ROUNDS = NCH // 2

            def lag_rows(eng, c, u, d, dst, full):
                for s in range(T8):
                    at = d * LAGS + s * GDIM
                    eng.dma_start(dst[u][s * GDIM:(s + 1) * GDIM], lag_scr[:, ds(c * CG, CG), at:at + P]).then_inc(full[u], 16)

            def pool_():
                g.wait_ge(v_sums, 2 + NCH)
                with g.Fori(0, ROUNDS) as r:
                    for u in range(2):
                        g.wait_ge(y_sums, r * 2 + (1 + u))
                        apart(g)
                        lag_rows(g, r * 2 + u, u, 1, DB, db_in)

            def sync():
                sp.dma_start(AR[:, 2 * D:N_MOD * D], row(mod_scr[1, 0, 2 * D:N_MOD * D])).then_inc(step_in, 16)
                in_sync()
                sp.wait_ge(sums_taken.sem, in_end)
                sp.dma_start(SM[:, 64:64 + 4 * GROUPS], step_scr).then_inc(step_in, 16)
                for tb, at in ((2, 0), (3, P), (0, 2 * P), (1, 3 * P)):
                    sp.dma_start(u_scr[at:at + P, :], H[:, tb, :]).then_inc(u_out, 16)
                sp.wait_ge(u_out, 64)
                u_steps = u_scr.rearrange("(k s) d -> k s d", s=T8)
                with sp.Fori(0, ROUNDS) as r:
                    for u in range(2):
                        c = r * 2 + u
                        sp.wait_ge(v_sums, 1 + c)
                        sp.dma_start(UC[u], u_steps[:, :, ds(c * P, P)]).then_inc(uc_in[u], 16)
                        sp.dma_start(SLM[u].rearrange("p g r x -> p (g r x)"), wblock(min_scr, c)).then_inc(slm_in[u], 16)
                sp.wait_ge(v_sums, 2 + NCH)

                def load_out(c, u):
                    sp.wait_ge(y_sums, 1 + c)
                    sp.dma_start(SLO[u].rearrange("p r g x -> p (r g x)"), wblock(mout_scr, c)).then_inc(slo_in[u], 16)
                    lag_rows(sp, c, u, 0, DF, df_in)

                def store_y(c, r, u):
                    sp.wait_ge(y_saved, 2 + c + 1)
                    sp.dma_start(y_scr.rearrange("(k s) d -> k s d", s=T8)[:, :, ds(c * P, P)], YC[u]).then_inc(y_out[u], 16)

                load_out(0, 0)
                with sp.Fori(0, ROUNDS - 1) as r:
                    for u in range(2):
                        load_out(r * 2 + (u + 1), 1 - u)
                        store_y(r * 2 + u, r, u)
                load_out(NCH - 1, 1)
                store_y(NCH - 2, ROUNDS - 1, 0)
                store_y(NCH - 1, ROUNDS - 1, 1)
                for u in range(2):
                    sp.wait_ge(y_out[u], 1 + 16 * ROUNDS)
                sp.dma_start(Y, y_scr.rearrange("(t p) d -> p t d", p=P)).then_inc(y_in, 16)
                sp.dma_start(DROW, row(t["ssm_d"])).then_inc(y_in, 16)
                with sp.Fori(0, NW // 4) as r:
                    for s in range(SLOTS):
                        load(s, r + uw[s], wblock(t["ssm_w_out"], r * 4 + s))

            def pe_():
                in_pe()
                def turn_inputs(c, u):
                    pe.wait_ge(uc_cut, c + 1)
                    pe.wait_ge(ut_saved, 1 + c)
                    apart(pe)
                    for i in range(CG):
                        mm = pe.transpose(PS[:, 4 + 3 * u, i * NBLK:(i + 1) * NBLK], UCG[u][:, i, :], IDENT[0:NBLK, 0:NBLK])
                    mm.then_inc(ut_sums, 1)

                def states(c, r, u):
                    pe.wait_ge(slm_in[u], r * 16 + 16)
                    pe.wait_ge(ut_saved, 2 + c + 1)
                    pe.wait_ge(vf_saved, 1 + c)
                    pe.wait_ge(vb_saved, 1 + c)
                    for i in range(CG):
                        for x in range(2):
                            mm = pe.matmul(PS[:, 5 - 5 * u + i // 4, ((i % 4) * 2 + x) * NBLK:((i % 4) * 2 + x + 1) * NBLK],
                                           SLM[u][:, i, x, :], UTST[u][:, i, :], start=True, stop=True)
                    mm.then_inc(v_sums, 1)

                def state_round(r, more):
                    for u in range(2):
                        states(r * 2 + u, r, u)
                        if more or u == 0:
                            turn_inputs(r * 2 + (u + 1), 1 - u)

                turn_inputs(0, 0)
                with pe.Fori(0, ROUNDS - 1) as r:
                    state_round(r, True)
                state_round(ROUNDS - 1, False)
                with pe.Fori(0, ROUNDS) as r:
                    for u in range(2):
                        c = r * 2 + u
                        pe.wait_ge(slo_in[u], r * 16 + 16)
                        pe.wait_ge(d_sum, c + 1)
                        pe.wait_ge(hst_done, c * 3 + 3)
                        pe.wait_ge(y_saved, 1 + c)
                        for i in range(CG):
                            out = PS[0:LATB, 2 * u + i // 4, (i % 4) * P:(i % 4 + 1) * P]
                            pe.matmul(out, UTLS[u][:, i, :], DF[u][:, i, :], start=True, stop=False)
                            pe.matmul(out, HST[u][:, 0, i, :], SLO[u][:, 0, i, :], start=False, stop=False)
                            mm = pe.matmul(out, HST[u][:, 1, i, :], SLO[u][:, 1, i, :], start=False, stop=True)
                        mm.then_inc(y_sums, 1)
                turn_pe()
                pe.wait_ge(n_ht.sem, turn_end)
                pe.wait_ge(y_saved, 2 + NCH)
                with pe.Fori(0, NW // 4) as r:
                    for s in range(4):
                        pe.wait_ge(w_full[s], (r + uw[s] + 1) * 16)
                        pe.wait_ge(sums_taken.sem, r * 8 + (st + (s // 2 - 1) * 4))
                        for tb in range(2):
                            for k in range(KT):
                                mm = pe.matmul(PS[:, s, tb * COLS:(tb + 1) * COLS], HT[:, k, tb * P:(tb + 1) * P],
                                               W[:, s, k * COLS:(k + 1) * COLS], start=(k == 0), stop=(k == KT - 1))
                        mm.then_inc(w_used[s], 1)

            def act_():
                in_take(a)
                def cut_inputs(c, r, u):
                    a.wait_ge(uc_in[u], r * 16 + 16)
                    a.wait_ge(ut_sums, 1 + c)
                    a.copy(UCG[u].rearrange("k g (s c) -> k g s c", s=T8), UC[u].rearrange("k s (g c) -> k g s c", g=CG)).then_inc(uc_cut, 1)

                def save_round(r, more):
                    for u in range(2):
                        c = r * 2 + u
                        a.wait_ge(ut_sums, 2 + c + 1)
                        a.wait_ge(v_sums, 1 + c)
                        a.wait_ge(utl_saved, 1 + c)
                        a.copy(UTST[u], PS[:, 4 + 3 * u, :].rearrange("p (g k) -> p g k", g=CG)).then_inc(ut_saved, 1)
                        if u == 0:
                            cut_inputs(c + 1, r, 1)
                        elif more:
                            cut_inputs(c + 1, r + 1, 0)
                        a.wait_ge(v_sums, 2 + c + 1)
                        for x in range(2):
                            ins = a.copy(V[0:64, :, x, ds(c * CG, CG)].rearrange("p k g -> p g k"), parts(u)[0:64, :, x, :])
                        ins.then_inc(vf_saved, 1)

                cut_inputs(0, 0, 0)
                with a.Fori(0, ROUNDS - 1) as r:
                    save_round(r, True)
                save_round(ROUNDS - 1, False)
                a.wait_ge(utl_saved, 2 + NCH)
                with a.Fori(1, NBLK - 1) as j:
                    for h in range(2):
                        a.wait_ge(whole[h], j + 1)
                    a.copy(V[:, ds(j, 1)].rearrange("p a r g -> p (a r) g"), STATE_).then_inc(placed, 1)
                a.wait_ge(placed, NBLK - 1)

                def cut_states(c, u):
                    a.wait_ge(y_sums, 1 + c)
                    a.copy(UTLS[u], UTL[:, ds(c * CG, CG), :]).then_inc(hst_done, 1)
                    first = NBLK - LATB - 1
                    fwd = V[0:64, first:NBLK - 1, :, ds(c * CG, CG)].rearrange("p k r g -> p r g k")
                    bwd = V[64:P, first:NBLK - 1, :, ds(c * CG, CG)].rearrange("p k r g -> p r g k")
                    a.copy(HST[u][0:64], fwd).then_inc(hst_done, 1)
                    a.copy(HST[u][64:P][:, :, :, ::-1], bwd).then_inc(hst_done, 1)

                def save_y(c, r, u):
                    a.wait_ge(y_sums, 2 + c + 1)
                    a.wait_ge(y_out[u], 1 + r * 16)
                    a.copy(YC[u].rearrange("k t (g x) -> k g t x", g=CG)[:, :, ::-1, :],
                           PS[0:LATB, 2 * u:2 * u + 2, :].rearrange("k b (g t x) -> k (b g) t x", g=4, t=T8)).then_inc(y_saved, 1)

                cut_states(0, 0)
                with a.Fori(0, ROUNDS - 1) as r:
                    for u in range(2):
                        cut_states(r * 2 + (u + 1), 1 - u)
                        save_y(r * 2 + u, r, u)
                cut_states(NCH - 1, 1)
                save_y(NCH - 2, ROUNDS - 1, 0)
                save_y(NCH - 1, ROUNDS - 1, 1)
                for tb in range(2):
                    a.wait_ge(y_done, tb + 1)
                    a.activation(VAL[:, tb, :], Y[:, tb, :], ACT.Gelu_apprx_tanh).then_inc(z_done, 1)
                turn_act()
                with a.Fori(0, NW // 4) as r:
                    for s in (1, 3):
                        a.wait_ge(w_used[s], r + uw[s] + 2)
                        a.wait_ge(sums_taken.sem, r * 8 + (st + (s // 2) * 4))
                        a.activation(SG, PS[:, s, :].rearrange("p (t c) -> p t c", t=2), ACT.Sigmoid).then_inc(sg_done, 1)

            def dve_():
                with v.Fori(0, ROUNDS) as r:
                    for u in range(2):
                        c = r * 2 + u
                        v.wait_ge(ut_saved, 2 + c + 1)
                        v.tensor_copy(UTL[:, ds(c * CG, CG), :], UTST[u][:, :, NBLK - LATB:NBLK]).then_inc(utl_saved, 1)
                        v.wait_ge(v_sums, 2 + c + 1)
                        for lo, hi in ((0, NBLK - LATB), (NBLK - LATB, NBLK)):
                            for x in range(2):
                                last = v.tensor_copy(V[64:P, lo:hi, x, ds(c * CG, CG)].rearrange("p k g -> p g k"),
                                                     parts(u)[64:P, :, x, lo:hi][:, :, ::-1])
                        last.then_inc(vb_saved, 1)
                v.wait_ge(vf_saved, 2 + NCH)
                v.wait_ge(vb_saved, 2 + NCH)
                v.wait_ge(step_in, 32)
                halves = [slice(h * (GROUPS // 2), (h + 1) * (GROUPS // 2)) for h in range(2)]
                for h, gr in enumerate(halves):
                    v.tensor_copy(STATE_[:, :, gr], V[:, 0, :, gr]).then_inc(whole[h], 1)
                def step(j):
                    cur = V[:, ds(j, 1)].rearrange("p a r g -> p (a r) g")
                    for h, gr in enumerate(halves):
                        v.wait_ge(whole[h], j)
                        v.tensor_tensor(TA[:, :, gr], A8R[:, :, gr], STATE_[:, :, gr], ALU.mult)
                        v.tensor_tensor(TB_[:, ::-1, gr], A8S[:, ::-1, gr], STATE_[:, :, gr], ALU.mult).then_inc(scaled[h], 1)
                    for h, gr in enumerate(halves):
                        v.wait_ge(scaled[h], j)
                        v.tensor_tensor(TA[:, :, gr], TA[:, :, gr], TB_[:, :, gr], ALU.add).then_inc(turned[h], 1)
                    v.wait_ge(placed, j)
                    for h, gr in enumerate(halves):
                        v.wait_ge(turned[h], j)
                        v.tensor_tensor(STATE_[:, :, gr], TA[:, :, gr], cur[:, :, gr], ALU.add).then_inc(whole[h], 1)
                with v.Fori(1, NBLK - 1, 2) as j:
                    step(j)
                    step(j + 1)
                v.wait_ge(placed, NBLK - 1)
                with v.Fori(0, ROUNDS) as r:
                    for u in range(2):
                        v.wait_ge(df_in[u], r * N_D + N_D)
                        v.wait_ge(db_in[u], r * N_D + N_D)
                        v.tensor_tensor(DF[u], DF[u], DB[u], ALU.add).then_inc(d_sum, 1)
                v.wait_ge(y_in, 32)
                for tb in range(2):
                    dve.link(v, v.tensor_tensor(H[:, tb, :], H[:, tb, :], DROW, ALU.mult))
                    v.tensor_tensor(Y[:, tb, :], Y[:, tb, :], H[:, tb, :], ALU.add).then_inc(y_done, 1)
                with v.Fori(0, NW // 4) as r:
                    dve.enter(r, 8)
                    for s in (1, 3):
                        v.wait_ge(sg_done, r * 2 + (s // 2 + 1))
                        v.wait_ge(w_used[s - 1], r + uw[s - 1] + 2)
                        for tb in range(2):
                            col = r * (2 * COLS) + (s // 2) * COLS
                            dst = XA[:, tb, ds(col, COLS)]
                            x = TMP[:, tb, :]
                            dve.link(v, v.tensor_tensor(x, PS[:, s - 1, tb * COLS:(tb + 1) * COLS], SG[:, tb, :], ALU.mult))
                            dve.link(v, v.tensor_tensor(x, x, AR[:, ds(col + 2 * D, COLS)], ALU.mult))
                            v.tensor_tensor(dst, dst, x, ALU.add).then_inc(sums_taken.sem, 2)
                    dve.leave(NW // 4)
                mark()

            mark = mark_x()
            return Stage(sync=sync, pe=pe_, act=act_, dve=dve_, pool=pool_)

        PIECES = ((0, P), (P, 3 * P))
        SCORES = 3 * P

        att_sums, neg_ready, pv_sums = (sem("att_" + n) for n in ("sums", "negmax", "pv_sums"))
        s_taken, att_exp, pt_sums, pt_saved, o_taken = (primed("att_" + n) for n in ("s_taken", "exp", "turned", "pt_saved", "o_taken"))

        def fox(ht_at):
            O = view(0, 2, D)
            VT = view(2048, 2, D)
            QP, KP = view(4096, 2, SEQ), view(4608, 2, SEQ)
            LT = view(5120, 2, SCORES)
            SB = view(5888, 2, SCORES)
            PB = view(6656, 2, SCORES)
            PTB = view(7424, 2, SCORES)
            FW = view(8192, KT, FOX_H)
            BF = view(8320, FOX_H)
            ZF, AF, LF = view(8336, 2, FOX_H), view(8368, 2, FOX_H), view(8400, 2, FOX_H)
            NM, SUMS, RS = view(8432, 4), view(8436, 4), view(8440, 4)
            TMPM = view(8444, 4)
            SUF = view(8448, 2, SEQ)
            PAIRS = FOX_H // 2
            ROUNDS = PAIRS // 2
            par_in, f_sums, f_z, f_exp, f_one, f_log = (sem("fox_" + n) for n in ("par_in", "f_sums", "f_abs", "f_exp", "f_one", "f_log"))
            lt_ready = sem("fox_gates")
            qk_saved, v_saved = sem("fox_qk_saved"), sem("fox_v_saved")
            uw = take([ROUNDS, ROUNDS, ROUNDS, 0])
            turn_pe, turn_act, turn_end = turn(lambda tb: O[:, tb, :], range(2), KT, o_taken, lambda i: 1 + 4 * PAIRS,
                                               lambda q, i: HT[:, 4 * q:4 * q + 4, i * P:(i + 1) * P])
            out_sync, out_pe, out_take, out_end = linear(t["fox_out"], 4, 2, lambda k, tb: HT[:, k, tb * P:(tb + 1) * P],
                                                         add_gated(None, 2, None), ht_at=turn_end)
            mark = mark_x()
            st = sums_taken.total - 8

            def sync():
                sp.wait_ge(n_ht.sem, ht_at)
                sp.sem_inc(qk_saved, 4)
                sp.dma_start(FW, t["fox_f"]).then_inc(par_in, 16)
                sp.dma_start(BF, row(t["fox_b"])).then_inc(par_in, 16)
                sp.dma_start(SUF.rearrange("p b k -> p (b k)"), t["consts"][:, C_SUF:C_SUF + 2 * SEQ]).then_inc(par_in, 16)
                with sp.Fori(0, ROUNDS) as r:
                    load(0, r + uw[0], wblock(t["fox_qk"], r * 2))
                    load(2, r + uw[2], wblock(t["fox_v"], r))
                    load(1, r + uw[1], wblock(t["fox_qk"], r * 2 + 1))
                out_sync()

            def pe_():
                def project(r, s):
                    j = r * 2 + s
                    pe.wait_ge(w_full[s], (r + uw[s] + 1) * 16)
                    pe.wait_ge(qk_saved, j * 2 + 2)
                    for part in range(2):
                        for k in range(KT):
                            mm = pe.matmul(PS[:, s, part * SEQ:(part + 1) * SEQ], W[:, s, k * COLS + part * P:k * COLS + (part + 1) * P],
                                           HT[:, k, 0:SEQ], start=(k == 0), stop=(k == KT - 1))
                    mm.then_inc(w_used[s], 1)
                    if s == 0:
                        pe.wait_ge(w_full[2], (r + uw[2] + 1) * 16)
                        pe.wait_ge(v_saved, r)
                        for tb in range(2):
                            for k in range(KT):
                                mm = pe.matmul(PS[:, 2, tb * COLS:(tb + 1) * COLS], HT[:, k, tb * P:(tb + 1) * P],
                                               W[:, 2, k * COLS:(k + 1) * COLS], start=(k == 0), stop=(k == KT - 1))
                        mm.then_inc(w_used[2], 1)

                def scores(r, s):
                    j = r * 2 + s
                    pe.wait_ge(qk_saved, j * 2 + 6)
                    pe.wait_ge(lt_ready, j * 2 + 2)
                    pe.wait_ge(s_taken, 1 + j * 2)
                    for i in range(2):
                        h = slice(i * FOX_D, (i + 1) * FOX_D)
                        first, second = PS[:, 3 + i, 0:P], PS[:, 3 + i, P:SCORES]
                        pe.matmul(first, QP[h, s, 0:P], KP[h, s, 0:P], start=True, stop=False)
                        pe.matmul(first, LT[:, i, 0:P], SUF[:, 0, 0:P], start=False, stop=True)
                        pe.matmul(second, QP[h, s, P:SEQ], KP[h, s, :], start=True, stop=False)
                        pe.matmul(second, LT[:, i, P:SEQ], SUF[:, 0, :], start=False, stop=False)
                        mm = pe.matmul(second, LT[:, i, SEQ:SCORES], SUF[:, 1, :], start=False, stop=True)
                    mm.then_inc(att_sums, 1)

                def values(r, s):
                    j = r * 2 + s
                    for i in range(2):
                        pe.wait_ge(att_exp, 1 + j * 4 + (2 * i + 2))
                        pe.wait_ge(pt_saved, 1 + j * 2)
                        for k in range(3):
                            mm = pe.transpose(PS[:, 5 + i, k * P:(k + 1) * P], PB[:, i, k * P:(k + 1) * P], IDENT)
                        mm.then_inc(pt_sums, 1)
                    pe.wait_ge(v_saved, r + 1)
                    pe.wait_ge(o_taken, 1 + j * 4)
                    for i in range(2):
                        pe.wait_ge(pt_saved, 1 + j * 2 + (i + 1))
                        vh = [VT[:, kb, ds(r * COLS + (s * 2 + i) * FOX_D, FOX_D)] for kb in range(2)]
                        outs = [PS[:, 7, (2 * i + q) * FOX_D:(2 * i + q + 1) * FOX_D] for q in range(2)]
                        pe.matmul(outs[0], PTB[:, i, 0:P], vh[0], start=True, stop=True)
                        pe.matmul(outs[1], PTB[:, i, P:SEQ], vh[0], start=True, stop=False)
                        pe.matmul(outs[1], PTB[:, i, SEQ:SCORES], vh[1], start=False, stop=True).then_inc(pv_sums, 1)

                def pe_round(r, more):
                    for s in range(2):
                        scores(r, s)
                        if s == 0:
                            project(r, 1)
                        elif more:
                            project(r + 1, 0)
                        values(r, s)

                pe.wait_ge(n_ht.sem, ht_at)
                pe.wait_ge(par_in, 48)
                pe.wait_ge(sums_taken.sem, st)
                for tb in range(2):
                    for k in range(KT):
                        mm = pe.matmul(PS[:, 7, tb * FOX_H:(tb + 1) * FOX_H], HT[:, k, tb * P:(tb + 1) * P], FW[:, k, :],
                                       start=(k == 0), stop=(k == KT - 1))
                mm.then_inc(f_sums, 1)
                project(0, 0)
                with pe.Fori(0, ROUNDS - 1) as r:
                    pe_round(r, True)
                pe_round(ROUNDS - 1, False)
                turn_pe()
                out_pe()

            def act_():
                def save(r, s):
                    a.wait_ge(w_used[s], r + uw[s] + 2)
                    a.activation(QP[:, s, :], PS[:, s, 0:SEQ], ACT.Copy, scale=FOX_D ** -0.5).then_inc(qk_saved, 1)
                    a.copy(KP[:, s, :], PS[:, s, SEQ:2 * SEQ]).then_inc(qk_saved, 1)
                    if s == 0:
                        a.wait_ge(w_used[2], r + uw[2] + 2)
                        a.copy(VT[:, :, ds(r * COLS, COLS)], PS[:, 2, :].rearrange("p (t c) -> p t c", t=2)).then_inc(v_saved, 1)

                def soft(r, s):
                    j = r * 2 + s
                    a.wait_ge(neg_ready, j + 1)
                    a.wait_ge(pt_sums, 1 + j * 2)
                    for i in range(2):
                        for q, (lo, hi) in enumerate(PIECES):
                            c = 2 * i + q
                            a.activation(PB[:, i, lo:hi], SB[:, i, lo:hi], ACT.Exp, bias=NM[:, c:c + 1],
                                         accum_out=SUMS[:, c:c + 1]).then_inc(att_exp, 1)

                def save_turned(r, s):
                    j = r * 2 + s
                    for i in range(2):
                        a.wait_ge(pt_sums, 1 + j * 2 + (i + 1))
                        a.copy(PTB[:, i, :], PS[:, 5 + i, 0:SCORES]).then_inc(pt_saved, 1)

                def act_round(r, more):
                    for s in range(2):
                        soft(r, s)
                        if s == 0:
                            save(r, 1)
                        elif more:
                            save(r + 1, 0)
                        save_turned(r, s)

                a.wait_ge(f_z, 1)
                a.activation(AF, AF, ACT.Exp, scale=-1.0).then_inc(f_exp, 1)
                a.wait_ge(f_one, 1)
                a.activation(AF, AF, ACT.Ln).then_inc(f_log, 1)
                save(0, 0)
                with a.Fori(0, ROUNDS - 1) as r:
                    act_round(r, True)
                act_round(ROUNDS - 1, False)
                turn_act()

            def dve_():
                def gates(j):
                    v.wait_ge(att_sums, j)
                    for i in range(2):
                        for lo, hi, tb in ((0, SEQ, 0), (SEQ, SCORES, 1)):
                            one = v.tensor_tensor(LT[:, i, lo:hi], TRI[:, lo:hi], LF[:, tb, ds(j * 2 + i, 1)].to_broadcast([P, hi - lo]), ALU.mult)
                        one.then_inc(lt_ready, 1)

                def pair(j, more):
                    v.wait_ge(att_sums, j + 1)
                    v.wait_ge(att_exp, 1 + j * 4)
                    for i in range(2):
                        last = v.tensor_tensor(SB[:, i, :], PS[:, 3 + i, 0:SCORES], FOX_MASK, ALU.add)
                        last.then_inc(s_taken, 1)
                    v.wait_ge(s_taken, 1 + j * 2 + 2)
                    for i in range(2):
                        for q, (lo, hi) in enumerate(PIECES):
                            last = v.tensor_reduce(TMPM[:, 2 * i + q:2 * i + q + 1], SB[:, i, lo:hi], AX_X, ALU.max)
                    dve.link(v, last)
                    v.tensor_scalar(NM, TMPM, -1.0, None, ALU.mult).then_inc(neg_ready, 1)
                    if more:
                        gates(j + 1)
                    v.wait_ge(att_exp, 1 + j * 4 + 4)
                    dve.link(v, v.reciprocal(RS, SUMS))
                    v.wait_ge(pv_sums, j * 2 + 2)
                    for i in range(2):
                        for q in range(2):
                            c = 2 * i + q
                            v.tensor_scalar(O[:, q, ds(j * P + i * FOX_D, FOX_D)], PS[:, 7, c * FOX_D:(c + 1) * FOX_D],
                                            RS[:, c:c + 1], None, ALU.mult).then_inc(o_taken, 1)

                v.wait_ge(par_in, 48)
                v.wait_ge(f_sums, 1)
                sums = PS[:, 7, 0:2 * FOX_H].rearrange("p (t h) -> p t h", t=2)
                dve.link(v, v.tensor_tensor(ZF, sums, BF.unsqueeze(1).to_broadcast([P, 2, FOX_H]), ALU.add))
                v.scalar_tensor_tensor(AF, ZF, -1.0, ZF, ALU.mult, ALU.max).then_inc(f_z, 1)
                v.wait_ge(f_exp, 1)
                v.tensor_scalar(AF, AF, 1.0, None, ALU.add).then_inc(f_one, 1)
                v.wait_ge(f_log, 1)
                dve.link(v, v.scalar_tensor_tensor(LF, ZF, 0.0, AF, ALU.min, ALU.subtract))
                gates(0)
                with v.Fori(0, PAIRS - 1) as j:
                    dve.enter(j, 2)
                    pair(j, True)
                    dve.leave(PAIRS - 1)
                pair(PAIRS - 1, False)
                out_take(v)
                mark()

            return Stage(sync=sync, pe=pe_, act=act_, dve=dve_)

        def mask(high, src):
            return v.tensor_scalar(high.bitcast(U32), src.bitcast(U32), HIGH, None, ALU.bitwise_and)

        def split(parts, src, tmp):
            dve.link(v, mask(tmp, src))
            v.tensor_copy(parts[0], tmp)
            return v.tensor_tensor(parts[1], src, tmp, ALU.subtract)

        def products(out, lhs, rhs, start, stop):
            for n, (i, j) in enumerate(((0, 0), (0, 1), (1, 0))):
                mm = pe.matmul(out, lhs[i], rhs[j], start=(start and n == 0), stop=(stop and n == 2))
            return mm

        def split_rows(ht_at, tmp, halves=2):
            for tb in range(2):
                for q in range(halves):
                    v.wait_ge(n_ht.sem, ht_at - 2 * halves + tb * halves + q + 1)
                    k4, cols = slice(4 * q, 4 * q + 4), slice(tb * P, (tb + 1) * P)
                    last = split([XP[:, x, k4, cols] for x in range(2)], HT[:, k4, cols], tmp[:, k4, cols])
            dve.link(v, last)

        cw_in, pad_done, cw_ready, silu_done = (sem("ffn_" + n) for n in ("taps_in", "pad", "taps_cut", "silu"))
        split_done, high_done, masked = sem("ffn_split"), sem("ffn_high"), sem("ffn_masked")
        u_saved, conv_done, gv_ready = (primed("ffn_" + n) for n in ("u_saved", "conv", "gated"))

        def ffn(layer, ht_at):
            U = view(0, 4, SEQ + 2)
            CT = view(1040, 4, SEQ)
            SIL = view(2064, 2, SEQ)
            GV = view(2576, 2, SEQ)
            CW = view(3088, FFC, 16)
            CWC = view(3088 + 16 * FFC, 4, 4)
            GVT = view(4096, 2, SEQ)
            WT = view(PARTS_END, BLK)
            XT = view(PARTS_END + BLK, KT, SEQ)
            uw = take([FFC, FFC, FFC, 0])
            c0 = layer * FFC
            st = sums_taken.plan(4)
            xr = x_ready.total
            names = [f"ffn_gate{layer}", f"ffn_val{layer}", f"ffn_out{layer}"]

            def split_at(s, c):
                base = layer * (3 * FFC + 1)
                if s < 2:
                    return base + s + (2 if isinstance(c, int) and c == 0 else c * 3 + 1)
                return base + (3 * FFC + 1 if isinstance(c, int) and c == FFC - 1 else c * 3 + 6)

            def sync():
                sp.wait_ge(x_ready.sem, xr)
                sp.dma_start(CW, t["ffn_conv"][layer]).then_inc(cw_in, 16)

                def fetch(s, c, first=False):
                    if first:
                        load(s, uw[s], t[names[s]][c])
                    else:
                        sp.wait_ge(split_done, split_at(s, c - 1))
                        sp.dma_start(W[:, s, :], wblock(t[names[s]], c)).then_inc(w_full[s], 16)

                sp.sem_inc(split_done, 1)
                sp.sem_inc(high_done, 1)
                sp.sem_inc(masked, 1)
                for s in range(3):
                    fetch(s, 0, first=True)
                for s in range(2):
                    sp.wait_ge(split_done, split_at(s, 0))
                    sp.dma_start(W[:, s, :], t[names[s]][1]).then_inc(w_full[s], 16)
                with sp.Fori(1, FFC - 1) as c:
                    fetch(0, c + 1)
                    fetch(1, c + 1)
                    fetch(2, c)
                sp.wait_ge(split_done, split_at(2, FFC - 2))
                sp.dma_start(W[:, 2, :], t[names[2]][FFC - 1]).then_inc(w_full[2], 16)

            def pe_():
                def project(c):
                    for s in range(2):
                        pe.wait_ge(split_done, split_at(s, c))
                        pe.wait_ge(high_done, split_at(s, c))
                        pe.wait_ge(u_saved, 1 + (c + c0) * 8)
                        for m in range(2):
                            for k in range(KT):
                                w = [WP[:, s, x, k * COLS + m * P:k * COLS + (m + 1) * P] for x in range(2)]
                                mm = products(PS[:, 4 + s, m * SEQ:(m + 1) * SEQ], w, [XP[:, x, k, :] for x in range(2)], k == 0, k == KT - 1)
                        mm.then_inc(w_used[s], 1)

                def output(c, start, stop):
                    pe.wait_ge(split_done, split_at(2, c))
                    pe.wait_ge(high_done, split_at(2, c))
                    pe.wait_ge(gv_ready, 1 + c0 + c + 1)
                    for tb in range(2):
                        for half in range(2):
                            for k in range(2):
                                g_ = [GVP[:, x, k, tb * P:(tb + 1) * P] for x in range(2)]
                                w = [WP[:, 2, x, k * D + half * 512:k * D + (half + 1) * 512] for x in range(2)]
                                mm = products(PS[:, tb * 2 + half, :], g_, w, start and k == 0, stop and k == 1)
                    mm.then_inc(w_used[2], 1)

                pe.wait_ge(n_ht.sem, ht_at)
                pe.wait_ge(sums_taken.sem, st)
                project(0)
                project(1)
                output(0, True, False)
                with pe.Fori(1, FFC - 1) as c:
                    project(c + 1)
                    output(c, False, False)
                output(FFC - 1, False, True)

            def act_():
                def save_high(s, c):
                    a.wait_ge(masked, split_at(s, c))
                    a.copy(WP[:, s, 0, :], WT).then_inc(high_done, 1)

                def chunk(c, more):
                    a.wait_ge(cw_ready, c0 + c + 1)
                    a.wait_ge(conv_done, 1 + c0 + c)
                    for s in range(2):
                        a.wait_ge(w_used[s], c + uw[s] + 2)
                        for m in range(2):
                            i = s * 2 + m
                            src = PS[:, 4 + s, m * SEQ:(m + 1) * SEQ]
                            a.copy(U[:, i, 2:SEQ + 2], src).then_inc(u_saved, 1)
                            a.activation(CT[:, i, :], src, ACT.Identity, scale=CWC[:, i, 2:3], bias=CWC[:, i, 3:4]).then_inc(u_saved, 1)
                    if more:
                        save_high(0, c + 1)
                    a.wait_ge(conv_done, 1 + c0 + c + 1)
                    a.wait_ge(gv_ready, 1 + c0 + c)
                    a.activation(SIL, CT[:, 0:2, :], ACT.Silu).then_inc(silu_done, 1)
                    if more:
                        save_high(1, c + 1)
                    save_high(2, c)

                a.wait_ge(pad_done, layer + 1)
                for s in range(2):
                    save_high(s, 0)
                with a.Fori(0, FFC - 1) as c:
                    chunk(c, True)
                chunk(FFC - 1, False)

            def dve_():
                v.wait_ge(x_ready.sem, xr)
                v.memset(U[:, :, 0:2], 0.0).then_inc(pad_done, 1)
                v.wait_ge(pad_done, layer + 1)
                v.wait_ge(cw_in, 16 * (layer + 1))
                split_rows(ht_at, XT)

                def split_block(s, c):
                    v.wait_ge(w_full[s], (c + uw[s] + 1) * 16)
                    v.wait_ge(w_used[s], c + (uw[s] + 1))
                    n = split_at(s, c)
                    v.wait_ge(high_done, n - 1)
                    v.wait_ge(split_done, n - 1)
                    mask(WT, W[:, s, :]).then_inc(masked, 1)
                    v.wait_ge(masked, n)
                    v.tensor_tensor(WP[:, s, 1, :], W[:, s, :], WT, ALU.subtract).then_inc(split_done, 1)

                def chunk(c, more):
                    v.wait_ge(u_saved, 1 + (c + c0) * 8)
                    v.wait_ge(conv_done, 1 + c0 + c)
                    v.tensor_copy(CWC.rearrange("p i j -> p (i j)"), CW[:, ds(c, 1), :].rearrange("p a j -> p (a j)")).then_inc(cw_ready, 1)
                    if more:
                        split_block(0, c + 1)
                    v.wait_ge(u_saved, 1 + (c + c0) * 8 + 8)
                    for i in range(4):
                        last = v.scalar_tensor_tensor(CT[:, i, :], U[:, i, 1:SEQ + 1], CWC[:, i, 1:2], CT[:, i, :], ALU.mult, ALU.add)
                    dve.link(v, last)
                    for i in range(4):
                        last = v.scalar_tensor_tensor(CT[:, i, :], U[:, i, 0:SEQ], CWC[:, i, 0:1], CT[:, i, :], ALU.mult, ALU.add)
                    last.then_inc(conv_done, 1)
                    if more:
                        split_block(1, c + 1)
                    split_block(2, c)
                    v.wait_ge(silu_done, c0 + c + 1)
                    dve.link(v, v.tensor_tensor(GV, SIL, CT[:, 2:4, :], ALU.mult))
                    split([GVP[:, 0], GVP[:, 1]], GV, GVT).then_inc(gv_ready, 1)

                for s in range(2):
                    split_block(s, 0)
                with v.Fori(0, FFC - 1) as c:
                    dve.enter(c, 3)
                    chunk(c, True)
                    dve.leave(FFC - 1)
                chunk(FFC - 1, False)
                v.wait_ge(w_used[2], uw[2] + FFC + 1)
                for tb in range(2):
                    for half in range(2):
                        dst = XA[:, tb, half * 512:(half + 1) * 512]
                        v.tensor_tensor(dst, dst, PS[:, tb * 2 + half, :], ALU.add).then_inc(sums_taken.sem, 1)
                mark()

            mark = mark_x()
            return Stage(sync=sync, pe=pe_, act=act_, dve=dve_)

        KR = view(28160, 2, SEQ)
        QD = lambda tb: H[:, tb, 0:QL]
        CKV = lambda tb: H[:, 2 + tb, 0:KVL]

        def rope(dst, src, t1, t2, done):
            x1, x2 = src[:, 0, :], src[:, 1, :]
            v.tensor_tensor(t1[:, 0, :], x1, COS, ALU.mult)
            v.tensor_tensor(t2[:, 0, :], x2, SIN, ALU.mult)
            v.tensor_tensor(t1[:, 1, :], x1, SIN, ALU.mult)
            dve.link(v, v.tensor_tensor(t2[:, 1, :], x2, COS, ALU.mult))
            v.tensor_tensor(dst[:, 0, :], t1[:, 0, :], t2[:, 0, :], ALU.subtract)
            return v.tensor_tensor(dst[:, 1, :], t1[:, 1, :], t2[:, 1, :], ALU.add).then_inc(done, 1)

        def mla_down(ht_at):
            RAW, T1, T2 = view(0, 2, SEQ), view(512, 2, SEQ), view(1024, 2, SEQ)
            n_blk = QL // COLS + 2
            uw = take([2, 1, 1, 1])
            saved, roped = sem("mla_down_saved"), sem("mla_key_roped")
            st = sums_taken.total
            x_ready.plan(1)

            def sync():
                for b in range(n_blk):
                    load(b % SLOTS, uw[b % SLOTS] + b // SLOTS, t["mla_down"][b])

            def pe_():
                pe.wait_ge(n_ht.sem, ht_at)
                pe.wait_ge(sums_taken.sem, st)
                for b in range(n_blk):
                    s = b % SLOTS
                    pe.wait_ge(w_full[s], (uw[s] + b // SLOTS + 1) * 16)
                    for half in range(2):
                        for k in range(KT):
                            if b < n_blk - 1:
                                at = half * P + (SEQ if b == n_blk - 2 else 0)
                                ops = HT[:, k, at:at + P], W[:, s, k * COLS:(k + 1) * COLS]
                            else:
                                ops = W[:, s, k * COLS + half * P:k * COLS + (half + 1) * P], HT[:, k, SEQ:2 * SEQ]
                            mm = pe.matmul(PS[:, b, half * COLS:(half + 1) * COLS], *ops, start=(k == 0), stop=(k == KT - 1))
                    mm.then_inc(w_used[s], 1)

            def act_():
                for b in range(n_blk):
                    s = b % SLOTS
                    a.wait_ge(w_used[s], uw[s] + b // SLOTS + 2)
                    sums = PS[:, b, :].rearrange("p (t c) -> p t c", t=2)
                    dst = H[:, 0:2, b * COLS:(b + 1) * COLS] if b < n_blk - 2 else H[:, 2:4, 0:KVL] if b == n_blk - 2 else RAW
                    a.copy(dst, sums).then_inc(saved, 1)

            def dve_():
                v.wait_ge(saved, n_blk)
                rope(KR, RAW, T1, T2, roped)
                v.memset(SM[:, 500:501], 0.0).then_inc(x_ready.sem, 1)

            return Stage(sync=sync, pe=pe_, act=act_, dve=dve_)

        def mla(ht_at):
            G4 = 4
            ROUNDS = MLA_H // G4
            HV = MLA_H * VD
            O = view(0, 2, HV)
            VT = view(4096, 2, HV)
            QN, KN = view(8192, G4, SEQ), view(9216, G4, SEQ)
            RAW, T1, T2, QR = view(10240, 2, SEQ), view(10752, 2, SEQ), view(11264, 2, SEQ), view(11776, 2, SEQ)
            SB, PB, PTB = view(12288, G4, SCORES), view(13824, G4, SCORES), view(15360, G4, SCORES)
            NM, SUMS, RS, TMPM = (view(16896 + 8 * i, 8) for i in range(4))
            QK, LK = QL // P, KVL // P
            OT = HT[:, :, :].rearrange("p k (a t) -> p (k a) t", a=2)
            UNITS = 7
            scale = (NOPE + ROPE) ** -0.5
            p_sums, p_taken, roped = sem("mla_p_sums"), sem("mla_p_taken"), sem("mla_q_roped")
            BY_PAIR, BY_HEAD, BY_ROWS = FOX_H // 2, FOX_H, 2 * FOX_H
            uw = take([ROUNDS] * SLOTS)
            turn_pe, turn_act, turn_end = turn(lambda tb: O[:, tb, :], range(2), HV // P, o_taken, lambda i: 1 + BY_ROWS + 2 * MLA_H,
                                               lambda q, i: OT[:, 4 * q:4 * q + 4, i * P:(i + 1) * P])
            out_sync, out_pe, out_take, out_end = linear(t["mla_out"], 8, 2, lambda k, tb: OT[:, k, tb * P:(tb + 1) * P],
                                                         add_gated(None, 2, None, cols=P), ht_at=turn_end, kt=HV // P)
            mark = mark_x()
            n_h_at = n_h.total

            def sync():
                with sp.Fori(0, ROUNDS) as r:
                    for s in range(3):
                        load(s, r + uw[s], wblock(t["mla_uq"], r * 3 + s), cols=QK * COLS)
                    load(3, r + uw[3], wblock(t["mla_ukv"], r))
                out_sync()

            def pe_():
                def project(r):
                    for u in range(UNITS):
                        s = min(u, 3)
                        if u <= 3:
                            pe.wait_ge(w_full[s], (r + uw[s] + 1) * 16)
                        pe.wait_ge(p_taken, r * UNITS + max(0, u - 3))
                        bank = PS[:, 4 + u % 4, :]
                        if u < 3:
                            for m in range(2):
                                for k in range(QK):
                                    mm = pe.matmul(bank[:, m * SEQ:(m + 1) * SEQ], W[:, s, k * COLS + m * P:k * COLS + (m + 1) * P],
                                                   HT[:, k, 0:SEQ], start=(k == 0), stop=(k == QK - 1))
                            mm.then_inc(w_used[s], 1)
                        elif u < 5:
                            for m in range(2):
                                col = ((u - 3) * 2 + m) * P
                                for k in range(LK):
                                    mm = pe.matmul(bank[:, m * SEQ:(m + 1) * SEQ], W[:, s, k * 512 + col:k * 512 + col + P],
                                                   HT[:, k, SEQ:2 * SEQ], start=(k == 0), stop=(k == LK - 1))
                            mm.then_inc(p_sums, 1)
                        else:
                            tb = u - 5
                            for k in range(LK):
                                mm = pe.matmul(bank, HT[:, k, SEQ + tb * P:SEQ + (tb + 1) * P], W[:, s, 1024 + k * 512:1024 + (k + 1) * 512],
                                               start=(k == 0), stop=(k == LK - 1))
                            mm.then_inc(p_sums if tb == 0 else w_used[s], 1)

                def scores(r):
                    pe.wait_ge(p_taken, r * UNITS + 5)
                    pe.wait_ge(roped, r + 1)
                    for i in range(G4):
                        pe.wait_ge(o_taken, BY_ROWS + 1 + r * (2 * G4))
                        b = slice(i * 32, (i + 1) * 32)
                        for (lo, hi), q in zip(PIECES, (slice(0, P), slice(P, SEQ))):
                            keys = slice(0, hi - lo)
                            out = PS[:, i, lo:hi]
                            pe.matmul(out, QN[:, i, q], KN[:, i, keys], start=True, stop=False)
                            for x in range(2):
                                mm = pe.matmul(out, QR[b, x, q], KR[b, x, keys], start=False, stop=(x == 1))
                        mm.then_inc(att_sums, 1)

                def values(r):
                    for i in range(G4):
                        pe.wait_ge(att_exp, BY_ROWS + 1 + r * (2 * G4) + (2 * i + 2))
                        for k in range(3):
                            mm = pe.transpose(PS[:, i, k * P:(k + 1) * P], PB[:, i, k * P:(k + 1) * P], IDENT)
                        mm.then_inc(pt_sums, 1)
                    pe.wait_ge(p_taken, r * UNITS + UNITS)
                    for i in range(G4):
                        pe.wait_ge(pt_saved, 1 + BY_HEAD + r * G4 + (i + 1))
                        vh = [VT[:, kb, ds(r * (G4 * VD) + i * VD, VD)] for kb in range(2)]
                        pe.matmul(PS[:, i, 0:VD], PTB[:, i, 0:P], vh[0], start=True, stop=True)
                        pe.matmul(PS[:, i, VD:2 * VD], PTB[:, i, P:SEQ], vh[0], start=True, stop=False)
                        pe.matmul(PS[:, i, VD:2 * VD], PTB[:, i, SEQ:SCORES], vh[1], start=False, stop=True).then_inc(pv_sums, 1)

                pe.wait_ge(n_ht.sem, ht_at)
                project(0)
                with pe.Fori(0, ROUNDS - 1) as r:
                    scores(r)
                    project(r + 1)
                    values(r)
                scores(ROUNDS - 1)
                values(ROUNDS - 1)
                turn_pe()
                out_pe()

            def act_():
                def save(r):
                    for u in range(UNITS):
                        if u < 3:
                            a.wait_ge(w_used[u], r + (uw[u] + 2))
                        elif u < 6:
                            a.wait_ge(p_sums, r * 3 + (u - 2))
                        else:
                            a.wait_ge(w_used[3], r + (uw[3] + 2))
                        sums = PS[:, 4 + u % 4, :]
                        two = sums.rearrange("p (m t) -> p m t", m=2)
                        if u < 2:
                            one = a.activation(QN[:, 2 * u:2 * u + 2, :], two, ACT.Copy, scale=scale)
                        elif u == 2:
                            a.wait_ge(roped, r)
                            one = a.activation(RAW, two, ACT.Copy, scale=scale)
                        elif u < 5:
                            one = a.copy(KN[:, 2 * (u - 3):2 * (u - 3) + 2, :], two)
                        else:
                            one = a.copy(VT[:, u - 5, ds(r * (G4 * VD), G4 * VD)], sums)
                        one.then_inc(p_taken, 1)

                def soft(r):
                    for i in range(G4):
                        a.wait_ge(neg_ready, BY_PAIR + r * G4 + (i + 1))
                        a.wait_ge(pt_sums, BY_HEAD + 1 + r * G4)
                        for q, (lo, hi) in enumerate(PIECES):
                            c = 2 * i + q
                            a.activation(PB[:, i, lo:hi], SB[:, i, lo:hi], ACT.Exp, bias=NM[:, c:c + 1],
                                         accum_out=SUMS[:, c:c + 1]).then_inc(att_exp, 1)

                def save_turned(r):
                    for i in range(G4):
                        a.wait_ge(pt_sums, BY_HEAD + 1 + r * G4 + (i + 1))
                        a.copy(PTB[:, i, :], PS[:, i, 0:SCORES]).then_inc(pt_saved, 1)

                a.wait_ge(n_ht.sem, ht_at)
                save(0)
                with a.Fori(0, ROUNDS - 1) as r:
                    soft(r)
                    save(r + 1)
                    save_turned(r)
                soft(ROUNDS - 1)
                save_turned(ROUNDS - 1)
                turn_act()

            def dve_():
                def turn_queries(r):
                    v.wait_ge(p_taken, r * UNITS + 3)
                    v.wait_ge(att_sums, BY_PAIR + r * G4)
                    rope(QR, RAW, T1, T2, roped)

                def four(r, more):
                    v.wait_ge(att_exp, BY_ROWS + 1 + r * (2 * G4))
                    for i in range(G4):
                        v.wait_ge(att_sums, BY_PAIR + r * G4 + (i + 1))
                        v.tensor_tensor(SB[:, i, :], PS[:, i, 0:SCORES], MLA_MASK, ALU.add).then_inc(s_taken, 1)
                    for i in range(G4):
                        v.wait_ge(s_taken, 1 + BY_HEAD + r * G4 + (i + 1))
                        for q, (lo, hi) in enumerate(PIECES):
                            c = 2 * i + q
                            last = v.tensor_reduce(TMPM[:, c:c + 1], SB[:, i, lo:hi], AX_X, ALU.max)
                        dve.link(v, last)
                        v.tensor_scalar(NM[:, 2 * i:2 * i + 2], TMPM[:, 2 * i:2 * i + 2], -1.0, None, ALU.mult).then_inc(neg_ready, 1)
                    if more:
                        turn_queries(r + 1)
                    v.wait_ge(att_exp, BY_ROWS + 1 + r * (2 * G4) + 2 * G4)
                    dve.link(v, v.reciprocal(RS, SUMS))
                    for i in range(G4):
                        v.wait_ge(pv_sums, BY_HEAD + r * G4 + (i + 1))
                        for q in range(2):
                            c = 2 * i + q
                            v.tensor_scalar(O[:, q, ds(r * (G4 * VD) + i * VD, VD)], PS[:, i, q * VD:(q + 1) * VD],
                                            RS[:, c:c + 1], None, ALU.mult).then_inc(o_taken, 1)

                v.wait_ge(n_h.sem, n_h_at)
                turn_queries(0)
                with v.Fori(0, ROUNDS - 1) as r:
                    dve.enter(r, G4 + 2)
                    four(r, True)
                    dve.leave(ROUNDS - 1)
                four(ROUNDS - 1, False)
                out_take(v)
                mark()

            return Stage(sync=sync, pe=pe_, act=act_, dve=dve_)

        def mark_norm():
            x_ready.plan(1)
            at = n_h.total

            def dve_():
                v.wait_ge(n_h.sem, at)
                v.memset(SM[:, 500:501], 0.0).then_inc(x_ready.sem, 1)
            return Stage(dve=dve_)

        def write_out():
            at, out_done = n_h.total, sem("out_done")

            def sync():
                sp.wait_ge(n_h.sem, at)
                sp.dma_start(t["out"].rearrange("(t p) d -> p t d", p=P), H[:, 0:2, :]).then_inc(out_done, 16)
                sp.wait_ge(out_done, 16)
            return Stage(sync=sync)

        stages = []
        first, positions, load_x, cs_done, CS = setup()
        stages.append(first)
        stages.append(front(cs_done, CS, load_x))
        stages.append(positions)
        stages.append(load_mod(0, N_MOD))
        mod1 = [(0, D)] * 2 + [(6 * D, 7 * D)] * 2
        stages.append(norm(None, range(4), gain=t["norm1_g"][0], mod=mod1))
        stages.append(chunk_mixer(n_ht.total))
        mod2 = [(3 * D, 4 * D)] * 2 + [(9 * D, 10 * D)] * 2
        stages.append(norm(None, range(4), gain=t["norm2_g"][0], mod=mod2))
        stages.append(peer(0, 4, n_ht.total))
        stages.append(load_mod(1, 2))
        stages.append(norm(None, range(4), gain=t["norm1_g"][1], mod=mod1))
        stages.append(ssm(n_ht.total))
        stages.append(norm(None, range(2), gain=t["norm2_g"][1], mod=mod2[:2]))
        stages.append(peer(1, 2, n_ht.total))
        stages.append(norm(None, range(2), gain=t["final_g"], dst=lambda tb: XA[:, tb, :], junk=lambda tb: H[:, tb, :], out_ht=False))
        stages.append(mark_norm())
        stages.append(norm(None, range(2), gain=t["fox_norm"]))
        stages.append(fox(n_ht.total))
        stages.append(norm(None, range(2), gain=t["ffn_norm"][0]))
        stages.append(ffn(0, n_ht.total))
        stages.append(norm(None, range(2), gain=t["kv_in_norm"], ht_off=SEQ))
        stages.append(norm(None, range(2), gain=t["mla_norm"], dst=lambda tb: H[:, 2 + tb, :], grow=view(27136, D), keep=True))
        stages.append(mla_down(n_ht.total))
        stages.append(norm(CKV, range(2), gain=t["kv_norm"], width=KVL, dst=CKV, junk=lambda tb: view(2048 + tb * D, KVL), ht_off=SEQ))
        stages.append(norm(QD, range(2), gain=t["q_norm"], width=QL, dst=QD, junk=lambda tb: view(2048 + tb * D, QL)))
        stages.append(mla(n_ht.total))
        stages.append(norm(None, range(2), gain=t["ffn_norm"][1]))
        stages.append(ffn(1, n_ht.total))
        stages.append(norm(None, range(2), gain=t["final_norm"], out_ht=False))
        stages.append(write_out())
        block = ctx.enter_context(nc.Block())

        @block.sync
        def _(eng):
            for s in stages:
                if s.sync:
                    s.sync()

        @block.tensor
        def _(eng):
            for s in stages:
                if s.pe:
                    s.pe()

        @block.scalar
        def _(eng):
            for s in stages:
                if s.act:
                    s.act()

        @block.vector
        def _(eng):
            for s in stages:
                if s.dve:
                    s.dve()

        @block.gpsimd
        def _(eng):
            for s in stages:
                if s.pool:
                    s.pool()


def blocks(w):
    k, n = w.shape
    return np.ascontiguousarray(w.reshape(k // P, P, n // COLS, COLS).transpose(2, 1, 0, 3).reshape(n // COLS, P, -1))


def sincos(pos, dim):
    omega = 1.0 / (10000.0 ** (np.arange(dim // 2, dtype=np.float32) / np.float32(dim // 2)))
    ang = (pos[:, None] * omega[None, :].astype(np.float32)).astype(np.float32)
    return np.concatenate([np.sin(ang), np.cos(ang)], axis=-1)


def constants():
    rows = np.repeat(np.arange(SEQ // GRID_W, dtype=np.float32), GRID_W)
    cols = np.tile(np.arange(GRID_W, dtype=np.float32), SEQ // GRID_W)
    pos = np.concatenate([sincos(rows, D // 2), sincos(cols, D // 2)], axis=-1).astype(np.float32)
    c = np.zeros((P, C_SUF + 2 * SEQ), np.float32)
    c[:, C_ID:C_ID + P] = np.eye(P)
    s, tt = np.arange(SEQ)[:, None], np.arange(SEQ)[None, :]
    tri = (s <= tt).astype(np.float32)
    c[:, C_TRI:C_TRI + SEQ], c[:, C_TRI + SEQ:C_TRI + 3 * P] = tri[:P], tri[P:, P:]
    c[:, C_SUF:C_SUF + SEQ], c[:, C_SUF + SEQ:C_SUF + 2 * SEQ] = 1 - tri[:P], 1 - tri[P:]
    q, k = np.arange(P)[:, None], np.arange(P)[None, :]
    for at, seen in ((C_FOX, k <= q), (C_MLA, k // 64 <= q // 64)):
        m = np.where(seen, 0.0, MASKED)
        c[:, at:at + P] = m
        c[:, at + 2 * P:at + 3 * P] = m
    inv = (np.float32(10000.0) ** (-np.arange(0, ROPE, 2, dtype=np.float32) / np.float32(ROPE))).astype(np.float32)
    ang = (np.arange(SEQ, dtype=np.float32)[:, None] * inv[None, :]).astype(np.float32)
    c[:, C_COS:C_COS + SEQ] = np.tile(np.cos(ang).T, (4, 1))
    c[:, C_SIN:C_SIN + SEQ] = np.tile(np.sin(ang).T, (4, 1))
    c[:, C_IOTA:C_IOTA + TOPK] = np.arange(TOPK)
    return pos, c


def layout(i):
    i = {k: np.asarray(x) for k, x in i.items()}
    pos, consts = constants()
    o = {
        "x": i["x"][0], "ctx": i["ctx"][0], "pos": pos, "consts": consts,
        "cond": np.stack([i["c"][0], i["c_ctx"]], -1).reshape(KT, P, 2).transpose(1, 0, 2),
        "ada_w": np.concatenate([blocks(w) for w in i["ada_w"]]), "ada_b": i["ada_b"], "norm1_g": i["norm1_g"], "norm2_g": i["norm2_g"], "final_g": i["final_g"],
        "cm_w_in": blocks(np.roll(i["cm_w_in"][0], D, axis=1)), "cm_w_out": blocks(i["cm_w_out"][0]),
        "cm_ws": i["cm_w_s"][0].transpose(2, 0, 1), "cm_bs": i["cm_b_s"][0].T,
        "cm_ln_g": i["cm_ln_g"][0], "cm_ln_b": i["cm_ln_b"][0],
        "peer_u": i["peer_u"].reshape(-1, D), "peer_v": i["peer_v"].reshape(-1, D),
        "peer_keys": i["peer_keys"].transpose(0, 4, 1, 2, 3).reshape(DEPTH, 2, P, HEADS, 2, KEYS).transpose(0, 2, 3, 4, 1, 5),
    }
    for l in range(DEPTH):
        o[f"peer_w_q{l}"] = blocks(i["peer_w_q"][l])
    pairs = np.stack(np.split(i["ssm_w_out"][0].reshape(D, 2 * D // COLS, COLS), 2, axis=1), 2).reshape(D, 2 * D)
    both = lambda x: x[0].transpose(0, 2, 1).reshape(P, GROUPS)
    o |= {
        "ssm_w_in": blocks(i["ssm_w_in"][0]), "ssm_w_out": blocks(pairs), "ssm_d": i["ssm_d"][0],
        "ssm_lr": both(i["ssm_lam_re"]), "ssm_li": both(i["ssm_lam_im"]),
        "ssm_ls": np.repeat(i["ssm_log_step"][0], STATE, axis=0),
    }
    for n in ("re", "im"):
        o["ssm_b" + n[0]] = i["ssm_b_" + n][0].transpose(0, 2, 1, 3).reshape(P, GROUPS, GDIM)
        o["ssm_c" + n[0]] = i["ssm_c_" + n][0].transpose(0, 3, 1, 2).reshape(P, GROUPS, GDIM)
    w, h3 = i["w_fox_in_2"][0], FOX_H * FOX_D
    q, k, v = (w[:, n * h3:(n + 1) * h3].reshape(D, FOX_H // 2, P) for n in range(3))
    down, uq = i["w_dkv_2"], i["w_uq_2"][0].reshape(QL, MLA_H // 4, 4, NOPE + ROPE)
    half = ROPE // 2
    uq = np.concatenate([uq[..., :NOPE].reshape(QL, 4, -1), uq[..., NOPE:NOPE + half].reshape(QL, 4, -1),
                         uq[..., NOPE + half:].reshape(QL, 4, -1)], -1).reshape(QL, -1)
    fours = lambda m: m.reshape(KVL // P, P, MLA_H // 4, 4 * P).transpose(2, 1, 0, 3).reshape(MLA_H // 4, P, -1)
    o |= {
        "fox_norm": i["fox_norm_2"][0], "fox_b": i["b_fox_f_2"][0], "fox_out": blocks(i["w_fox_out_2"][0]),
        "fox_qk": blocks(np.concatenate([q, k], -1).reshape(D, -1)), "fox_v": blocks(v.reshape(D, -1)),
        "fox_f": w[:, 3 * h3:].reshape(KT, P, FOX_H).transpose(1, 0, 2),
        "ffn_norm": i["ffn_norm_2"], "kv_in_norm": i["kv_in_norm_2"], "kv_norm": i["kv_norm_2"],
        "mla_norm": i["mla_norm_2"][0], "q_norm": i["q_norm_2"][0], "final_norm": i["final_norm_2"],
        "mla_down": blocks(np.concatenate([i["w_dq_2"][0], down[:, :KVL]] + [down[:, KVL:KVL + half]] * 4
                                          + [down[:, KVL + half:]] * 4, -1)),
        "mla_uq": blocks(uq), "mla_ukv": np.concatenate([fours(i["w_uk_2"]), fours(i["w_uv_2"])], -1),
        "mla_out": i["w_mla_out_2"][0].reshape(-1, P, KT, P).transpose(2, 1, 0, 3).reshape(KT, P, -1),
    }
    taps = np.concatenate([i["ffn_conv_w_2"], i["ffn_conv_b_2"][:, None]], 1)
    o["ffn_conv"] = taps.reshape(DEPTH, 4, 2, FFC, 2, P).transpose(0, 5, 3, 2, 4, 1).reshape(DEPTH, P, FFC, 16)
    for l in range(DEPTH):
        o[f"ffn_gate{l}"], o[f"ffn_val{l}"] = (blocks(m) for m in np.split(i["w_ffn_in_2"][l], 2, axis=1))
        o[f"ffn_out{l}"] = i["w_ffn_out_2"][l].reshape(FFC, 2, P, D).transpose(0, 2, 1, 3).reshape(FFC, P, -1)
    return {k: np.ascontiguousarray(x) for k, x in o.items()}


def kernel(**inputs):
    import concourse.bacc as bacc
    from concourse.bass_utils import run_bass_kernel_spmd as run

    nc = bacc.Bacc("TRN2", target_bir_lowering=False, num_devices=1)
    arrays = {f"in_{n}": x for n, x in layout(inputs).items()}
    t = {n[3:]: nc.dram_tensor(n, x.shape, mybir.dt.from_np(x.dtype), kind="ExternalInput").ap() for n, x in arrays.items()}
    t["out"] = nc.dram_tensor("out", [SEQ, D], F32, kind="ExternalOutput").ap()
    program(nc, t)
    return run(nc, [arrays], core_ids=[0]).results[0]["out"].reshape(1, SEQ, D)
```
